# Optimizing a Trainium2 kernel written in Bass

```python
import math
import jax, jax.numpy as jnp
from jax import lax
import numpy as np

D_MODEL = 1024
BATCH = 1
SEQ = 512
DEPTH = 1

M_HEADS = 4
M_HEAD_DIM = 256
M_WIDTH = M_HEADS * M_HEAD_DIM
M_CHUNK = 64
CONV_WIDTH = 4
N_HEADS = 8
N_KV_GROUPS = 2
N_HPG = N_HEADS // N_KV_GROUPS
N_HEAD_DIM = 64
N_WIDTH = N_HEADS * N_HEAD_DIM
N_KV_WIDTH = N_KV_GROUPS * N_HEAD_DIM
CMP_BLOCK = 32
CMP_STRIDE = 16
CMP_HIDDEN = 128
SEL_BLOCK = 64
SEL_TOPK = 16
WINDOW = 512
Q_BLOCK = 128
ROPE_THETA = 500000.0
ROPE_DIM = N_HEAD_DIM // 4
NORM_EPS = 1e-6
NEG = -1e30
FORCE = 1e9

IN_SPLITS = (
    ("m_q", M_WIDTH), ("m_k", M_WIDTH), ("m_v", M_WIDTH), ("m_o", M_WIDTH), ("m_z", M_WIDTH),
    ("m_i", M_HEADS), ("m_f", M_HEADS),
    ("n_q", N_WIDTH), ("n_kc", N_KV_WIDTH), ("n_vc", N_KV_WIDTH),
    ("n_ks", N_KV_WIDTH), ("n_vs", N_KV_WIDTH), ("n_kw", N_KV_WIDTH), ("n_vw", N_KV_WIDTH),
    ("n_g", 3 * N_HEADS), ("n_z", N_WIDTH),
    ("g_a", D_MODEL), ("g_b", D_MODEL),
)
IN_WIDTH = sum(w for _, w in IN_SPLITS)


def _rmsnorm(x, g):
    xf = x.astype(jnp.float32)
    r = lax.rsqrt(jnp.mean(xf * xf, axis=-1, keepdims=True) + NORM_EPS)
    return (xf * r * g).astype(x.dtype)

def _split_in(u):
    names = [n for n, _ in IN_SPLITS]
    cuts = np.cumsum([w for _, w in IN_SPLITS])[:-1].tolist()
    return dict(zip(names, jnp.split(u, cuts, axis=-1)))

def _causal_dwconv(u, w, b):
    K = w.shape[0]
    T = u.shape[1]
    up = jnp.pad(u, ((0, 0), (K - 1, 0), (0, 0)))
    return b + sum(up[:, j:j + T] * w[j] for j in range(K))

def _partial_rope(u, pos):
    half = ROPE_DIM // 2
    inv = jnp.power(jnp.float32(ROPE_THETA), -jnp.arange(half, dtype=jnp.float32) * (2.0 / ROPE_DIM))
    ang = pos.astype(jnp.float32)[..., None] * inv
    cos = jnp.cos(ang)[:, :, None, :]
    sin = jnp.sin(ang)[:, :, None, :]
    u1 = u[..., :half]
    u2 = u[..., half:ROPE_DIM]
    r1 = u1 * cos - u2 * sin
    r2 = u2 * cos + u1 * sin
    return jnp.concatenate([r1.astype(u.dtype), r2.astype(u.dtype), u[..., ROPE_DIM:]], axis=-1)

def _mlstm(q, k, v, i_pre, f_pre):
    B, T, H, d = q.shape
    L = M_CHUNK
    NC = T // L
    k = k * (d ** -0.5)

    def to_chunks(a):
        a = a.reshape((B, NC, L, H) + a.shape[3:])
        return jnp.moveaxis(a, (1, 3), (0, 2))

    log_f = jax.nn.log_sigmoid(f_pre)
    log_i = i_pre
    causal = jnp.tril(jnp.ones((L, L), dtype=bool))

    def step(carry, xs):
        C, n, m = carry
        qc, kc, vc, li, lf = xs
        a = jnp.cumsum(lf, axis=-1)
        A = a[..., -1]
        logD = a[..., :, None] - a[..., None, :] + li[..., None, :]
        logD = jnp.where(causal, logD, -jnp.inf)
        inter = a + m[..., None]
        m_t = jnp.maximum(inter, jnp.max(logD, axis=-1))
        w_inter = jnp.exp(inter - m_t)
        s = jnp.einsum('bhld,bhsd->bhls', qc, kc) * jnp.exp(logD - m_t[..., None])
        num = w_inter[..., None] * jnp.einsum('bhld,bhde->bhle', qc, C) + jnp.einsum('bhls,bhse->bhle', s, vc)
        den = w_inter * jnp.einsum('bhld,bhd->bhl', qc, n) + jnp.sum(s, axis=-1)
        h = num / jnp.maximum(jnp.abs(den), jnp.exp(-m_t))[..., None]
        logw = A[..., None] - a + li
        m_new = jnp.maximum(A + m, jnp.max(logw, axis=-1))
        wk = jnp.exp(logw - m_new[..., None])
        decay = jnp.exp(A + m - m_new)
        C_new = decay[..., None, None] * C + jnp.einsum('bhs,bhsd,bhse->bhde', wk, kc, vc)
        n_new = decay[..., None] * n + jnp.einsum('bhs,bhsd->bhd', wk, kc)
        return (C_new, n_new, m_new), h

    init = (jnp.zeros((B, H, d, d), jnp.float32), jnp.zeros((B, H, d), jnp.float32),
            jnp.zeros((B, H), jnp.float32))
    xs = (to_chunks(q), to_chunks(k), to_chunks(v), to_chunks(log_i), to_chunks(log_f))
    _, hs = lax.scan(step, init, xs)
    hs = jnp.moveaxis(hs, (0, 2), (1, 3))
    return hs.reshape(B, T, H, d)

def _head_layernorm(h, g):
    B, T = h.shape[0], h.shape[1]
    mu = jnp.mean(h, axis=-1, keepdims=True)
    var = jnp.mean(jnp.square(h - mu), axis=-1, keepdims=True)
    hn = (h - mu) * lax.rsqrt(var + NORM_EPS)
    return hn.reshape(B, T, -1) * g

def _compress(kv, pos_emb, w1, w2):
    B, T, G, dk = kv.shape
    n_cmp = (T - CMP_BLOCK) // CMP_STRIDE + 1
    idx = jnp.arange(n_cmp)[:, None] * CMP_STRIDE + jnp.arange(CMP_BLOCK)[None, :]
    blocks = kv[:, idx] + pos_emb[None, None, :, None, :]
    blocks = jnp.moveaxis(blocks, 3, 1).reshape(B, G, n_cmp, CMP_BLOCK * dk)
    return jax.nn.gelu(blocks @ w1) @ w2

def _nsa(q_raw, q_rope, kc, vc, ks, vs, kw, vw, gates):
    B, G, h, T, dk = q_raw.shape
    n_cmp = kc.shape[2]
    n_sel = T // SEL_BLOCK
    n_top = min(SEL_TOPK, n_sel)
    scale = dk ** -0.5
    cmp_end = jnp.arange(n_cmp) * CMP_STRIDE + (CMP_BLOCK - 1)
    ci = jnp.arange(n_cmp)[:, None] * CMP_STRIDE
    sj = jnp.arange(n_sel)[None, :] * SEL_BLOCK
    overlap = ((ci < sj + SEL_BLOCK) & (ci + CMP_BLOCK > sj)).astype(jnp.float32)
    ks_blocks = ks.reshape(B, G, n_sel, SEL_BLOCK, dk)
    vs_blocks = vs.reshape(B, G, n_sel, SEL_BLOCK, dk)
    kw_pad = jnp.pad(kw, ((0, 0), (0, 0), (WINDOW, 0), (0, 0)))
    vw_pad = jnp.pad(vw, ((0, 0), (0, 0), (WINDOW, 0), (0, 0)))
    bi = jnp.arange(B)[:, None, None, None]
    gi = jnp.arange(G)[None, :, None, None]
    blk = jnp.arange(n_sel)

    def block(i):
        t0 = i * Q_BLOCK
        tq = t0 + jnp.arange(Q_BLOCK)
        qr = lax.dynamic_slice_in_dim(q_raw, t0, Q_BLOCK, axis=3)
        qp = lax.dynamic_slice_in_dim(q_rope, t0, Q_BLOCK, axis=3)
        g = lax.dynamic_slice_in_dim(gates, t0, Q_BLOCK, axis=3)
        s_c = jnp.einsum('bghqd,bgnd->bghqn', qr, kc).astype(jnp.float32) * scale
        m_c = cmp_end[None, :] <= tq[:, None]
        p_c = jax.nn.softmax(jnp.where(m_c, s_c, NEG), axis=-1) * m_c
        o_c = jnp.einsum('bghqn,bgnd->bghqd', p_c.astype(vc.dtype), vc)
        imp = jnp.einsum('bghqn,ns->bgqs', p_c, overlap)
        cur = tq // SEL_BLOCK
        forced = (blk[None, :] == 0) | (blk[None, :] == cur[:, None]) | (blk[None, :] == cur[:, None] - 1)
        valid = blk[None, :] * SEL_BLOCK <= tq[:, None]
        score = jnp.where(forced, FORCE, jnp.where(valid, imp, -1.0))
        _, idx = lax.top_k(score, n_top)
        kg = ks_blocks[bi, gi, idx]
        vg = vs_blocks[bi, gi, idx]
        kpos = idx[..., None] * SEL_BLOCK + jnp.arange(SEL_BLOCK)
        m_s = kpos <= tq[:, None, None]
        s_s = jnp.einsum('bghqd,bgqnsd->bghqns', qp, kg).astype(jnp.float32) * scale
        s_s = jnp.where(m_s[:, :, None], s_s, NEG).reshape(B, G, h, Q_BLOCK, n_top * SEL_BLOCK)
        p_s = jax.nn.softmax(s_s, axis=-1).reshape(B, G, h, Q_BLOCK, n_top, SEL_BLOCK)
        o_s = jnp.einsum('bghqns,bgqnsd->bghqd', p_s.astype(vg.dtype), vg)
        kwb = lax.dynamic_slice_in_dim(kw_pad, t0, Q_BLOCK + WINDOW, axis=2)
        vwb = lax.dynamic_slice_in_dim(vw_pad, t0, Q_BLOCK + WINDOW, axis=2)
        wpos = t0 - WINDOW + jnp.arange(Q_BLOCK + WINDOW)
        diff = tq[:, None] - wpos[None, :]
        m_w = (diff >= 0) & (diff < WINDOW) & (wpos[None, :] >= 0)
        s_w = jnp.einsum('bghqd,bgkd->bghqk', qp, kwb).astype(jnp.float32) * scale
        p_w = jax.nn.softmax(jnp.where(m_w, s_w, NEG), axis=-1)
        o_w = jnp.einsum('bghqk,bgkd->bghqd', p_w.astype(vwb.dtype), vwb)
        return g[..., 0:1] * o_c + g[..., 1:2] * o_s + g[..., 2:3] * o_w

    out = lax.map(block, jnp.arange(T // Q_BLOCK))
    out = jnp.moveaxis(out, 0, 3).reshape(B, G, h, T, dk)
    return out.transpose(0, 3, 1, 2, 4).reshape(B, T, G * h * dk)

def first_inputs(seed: int = 0) -> dict:
    key = jax.random.key(seed)
    ks = jax.random.split(key, 24)
    f32 = jnp.float32

    def nrm(k, shape, scale):
        return jax.random.normal(k, shape, f32) * scale

    x = nrm(ks[0], (BATCH, SEQ, D_MODEL), 1.0)
    positions = jnp.tile(jnp.arange(SEQ, dtype=jnp.int32)[None, :], (BATCH, 1))
    norm_g = 1.0 + nrm(ks[1], (DEPTH, D_MODEL), 0.05)
    w_in = nrm(ks[2], (DEPTH, D_MODEL, IN_WIDTH), D_MODEL ** -0.5)
    conv_q_w = nrm(ks[3], (DEPTH, CONV_WIDTH, M_WIDTH), CONV_WIDTH ** -0.5)
    conv_q_b = nrm(ks[4], (DEPTH, M_WIDTH), 0.02)
    conv_k_w = nrm(ks[5], (DEPTH, CONV_WIDTH, M_WIDTH), CONV_WIDTH ** -0.5)
    conv_k_b = nrm(ks[6], (DEPTH, M_WIDTH), 0.02)
    b_igate = nrm(ks[7], (DEPTH, M_HEADS), 0.1)
    b_fgate = jnp.linspace(3.0, 6.0, M_HEADS, dtype=f32)[None, :] + nrm(ks[8], (DEPTH, M_HEADS), 0.1)
    mh_norm_g = 1.0 + nrm(ks[9], (DEPTH, M_WIDTH), 0.05)
    cmp_pos_k = nrm(ks[10], (DEPTH, CMP_BLOCK, N_HEAD_DIM), 0.1)
    cmp_w1_k = nrm(ks[11], (DEPTH, CMP_BLOCK * N_HEAD_DIM, CMP_HIDDEN), (CMP_BLOCK * N_HEAD_DIM) ** -0.5)
    cmp_w2_k = nrm(ks[12], (DEPTH, CMP_HIDDEN, N_HEAD_DIM), CMP_HIDDEN ** -0.5)
    cmp_pos_v = nrm(ks[13], (DEPTH, CMP_BLOCK, N_HEAD_DIM), 0.1)
    cmp_w1_v = nrm(ks[14], (DEPTH, CMP_BLOCK * N_HEAD_DIM, CMP_HIDDEN), (CMP_BLOCK * N_HEAD_DIM) ** -0.5)
    cmp_w2_v = nrm(ks[15], (DEPTH, CMP_HIDDEN, N_HEAD_DIM), CMP_HIDDEN ** -0.5)
    b_nsa_gate = nrm(ks[16], (DEPTH, 3 * N_HEADS), 0.1)
    w_branch_a = nrm(ks[17], (DEPTH, M_WIDTH, D_MODEL), M_WIDTH ** -0.5)
    w_branch_b = nrm(ks[18], (DEPTH, N_WIDTH, D_MODEL), N_WIDTH ** -0.5)
    w_out = nrm(ks[19], (DEPTH, D_MODEL, D_MODEL), D_MODEL ** -0.5)
    final_norm_g = 1.0 + nrm(ks[20], (D_MODEL,), 0.05)
    return {"x": x, "positions": positions, "norm_g": norm_g, "w_in": w_in,
            "conv_q_w": conv_q_w, "conv_q_b": conv_q_b, "conv_k_w": conv_k_w, "conv_k_b": conv_k_b,
            "b_igate": b_igate, "b_fgate": b_fgate, "mh_norm_g": mh_norm_g,
            "cmp_pos_k": cmp_pos_k, "cmp_w1_k": cmp_w1_k, "cmp_w2_k": cmp_w2_k,
            "cmp_pos_v": cmp_pos_v, "cmp_w1_v": cmp_w1_v, "cmp_w2_v": cmp_w2_v,
            "b_nsa_gate": b_nsa_gate, "w_branch_a": w_branch_a, "w_branch_b": w_branch_b,
            "w_out": w_out, "final_norm_g": final_norm_g}

def first_block(x, positions, norm_g, w_in, conv_q_w, conv_q_b, conv_k_w, conv_k_b, b_igate, b_fgate,
              mh_norm_g, cmp_pos_k, cmp_w1_k, cmp_w2_k, cmp_pos_v, cmp_w1_v, cmp_w2_v, b_nsa_gate,
              w_branch_a, w_branch_b, w_out, final_norm_g):
    B, T, _ = x.shape
    f32 = jnp.float32
    for l in range(DEPTH):
        hN = _rmsnorm(x, norm_g[l])
        p = _split_in(hN @ w_in[l])
        mq = jax.nn.silu(_causal_dwconv(p["m_q"], conv_q_w[l], conv_q_b[l]))
        mk = jax.nn.silu(_causal_dwconv(p["m_k"], conv_k_w[l], conv_k_b[l]))
        mh = _mlstm(mq.reshape(B, T, M_HEADS, M_HEAD_DIM).astype(f32),
                    mk.reshape(B, T, M_HEADS, M_HEAD_DIM).astype(f32),
                    p["m_v"].reshape(B, T, M_HEADS, M_HEAD_DIM).astype(f32),
                    (p["m_i"] + b_igate[l]).astype(f32),
                    (p["m_f"] + b_fgate[l]).astype(f32))
        mh = _head_layernorm(mh, mh_norm_g[l]).astype(x.dtype)
        ya = jax.nn.sigmoid(p["m_o"]) * mh * jax.nn.silu(p["m_z"])
        nq = p["n_q"].reshape(B, T, N_HEADS, N_HEAD_DIM)
        q_raw = nq.reshape(B, T, N_KV_GROUPS, N_HPG, N_HEAD_DIM).transpose(0, 2, 3, 1, 4)
        q_rope = _partial_rope(nq, positions).reshape(B, T, N_KV_GROUPS, N_HPG, N_HEAD_DIM).transpose(0, 2, 3, 1, 4)

        def kvh(a):
            return a.reshape(B, T, N_KV_GROUPS, N_HEAD_DIM)

        kc = _compress(kvh(p["n_kc"]), cmp_pos_k[l], cmp_w1_k[l], cmp_w2_k[l])
        vc = _compress(kvh(p["n_vc"]), cmp_pos_v[l], cmp_w1_v[l], cmp_w2_v[l])
        ks = _partial_rope(kvh(p["n_ks"]), positions).transpose(0, 2, 1, 3)
        vs = kvh(p["n_vs"]).transpose(0, 2, 1, 3)
        kw = _partial_rope(kvh(p["n_kw"]), positions).transpose(0, 2, 1, 3)
        vw = kvh(p["n_vw"]).transpose(0, 2, 1, 3)
        gates = jax.nn.sigmoid(p["n_g"] + b_nsa_gate[l]).reshape(B, T, N_KV_GROUPS, N_HPG, 3).transpose(0, 2, 3, 1, 4)
        yn = _nsa(q_raw, q_rope, kc, vc, ks, vs, kw, vw, gates)
        yb = yn * jax.nn.silu(p["n_z"])
        merged = (jax.nn.sigmoid(p["g_a"]) * (ya @ w_branch_a[l])
                  + jax.nn.sigmoid(p["g_b"]) * (yb @ w_branch_b[l]))
        x = x + merged @ w_out[l]
    return _rmsnorm(x, final_norm_g)


POOL_WINDOWS = (2, 4, 8, 16)
POOL_GROUPS = len(POOL_WINDOWS)
POOL_GROUP_DIM = D_MODEL // 8
POOL_WIDTH = POOL_GROUPS * POOL_GROUP_DIM
DN_HEAD_DIM = 128
DN_HEADS = D_MODEL // 128
DN_WIDTH = DN_HEADS * DN_HEAD_DIM
CHUNK = 64
FFN_HIDDEN = ((8 * D_MODEL // 3) + 127) // 128 * 128
N_SUBLAYERS = 3
RMS_EPS = 1e-6
L2_EPS = 1e-6
MIX_IN_SIZES = (POOL_WIDTH, DN_WIDTH, DN_WIDTH, DN_WIDTH, DN_WIDTH, DN_HEADS, DN_HEADS, D_MODEL, D_MODEL)
MIX_IN_WIDTH = int(sum(MIX_IN_SIZES))
MIX_IN_SPLITS = tuple(int(s) for s in np.cumsum(MIX_IN_SIZES)[:-1])


def rms_norm(x, g):
    xf = x.astype(jnp.float32)
    xf = xf * lax.rsqrt(jnp.mean(xf * xf, axis=-1, keepdims=True) + RMS_EPS)
    return (xf * g.astype(jnp.float32)).astype(x.dtype)

def l2_normalize(x):
    return x * lax.rsqrt(jnp.sum(x * x, axis=-1, keepdims=True) + L2_EPS)

def modulate(h, shift, scale):
    return h * (1.0 + scale[:, None, :]) + shift[:, None, :]

def swiglu(h, w_in, w_out):
    gate, up = jnp.split(h @ w_in, 2, axis=-1)
    return (jax.nn.silu(gate) * up) @ w_out

def causal_depthwise_conv(x, w):
    C = x.shape[-1]
    return lax.conv_general_dilated(
        x, w[:, None, :].astype(x.dtype), window_strides=(1,),
        padding=[(CONV_WIDTH - 1, 0)],
        dimension_numbers=('NWC', 'WIO', 'NWC'), feature_group_count=C)

def multiscale_pool(xp):
    T = xp.shape[1]
    xf = xp.astype(jnp.float32)
    cs = jnp.cumsum(xf, axis=1)
    pos = jnp.arange(1, T + 1, dtype=jnp.float32)[:, None]
    outs = []
    for gi, w in enumerate(POOL_WINDOWS):
        sl = slice(gi * POOL_GROUP_DIM, (gi + 1) * POOL_GROUP_DIM)
        c_g = cs[..., sl]
        lagged = jnp.pad(c_g, ((0, 0), (w, 0), (0, 0)))[:, :T]
        mean = (c_g - lagged) / jnp.minimum(pos, float(w))
        outs.append(mean - xf[..., sl])
    return jnp.stack(outs, axis=2).astype(xp.dtype)

def gated_delta_rule_chunked(q, k, v, g, beta):
    B, T, H, K = q.shape
    V = v.shape[-1]
    N = T // CHUNK

    def to_chunks(a):
        a = a.reshape((B, N, CHUNK, H) + a.shape[3:])
        return jnp.moveaxis(a, (1, 3), (0, 2))

    qc, kc, vc, bc = to_chunks(q), to_chunks(k), to_chunks(v), to_chunks(beta)
    gc = jnp.cumsum(to_chunks(g), axis=-1)
    causal = jnp.tril(jnp.ones((CHUNK, CHUNK), dtype=bool))
    strict = jnp.tril(jnp.ones((CHUNK, CHUNK), dtype=bool), -1)
    decay = jnp.exp(jnp.where(causal, gc[..., :, None] - gc[..., None, :], -jnp.inf))
    kk = jnp.einsum('nbhik,nbhjk->nbhij', kc, kc)
    a_mat = jnp.where(strict, bc[..., :, None] * kk * decay, 0.0)
    eye = jnp.eye(CHUNK, dtype=q.dtype)
    rhs = jnp.concatenate([bc[..., None] * vc, (bc * jnp.exp(gc))[..., None] * kc], axis=-1)
    sol = lax.linalg.triangular_solve(a_mat + eye, rhs, left_side=True, lower=True,
                                      unit_diagonal=True)
    u, w = sol[..., :V], sol[..., V:]
    qk = jnp.where(causal, jnp.einsum('nbhik,nbhjk->nbhij', qc, kc) * decay, 0.0)
    q_dec = qc * jnp.exp(gc)[..., None]
    g_last = gc[..., -1]
    k_dec = kc * jnp.exp(g_last[..., None] - gc)[..., None]

    def step(S, xs):
        q_i, qk_i, u_i, w_i, k_i, gl_i = xs
        v_new = u_i - jnp.einsum('bhck,bhkv->bhcv', w_i, S)
        o_i = jnp.einsum('bhck,bhkv->bhcv', q_i, S) + jnp.einsum('bhij,bhjv->bhiv', qk_i, v_new)
        S = S * jnp.exp(gl_i)[..., None, None] + jnp.einsum('bhck,bhcv->bhkv', k_i, v_new)
        return S, o_i

    S0 = jnp.zeros((B, H, K, V), dtype=q.dtype)
    _, o = lax.scan(step, S0, (q_dec, qk, u, w, k_dec, g_last))
    return jnp.moveaxis(o, (0, 2), (1, 3)).reshape(B, T, H, V)

def token_mixer(h, mix_w_in, conv_w, a_log, dt_bias, dn_norm_g, pool_w, pool_scale,
                pool_proj, dn_proj, mix_w_out):
    B, T, _ = h.shape
    proj = h @ mix_w_in
    xp, q, k, v, z, b_raw, a_raw, g_pool, g_dn = jnp.split(proj, MIX_IN_SPLITS, axis=-1)

    pooled = multiscale_pool(xp)
    ya = jnp.einsum('btgc,gcd->btgd', pooled, pool_w).reshape(B, T, POOL_WIDTH) * pool_scale
    ya = ya @ pool_proj

    qkv = jax.nn.silu(causal_depthwise_conv(jnp.concatenate([q, k, v], axis=-1), conv_w))
    qkv = qkv.astype(jnp.float32).reshape(B, T, 3, DN_HEADS, DN_HEAD_DIM)
    qh = l2_normalize(qkv[:, :, 0]) * (DN_HEAD_DIM ** -0.5)
    kh = l2_normalize(qkv[:, :, 1])
    vh = qkv[:, :, 2]
    beta = jax.nn.sigmoid(b_raw.astype(jnp.float32))
    g = -jnp.exp(a_log.astype(jnp.float32)) * jax.nn.softplus(
        a_raw.astype(jnp.float32) + dt_bias.astype(jnp.float32))
    o = gated_delta_rule_chunked(qh, kh, vh, g, beta)
    o = rms_norm(o, dn_norm_g).astype(h.dtype).reshape(B, T, DN_WIDTH) * jax.nn.silu(z)
    yb = o @ dn_proj

    merged = jax.nn.sigmoid(g_pool) * ya + jax.nn.sigmoid(g_dn) * yb
    return merged @ mix_w_out

def second_inputs(seed: int = 0) -> dict:
    key = jax.random.key(seed)
    ks = jax.random.split(key, 20)
    D, L, F = D_MODEL, DEPTH, FFN_HIDDEN

    def nrm(k, shape, fan_in):
        return jax.random.normal(k, shape, jnp.float32) * fan_in ** -0.5

    x = jax.random.normal(ks[0], (BATCH, SEQ, D), jnp.float32)
    c = jax.random.normal(ks[1], (BATCH, D), jnp.float32)
    ada_w = 0.5 * nrm(ks[2], (L, D, N_SUBLAYERS * 3 * D), D)
    ada_b = 0.01 * jax.random.normal(ks[3], (L, N_SUBLAYERS * 3 * D), jnp.float32)
    norm_g = 1.0 + 0.05 * jax.random.normal(ks[4], (L, N_SUBLAYERS, D), jnp.float32)
    ffn1_w_in = nrm(ks[5], (L, D, 2 * F), D)
    ffn1_w_out = nrm(ks[6], (L, F, D), F)
    ffn2_w_in = nrm(ks[7], (L, D, 2 * F), D)
    ffn2_w_out = nrm(ks[8], (L, F, D), F)
    mix_w_in = nrm(ks[9], (L, D, MIX_IN_WIDTH), D)
    conv_w = nrm(ks[10], (L, CONV_WIDTH, 3 * DN_WIDTH), CONV_WIDTH)
    a_log = jnp.log(jax.random.uniform(ks[11], (L, DN_HEADS), jnp.float32, minval=1.0, maxval=16.0))
    dt = jnp.exp(jax.random.uniform(ks[12], (L, DN_HEADS), jnp.float32,
                                    minval=math.log(1e-3), maxval=math.log(1e-1)))
    dt_bias = dt + jnp.log(-jnp.expm1(-dt))
    dn_norm_g = 1.0 + 0.05 * jax.random.normal(ks[13], (L, DN_HEAD_DIM), jnp.float32)
    pool_w = nrm(ks[14], (L, POOL_GROUPS, POOL_GROUP_DIM, POOL_GROUP_DIM), POOL_GROUP_DIM)
    pool_scale = 1.0 + 0.1 * jax.random.normal(ks[15], (L, POOL_WIDTH), jnp.float32)
    pool_proj = nrm(ks[16], (L, POOL_WIDTH, D), POOL_WIDTH)
    dn_proj = nrm(ks[17], (L, DN_WIDTH, D), DN_WIDTH)
    mix_w_out = nrm(ks[18], (L, D, D), D)
    final_g = 1.0 + 0.05 * jax.random.normal(ks[19], (D,), jnp.float32)
    return {"x": x, "c": c, "ada_w": ada_w, "ada_b": ada_b, "norm_g": norm_g,
            "ffn1_w_in": ffn1_w_in, "ffn1_w_out": ffn1_w_out,
            "ffn2_w_in": ffn2_w_in, "ffn2_w_out": ffn2_w_out,
            "mix_w_in": mix_w_in, "conv_w": conv_w, "a_log": a_log, "dt_bias": dt_bias,
            "dn_norm_g": dn_norm_g, "pool_w": pool_w, "pool_scale": pool_scale,
            "pool_proj": pool_proj, "dn_proj": dn_proj, "mix_w_out": mix_w_out,
            "final_g": final_g}

def second_block(x, c, ada_w, ada_b, norm_g, ffn1_w_in, ffn1_w_out, ffn2_w_in, ffn2_w_out,
              mix_w_in, conv_w, a_log, dt_bias, dn_norm_g, pool_w, pool_scale, pool_proj,
              dn_proj, mix_w_out, final_g):
    B = x.shape[0]
    for l in range(DEPTH):
        mod = (jax.nn.silu(c) @ ada_w[l] + ada_b[l]).reshape(B, N_SUBLAYERS, 3, D_MODEL)
        shift, scale, gate = mod[:, :, 0], mod[:, :, 1], mod[:, :, 2]

        h = modulate(rms_norm(x, norm_g[l, 0]), shift[:, 0], scale[:, 0])
        x = x + 0.5 * gate[:, 0, None, :] * swiglu(h, ffn1_w_in[l], ffn1_w_out[l])

        h = modulate(rms_norm(x, norm_g[l, 1]), shift[:, 1], scale[:, 1])
        x = x + gate[:, 1, None, :] * token_mixer(
            h, mix_w_in[l], conv_w[l], a_log[l], dt_bias[l], dn_norm_g[l], pool_w[l],
            pool_scale[l], pool_proj[l], dn_proj[l], mix_w_out[l])

        h = modulate(rms_norm(x, norm_g[l, 2]), shift[:, 2], scale[:, 2])
        x = x + 0.5 * gate[:, 2, None, :] * swiglu(h, ffn2_w_in[l], ffn2_w_out[l])
    return rms_norm(x, final_g)


def setup_inputs(seed=0):
    out = dict(first_inputs(seed))
    for name, value in second_inputs(seed + 1).items():
        if name != "x":
            out[name + "_2"] = value
    return out


def reference(
    x, positions, norm_g, w_in, conv_q_w, conv_q_b, conv_k_w, conv_k_b, b_igate, b_fgate,
    mh_norm_g, cmp_pos_k, cmp_w1_k, cmp_w2_k, cmp_pos_v, cmp_w1_v, cmp_w2_v, b_nsa_gate,
    w_branch_a, w_branch_b, w_out, final_norm_g, c_2, ada_w_2, ada_b_2, norm_g_2, ffn1_w_in_2,
    ffn1_w_out_2, ffn2_w_in_2, ffn2_w_out_2, mix_w_in_2, conv_w_2, a_log_2, dt_bias_2,
    dn_norm_g_2, pool_w_2, pool_scale_2, pool_proj_2, dn_proj_2, mix_w_out_2, final_g_2,
):
    x = first_block(
        x, positions, norm_g, w_in, conv_q_w, conv_q_b, conv_k_w, conv_k_b, b_igate, b_fgate,
        mh_norm_g, cmp_pos_k, cmp_w1_k, cmp_w2_k, cmp_pos_v, cmp_w1_v, cmp_w2_v, b_nsa_gate,
        w_branch_a, w_branch_b, w_out, final_norm_g,
    )
    return second_block(
        x, c_2, ada_w_2, ada_b_2, norm_g_2, ffn1_w_in_2, ffn1_w_out_2, ffn2_w_in_2,
        ffn2_w_out_2, mix_w_in_2, conv_w_2, a_log_2, dt_bias_2, dn_norm_g_2, pool_w_2,
        pool_scale_2, pool_proj_2, dn_proj_2, mix_w_out_2, final_g_2,
    )


_drawn_inputs = setup_inputs


def setup_inputs(seed=0):
    import zlib

    import numpy as np

    out = dict(_drawn_inputs(seed))
    spreads = {}
    factors = {'norm_g': 2.865,
     'conv_q_b': 27.632,
     'conv_k_b': 34.373,
     'b_igate': 64.0,
     'mh_norm_g': 6.565,
     'cmp_pos_k': 8.0,
     'cmp_w1_k': 3.3,
     'cmp_w2_k': 3.124,
     'cmp_pos_v': 6.101,
     'b_nsa_gate': 8.0,
     'ada_b_2': 6.422,
     'norm_g_2': 3.548,
     'a_log_2': 2.925,
     'dn_norm_g_2': 8.0,
     'pool_scale_2': 3.86}
    for name, (base, spread) in spreads.items():
        noise = np.random.default_rng([zlib.crc32(name.encode()), seed]).standard_normal(out[name].shape)
        drawn = base * np.exp(spread * noise) if base else spread * noise
        out[name] = __import__('jax').numpy.asarray(drawn.astype(out[name].dtype))
    for name, factor in factors.items():
        out[name] = (out[name] * factor).astype(out[name].dtype)
    return out
```

```python
from contextlib import ExitStack

import numpy as np

import concourse.bass as bass
from concourse import mybir

F32 = mybir.dt.float32
F32R = mybir.dt.float32r
I32 = mybir.dt.int32
ALU = mybir.AluOpType
ACT = mybir.ActivationFunctionType
AX = mybir.AxisListType.X
ds = bass.ds

P = 128
T = 512
NT = T // P
D = 1024
KD = D // P
EPS = 1e-6
NEG = -1e30

MH, MD = 4, 256
NHD, NG, DK = 8, 2, 64
C_Q, C_K, C_V, C_O, C_Z = 0, 1024, 2048, 3072, 4096
C_I, C_F = 5120, 5124
C_NQ, C_KC, C_VC, C_KS, C_VS, C_KW, C_VW = 5128, 5640, 5768, 5896, 6024, 6152, 6280
C_NG, C_NZ, C_GA, C_GB = 6408, 6432, 6944, 7968
CB, CS, CH = 32, 16, 128
NC = (T - CB) // CS + 1
ROPE_HALF = 8
X_P, X_Q, X_Z, X_B, X_A, X_GP, X_GD = 0, 512, 3584, 4608, 4616, 4624, 5648
DH = 8
FF = 2816
NF = FF // P
LEVELS = 7

K_ID, K_ONE, K_CM, K_CMT, K_ROPE, K_SWAP, K_LV = 0, 128, 256, 768, 896, 1024, 1152
K_CA = K_LV + LEVELS * P
K_CK = K_CA + 128
K_FIX = K_CK + 128
K_INV = K_FIX + 64
K_ALL = K_INV + 1


def constants():
    c = np.zeros((P, K_ALL), np.float32)
    r = np.arange(P)
    c[:, K_ID:K_ID + P] = np.eye(P)
    c[:, K_ONE:K_ONE + P] = 1
    c[:, K_CM + 384:K_CM + 512] = np.where(r[None, :] <= r[:, None], 0, NEG)
    c[:, K_CMT:K_CMT + P] = np.where(r[None, :] >= r[:, None], 0, NEG)
    for k in range(P):
        d = k % DK
        if d < ROPE_HALF:
            c[k, K_ROPE + k + ROPE_HALF] = 1
            c[k, K_INV] = np.power(np.float32(500000.0), np.float32(-d * (2.0 / 16)))
        elif d < 2 * ROPE_HALF:
            c[k, K_ROPE + k - ROPE_HALF] = -1
            c[k, K_INV] = np.power(np.float32(500000.0), np.float32(-(d - ROPE_HALF) * (2.0 / 16)))
        c[k, K_SWAP + (k + DK) % P] = 1
    for lv in range(LEVELS):
        b = 1 << lv
        i, j = r[None, :], r[:, None]
        c[:, K_LV + lv * P:K_LV + lv * P + P] = (i // (2 * b) == j // (2 * b)) & (i // b % 2 == 1) & (j // b % 2 == 0)
    t = (np.arange(NT)[None, :, None] * P + r[:, None, None])
    n = np.arange(32)[None, None, :]
    ok = (n * CS + CB - 1 <= t) & (n < NC)
    c[:, K_CA:K_CA + 128] = np.where(ok, 0, NEG).reshape(P, 128)
    c[:, K_CK:K_CK + 128] = ok.reshape(P, 128)
    for g in range(4):
        w = 2 << g
        c[:, K_FIX + 16 * g:K_FIX + 16 * g + 16] = w / np.minimum(np.arange(1, 17), w)
    return c


G1, CQW, CQB, MHG, FNG = 0, 8, 72, 88, 96
N1 = 104
G2, CW2 = N1, N1 + 24
N2 = 120
ADAB, DNG, PSC, FG2, CVEC = N1 + N2, N1 + N2 + 72, N1 + N2 + 73, N1 + N2 + 77, N1 + N2 + 85
N3 = 93
MOD = N1 + N2 + N3
COEF = MOD + 72
SILC = COEF + 8
SMB = SILC + 8
ALOG, DTB = SMB + 1, SMB + 2
POST = SMB + 3
MVS = POST + 64
RST = MVS + 32
NE = RST + 16
DEN = NE + 16
BST = DEN + 4
MX = BST + 6
SUM = MX + 8
AG = SUM + 8
KCT = AG + 8
CMX = KCT + 64
EG = CMX + 64
EKD = EG + 32
QEG = EKD + 32
EGL = QEG + 32
RSO = EGL + 8
HALF = RSO + 8
PAR_ALL = HALF + 8


class Count:

    def __init__(self, eng, sem):
        self.eng, self.sem, self.n, self.i, self.step = eng, sem, 0, 0, 0

    def mark(self, ins):
        ins.then_inc(self.sem, 1)
        self.n += 1
        return self.n

    def wait(self, n=None):
        n = self.n if n is None else n
        self.eng.wait_ge(self.sem, self.i * self.step + n if self.step else n)

    def loop(self, times, step, body):
        start, self.step = self.n, step
        with self.eng.Fori(0, times) as i:
            self.i = i
            body(i)
            assert self.n - start == step, (self.n - start, step)
        self.i, self.step = 0, 0
        self.n = start + times * step


def two_blocks(nc, cst, x, positions, norm_g, w_in, conv_q_w, conv_q_b, conv_k_w, conv_k_b, b_igate,
               b_fgate, mh_norm_g, cmp_pos_k, cmp_w1_k, cmp_w2_k, cmp_pos_v, cmp_w1_v, cmp_w2_v,
               b_nsa_gate, w_branch_a, w_branch_b, w_out, final_norm_g, c_2, ada_w_2, ada_b_2,
               norm_g_2, ffn1_w_in_2, ffn1_w_out_2, ffn2_w_in_2, ffn2_w_out_2, mix_w_in_2, conv_w_2,
               a_log_2, dt_bias_2, dn_norm_g_2, pool_w_2, pool_scale_2, pool_proj_2, dn_proj_2,
               mix_w_out_2, final_g_2, out):
    ctx = ExitStack()
    with ctx:
        BASE = 16512
        assert nc.sbuf_base <= BASE
        at = [BASE]
        KB = 1024

        def fixed(name, shape, dt=F32):
            t = nc.alloc_sbuf_tensor_at(name, [P, *shape], dt, offset=at[0])
            at[0] += -(-int(np.prod(shape)) * 4 // 32) * 32
            return t

        XT = fixed("residual", [KD, T])
        HHI, HLO = fixed("act_hi", [KD, T], F32R), fixed("act_lo", [KD, T], F32R)
        RAW = fixed("w_raw", [4, 1024])
        WHI, WLO = fixed("w_hi", [4, 1024], F32R), fixed("w_lo", [4, 1024], F32R)
        CST = fixed("constants", [K_ALL])
        PAR = fixed("params", [PAR_ALL])
        PH = at[0]

        def phase(name, kb, shape, dt=F32):
            off = PH + int(kb * KB)
            assert off + int(np.prod(shape)) * 4 <= 229344, (name, off, shape)
            return nc.alloc_sbuf_tensor_at(name, [P, *shape], dt, offset=off)

        XTOK = phase("x_tokens", 0, [NT, D])
        PROW = phase("param_rows", 16, [4, P])
        SQ = phase("squares", 88, [2, T])
        RMS = phase("rms_recip", 92, [T])
        QK1 = phase("mlstm_qk_T", 0, [16, T])
        MTOK = phase("mlstm_h_tokens", 0, [MH, NT, MD])
        VTOK = phase("mlstm_v_tokens", 32, [NT, MH, MD + 1])
        MHT = phase("mlstm_h_T", 32, [KD, T])
        YAHI, YALO = phase("ya_hi", 0, [KD, T], F32R), phase("ya_lo", 16, [KD, T], F32R)
        QRAW = phase("nsa_q_T", 48.25, [4, T])
        KVR = phase("nsa_kv_T", 56.25, [4, T])
        YBHI, YBLO = phase("yb_hi", 48, [4, T], F32R), phase("yb_lo", 56, [4, T], F32R)
        ADAW = phase("ada_w", 66, [2, D])
        ADAC = phase("ada_sum", 74, [D])
        DP = phase("mlstm_decay_probs", 66, [2, 1280])
        VSW = phase("nsa_v_tokens", 78, [NT, 2, P])
        ROW = [phase(f"rows{i}", 82.5 + 2 * i, [T]) for i in range(4)] + [phase("rows4", 92, [T])]
        SMR = phase("gate_rows", 96, [T])
        SM = phase("packed_rows", 94, [T])
        SMT = phase("packed_cols", 96, [NT, P])
        QROPE = phase("nsa_q_rope", 66, [4, T])
        KR = phase("nsa_k_rope", 82.5, [4, T])
        RSIN, RTMP, RCOS = phase("rope_sin", 74, [T]), phase("rope_tmp", 76, [T]), phase("rope_cos", 92, [T])
        HID = phase("cmp_hidden", 90.5, [4, 32])
        VCB = phase("cmp_v_blocks", 94, [4, DK])
        POSI = phase("positions", 82.5, [T], I32)
        ANG, TRN = phase("angles", 84.5, [T]), phase("turns", 86.5, [T])
        W1 = phase("cmp_w1", 32, [CB, CH])
        W2 = phase("cmp_w2", 92, [2, P])
        BLK = phase("cmp_blocks", 74, [CB, NC])
        SC = phase("cmp_scores", 32, [NT, 2, 4, 32])
        PCT = phase("cmp_probs_T", 36, [NT, 2, P])
        PR = phase("nsa_probs", 32, [2, T])
        PT = phase("nsa_probs_T", 36, [2, T])
        YTOK = phase("nsa_y_tokens", 40, [NT, 4, 2, DK])
        OTMP = phase("nsa_o_tmp", 74, [T])
        YT = phase("nsa_y_T", 66, [4, T])
        MGHI, MGLO = phase("merged_hi", 72, [KD, T], F32R), phase("merged_lo", 32, [KD, T], F32R)
        GT = phase("merge_gates", 64, [4, T])
        NZS = phase("nz_gates", 74, [2, T])
        HIDHI, HIDLO = phase("ffn_hi", 0, [NF, T], F32R), phase("ffn_lo", 44, [NF, T], F32R)
        FS = phase("ffn_tmp", 88, [4, T])
        QKV = phase("delta_qkv_T", 0, [24, T])
        DD, MT, TT, TI = (phase(n, 48 + 4 * i, [DH, P]) for i, n in enumerate(
            ["delta_decay", "delta_a_T", "delta_inv_T", "delta_inv"]))
        XX, QKM, KDT, RV = (phase(n, 64 + 4 * i, [DH, P]) for i, n in enumerate(
            ["delta_x", "delta_qk_T", "delta_k_dec", "delta_rhs"]))
        VN, SS = phase("delta_v_new", 80, [DH, P]), phase("delta_state", 84, [DH, P])
        ML = phase("delta_level", 80, [DH, P])
        OO = phase("delta_o", 64, [DH, P])
        EROW = [phase(f"delta_rows{i}", 88 + 2 * i, [T]) for i in range(3)]
        NRM, NRT = phase("delta_squares", 48, [2, T]), phase("delta_roots", 52, [2, T])
        LPR = phase("softplus_rows", 56, [3, T])
        TMP2 = phase("z2_gates", 48, [4, T])
        Y2HI, Y2LO = phase("yb2_hi", 0, [KD, T], F32R), phase("yb2_lo", 16, [KD, T], F32R)
        PLHI, PLLO = phase("pool_hi", 48, [4, T], F32R), phase("pool_lo", 56, [4, T], F32R)
        PLW = phase("pool_w", 64, [4, P])
        PLS = phase("pool_sums", 66, [3, T])
        GT2 = phase("merge2_gates", 80, [4, T])
        PLT = phase("pool_out", 72, [T])
        M2HI, M2LO = phase("merged2_hi", 64, [KD, T], F32R), phase("merged2_lo", 32, [KD, T], F32R)
        YTOK2 = phase("out_tokens", 0, [NT, D])

        PS = ctx.enter_context(nc.psum_tensor("psum", [P, 8, 512], F32))
        block = ctx.enter_context(nc.Block())

        names = {}

        def sem(name):
            if name not in names:
                names[name] = ctx.enter_context(nc.semaphore(name))
            return names[name]

        w_loaded = [sem(f"w_loaded{k}") for k in range(4)]
        w_hi, w_lo, chunk_done = sem("w_hi_ready"), sem("w_lo_ready"), sem("chunk_done")
        bank_free = [sem(f"bank_free{k}") for k in range(4)]

        ID = CST[:, K_ID:K_ID + P]
        ONES = CST[:, K_ONE:K_ONE + P]

        def col(n, k=1):
            return PAR[:, n:n + k]

        def wchunk(w, kt0, kts, c0, cols):
            return w[0].rearrange("(kt p) n -> p kt n", p=P)[:, kt0:kt0 + kts, c0:c0 + cols]

        def wdyn(w, kt0, kts, c0, cols):
            return w[0].rearrange("(kt p) n -> p kt n", p=P)[:, kt0:kt0 + kts, ds(c0, cols)]

        def merge_body(wg, ca, cb, wa, ka, wb, kb, nf):
            return lambda i: [c for f in range(nf) for c in (
                (wg, 0, 8, i * (P * nf) + (ca + P * f), P), (wg, 0, 8, i * (P * nf) + (cb + P * f), P),
                (wa, 0, ka, i * (P * nf) + P * f, P), (wb, 0, kb, i * (P * nf) + P * f, P))]

        def cols_body(w, c0, n):
            return lambda i: [(w, 0, 8, i * (P * n) + (c0 + P * f), P) for f in range(n)]

        def ffn_in_body(w):
            return lambda i: [c for f in range(2) for c in (
                (w, 0, 8, i * 256 + P * f, P), (w, 0, 8, i * 256 + (FF + P * f), P))]

        def ffn_out_body(w):
            return lambda i: [(w, k0, kn, i * 512 + P * f, P)
                              for f in range(4) for k0, kn in ((0, 8), (8, 8), (16, 6))]

        STAGES = [
            ("v1", 1, lambda i: [(w_in, 2 * k, 2, C_V + 512 * h, 512) for h in range(2) for k in range(4)], 8),
            ("conv1", 2, cols_body(w_in, C_Q, 8), 8),
            ("small1", 1, lambda i: ["small1"], 1),
            ("nsa1", 1, lambda i: [(w_in, 0, 8, c, P) for c in
                                   [C_NQ + P * f for f in range(4)] + [C_KC, C_VC, C_KS, C_KW]], 8),
            ("vsw1", 1, lambda i: ["vsw0", "vsw1"], 4),
            ("oz1", 2, lambda i: [c for f in range(4) for c in (
                (w_in, 0, 8, i * 512 + (C_O + P * f), P), (w_in, 0, 8, i * 512 + (C_Z + P * f), P))], 8),
            ("nz1", 1, cols_body(w_in, C_NZ, 4), 4),
            ("merge1", 4, merge_body(w_in, C_GA, C_GB, w_branch_a, 8, w_branch_b, 4, 2), 8),
            ("out1", 2, cols_body(w_out, 0, 4), 4),
            ("ffn1_in", 11, ffn_in_body(ffn1_w_in_2), 4),
            ("ffn1_out", 2, ffn_out_body(ffn1_w_out_2), 4),
            ("conv2", 3, cols_body(mix_w_in_2, X_Q, 8), 8),
            ("small2", 1, lambda i: ["small2"], 1),
            ("z2", 2, cols_body(mix_w_in_2, X_Z, 4), 4),
            ("pool2", 1, cols_body(mix_w_in_2, X_P, 4), 4),
            ("merge2", 4, merge_body(mix_w_in_2, X_GP, X_GD, pool_proj_2, 4, dn_proj_2, 8, 2), 8),
            ("out2", 2, cols_body(mix_w_out_2, 0, 4), 4),
            ("ffn2_in", 11, ffn_in_body(ffn2_w_in_2), 4),
            ("ffn2_out", 2, ffn_out_body(ffn2_w_out_2), 4),
        ]
        INFO, c0, t0 = {}, 0, 0
        for name, iters, body, tiles in STAGES:
            nb = len(body(0))
            INFO[name] = dict(iters=iters, body=body, nb=nb, tb=tiles, chunk=c0, tile=t0)
            c0 += iters * nb
            t0 += iters * tiles
        N_CHUNKS = c0
        AHEAD = 2

        class Place:

            def __init__(self, name, i):
                stage = INFO[name]
                self.iters, self.nb, self.tb = stage["iters"], stage["nb"], stage["tb"]
                self.chunk, self.tile, self.i = stage["chunk"], stage["tile"], i

            def at_least(self, eng, s, base, k, per):
                v = base + k
                if self.iters > 1 and per:
                    v = self.i * per + v
                eng.wait_ge(s, v)

            def chunk_at(self, k):
                return (self.chunk + k) % 4

            def bank(self, t):
                return (self.tile + t) % 4

        def waited(eng, pl):
            if pl.iters > 1:
                eng.sem_inc(sem("loop_waits"), 1)

        def split_hi(act, pl, k):
            n = pl.chunk + k
            if n >= N_CHUNKS:
                return
            pl.at_least(act, w_loaded[n % 4], 16 * (n // 4 + 1), 0, 4 * pl.nb)
            if n >= 4:
                pl.at_least(act, chunk_done, n - 3, 0, pl.nb)
            act.activation(WHI[:, n % 4, :], RAW[:, n % 4, :], ACT.Copy).then_inc(w_hi, 1)

        def split_lo(dve, pl, k):
            n = pl.chunk + k
            if n >= N_CHUNKS:
                return
            pl.at_least(dve, w_hi, n + 1, 0, pl.nb)
            dve.tensor_tensor(WLO[:, n % 4, :], RAW[:, n % 4, :], WHI[:, n % 4, :].bitcast(F32),
                              ALU.subtract).then_inc(w_lo, 1)

        def tile_used(ins, pl, t):
            ins.then_inc(bank_free[pl.bank(t)], 1)

        def load_chunk(sp, pl, k, desc):
            n = pl.chunk + k
            if n >= 4:
                pl.at_least(sp, w_lo, n - 3, 0, pl.nb)
            slot = RAW[:, n % 4, :]
            if desc in ("small1", "small2"):
                wi = (w_in if desc == "small1" else mix_w_in_2)[0].rearrange("(kt p) n -> p kt n", p=P)
                v = slot.rearrange("p (k c) -> p k c", c=P)
                parts = ([(C_I, 4, 0), (C_F, 4, 32), (C_NG, 24, 64)] if desc == "small1"
                         else [(X_B, 8, 0), (X_A, 8, 32)])
                first = desc == "small1"
                for q, (c, m, to) in enumerate(parts):
                    d = sp.dma_start(v[:, :, to:to + m], wi[:, :, c:c + m])
                    if q < len(parts) - 1:
                        d.then_inc(sem("part_loaded"), 16)
                        sp.wait_ge(sem("part_loaded"), 16 * (q + 1 + (0 if first else 4)))
                    else:
                        d.then_inc(w_loaded[n % 4], 16)
                return
            if desc in ("vsw0", "vsw1"):
                h = int(desc[-1])
                v = slot.rearrange("p (k c) -> p k c", c=256)
                sp.dma_start(v[:, :, 0:P], wchunk((w_in), 4 * h, 4, C_VS, P)).then_inc(sem("part_loaded"), 16)
                sp.wait_ge(sem("part_loaded"), 16 * (3 + h))
                sp.dma_start(v[:, :, P:256], wchunk(w_in, 4 * h, 4, C_VW, P)).then_inc(w_loaded[n % 4], 16)
                return
            w, kt0, kts, c, cols = desc
            src = wchunk(w, kt0, kts, c, cols) if isinstance(c, int) else wdyn(w, kt0, kts, c, cols)
            waited(sp, pl)
            sp.dma_start(slot[:, 0:kts * cols].rearrange("p (k c) -> p k c", c=cols), src)\
              .then_inc(w_loaded[n % 4], 16)

        def mm3(pe, out, whi, wlo, hhi, hlo, start, stop):
            pe.matmul(out, whi, hhi, start=start, stop=False)
            pe.matmul(out, whi, hlo, start=False, stop=False)
            return pe.matmul(out, wlo, hhi, start=False, stop=stop)

        def pe_open(pe, pl, t):
            m = pl.tile + t
            if m >= 4:
                pl.at_least(pe, bank_free[m % 4], m // 4, 0, pl.tb // 4)
            return PS[:, m % 4, :]

        def pe_tile(pe, pl, k, t, kts, rhi, rlo, k0=0, first=True, last=True, act_ready=None):
            n = pl.chunk + k
            bank = pe_open(pe, pl, t) if first else PS[:, (pl.tile + t) % 4, :]
            pl.at_least(pe, w_lo, n + 1, 0, pl.nb)
            for kk in range(kts):
                if act_ready is not None:
                    act_ready(kk)
                a = slice(kk * P, kk * P + P)
                mm = mm3(pe, bank, WHI[:, n % 4, a], WLO[:, n % 4, a], rhi[:, k0 + kk, :], rlo[:, k0 + kk, :],
                         first and kk == 0, last and kk == kts - 1)
            mm.then_inc(chunk_done, 1)

        def stage_loop(cnt, name, step, body):
            it = INFO[name]["iters"]
            if it == 1:
                start = cnt.n
                body(Place(name, 0))
                assert cnt.n - start == step, (name, cnt.n - start, step)
            else:
                cnt.loop(it, step, lambda i: body(Place(name, i)))

        def tiles_ready(eng, pl, k):
            pl.at_least(eng, chunk_done, pl.chunk + k + 1, 0, pl.nb)

        UNITS, u0 = {}, 0
        for name, per in (("oz1", 8), ("nz1", 4), ("merge1", 8), ("ffn1_in", 22), ("z2", 8), ("pool2", 4),
                          ("merge2", 8), ("ffn2_in", 22)):
            UNITS[name] = u0
            u0 += per
        GATES = {"oz1": 0, "nz1": 8, "z2": 12}
        nonlin, product = sem("gate_ready"), sem("product_ready")
        u_hi, u_lo = sem("result_hi_ready"), sem("result_lo_ready")
        ADA = {"conv1": [1] * 8, "v1": [2] * 8, "small1": [3], "nsa1": [2] * 8, "vsw1": [2, 3], "oz1": [1] * 8}
        ADA0 = {"v1": 0, "conv1": 16, "small1": 32, "nsa1": 35, "vsw1": 51, "oz1": 56}
        NORM_X = [8, 16, 24, 32, 40, 48]
        x_ready, h_ready = sem("residual_ready"), sem("h_ready")

        def at_least_unit(eng, s, pl, name, per, k):
            pl.at_least(eng, s, UNITS[name] + k + 1, 0, per)

        def b3(ap, n):
            return ap.unsqueeze(2).to_broadcast([ap.shape[0], ap.shape[1], n])

        def b3m(ap, n):
            return ap.unsqueeze(1).to_broadcast([ap.shape[0], n, ap.shape[1]])

        @block.sync
        def _(sp):
            sp.dma_start(CST[:], cst).then_inc(sem("const_loaded"), 16)
            xv = x[0].rearrange("(n p) d -> p n d", p=P)
            for n in range(NT):
                sp.dma_start(XTOK[:, n, :], xv[:, n, :]).then_inc(sem("x_loaded"), 16)
            rows = [(0, norm_g, 0), (0, conv_q_w, 8), (0, conv_k_w, 40), (0, conv_q_b, 72),
                    (0, conv_k_b, 80), (0, mh_norm_g, 88), (0, final_norm_g, 96),
                    (1, norm_g_2, 0), (1, conv_w_2, 24),
                    (2, ada_b_2, 0), (2, dn_norm_g_2, 72), (2, pool_scale_2, 73), (2, final_g_2, 77), (2, c_2, 85)]
            for tile, w, r in rows:
                nd = len(w.shape)
                flat = w if nd == 1 else w.rearrange("a b -> (a b)") if nd == 2 else w.rearrange("a b c -> (a b c)")
                n = flat.shape[0] // P
                sp.dma_start(PROW[r:r + n, tile, :], flat.rearrange("(r q) -> r q", q=P))\
                  .then_inc(sem("rows_loaded"), 16)
            for s, pos in enumerate((cmp_pos_k, cmp_pos_v)):
                for half in range(2):
                    sp.dma_start(PROW[32 * s:32 * s + 32, 3, 64 * half:64 * half + 64], pos[0])\
                      .then_inc(sem("rows_loaded"), 16)
            sp.wait_ge(sem("bias_zero"), 1)
            for w, r, m, c in ((b_igate, 0, 4, SMB), (b_fgate, 32, 4, SMB), (b_nsa_gate, 64, 24, SMB),
                               (a_log_2, 0, 8, ALOG), (dt_bias_2, 0, 8, DTB)):
                sp.dma_start(PAR[r:r + m, c:c + 1], w[0].rearrange("(p a) -> p a", a=1))\
                  .then_inc(sem("biases_loaded"), 16)
            for name, iters, body, _ in STAGES:
                if name == "merge1":
                    sp.wait_ge(u_lo, UNITS["nz1"])
                    sp.dma_start(POSI[:], positions.to_broadcast([P, T])).then_inc(sem("pos_loaded"), 16)
                    for s, w1 in enumerate((cmp_w1_k, cmp_w1_v)):
                        if s:
                            sp.wait_ge(sem("cmp_hid_sum"), 1)
                        for half in range(2):
                            sp.dma_start(W1[64 * half:64 * half + 64], w1[0].rearrange("(l d) h -> d l h", d=DK))\
                              .then_inc(sem("w1_loaded"), 16)
                        if s == 0:
                            sp.wait_ge(sem("roped"), 6)
                            for q, w2 in enumerate((cmp_w2_k, cmp_w2_v)):
                                for half in range(2):
                                    sp.dma_start(W2[:, q, 64 * half:64 * half + 64], w2[0])\
                                      .then_inc(sem("w2_loaded"), 16)
                if name == "merge2":
                    sp.wait_ge(sem("o_T_taken"), 8)
                    sp.dma_start(PLW[:], pool_w_2[0].rearrange("g c d -> c g d")).then_inc(sem("pool_w_loaded"), 16)
                if iters == 1:
                    for k, desc in enumerate(body(0)):
                        load_chunk(sp, Place(name, 0), k, desc)
                else:
                    with sp.Fori(0, iters) as i:
                        for k, desc in enumerate(body(i)):
                            load_chunk(sp, Place(name, i), k, desc)
            ov = out[0].rearrange("(n p) d -> p n d", p=P)
            for n in range(NT):
                sp.wait_ge(sem("out_tokens"), 2 * n + 2)
                sp.dma_start(ov[:, n, :], YTOK2[:, n, :]).then_inc(sem("stored"), 16)
            sp.wait_ge(sem("stored"), 16 * NT)

        @block.gpsimd
        def _(pool):
            pool.memset(PAR[:, SMB:SMB + 3], 0.0).then_inc(sem("bias_zero"), 1)
            pool.memset(PAR[:, HALF:HALF + 8], -0.5).then_inc(sem("half_set"), 1)

            def load_ada(g):
                for k in range(8):
                    static = isinstance(g, int)
                    if static and 8 * g + k < 2:
                        pass
                    elif static:
                        pool.wait_ge(sem("ada_used"), 8 * g + k - 1)
                    else:
                        pool.wait_ge(sem("ada_used"), g * 8 + (k + 7))
                    src = ada_w_2[0, k * P:(k + 1) * P, :]
                    src = src[:, g * D:(g + 1) * D] if static else src[:, ds(g * D + D, D)]
                    pool.dma_start(ADAW[:, k % 2, :], src).then_inc(sem(f"ada_loaded{k % 2}"), 16)

            load_ada(0)
            with pool.Fori(0, 6) as g:
                load_ada(g)
            pool.memset(VTOK[:, :, :, MD:MD + 1], 1.0).then_inc(sem("v_ones"), 1)
            pool.memset(ROW[3][0:8, :], 0.0).then_inc(sem("row_zero"), 1)
            pool.memset(SM[:], 0.0).then_inc(sem("row_zero"), 1)
            pool.wait_ge(sem("mht_ready"), 8)
            for g in (7, 8):
                load_ada(g)
            pool.wait_ge(sem("rope_tables"), 1)
            for t in range(6):
                src = QRAW[:, t, :] if t < 4 else KVR[:, t - 2, :]
                dst = QROPE[:, t, :] if t < 4 else KR[:, t - 4, :]
                pool.tensor_tensor(dst, src, RCOS[:], ALU.mult).then_inc(sem("rope_cos_part"), 1)
            pool.wait_ge(sem("roped"), 6)
            pool.memset(HID[:], 0.0).then_inc(sem("hid_zero"), 1)
            pool.memset(VCB[:], 0.0).then_inc(sem("hid_zero"), 1)
            pool.wait_ge(sem("conv_ready"), 16 + 24)
            pool.memset(SM[:], 0.0).then_inc(sem("row_zero"), 1)
            pool.memset(EROW[2][0:8, :], 1.0).then_inc(sem("row_zero"), 1)
            pool.wait_ge(sem("row_zero"), 4)
            pool.memset(EROW[2][0:8, :].rearrange("p (c t) -> p c t", t=P)[:, :, 0:1], 0.0).then_inc(sem("row_zero"), 1)
            for h in range(16):
                if h >= 2:
                    pool.wait_ge(sem("norm_sum"), h - 1)
                pool.tensor_tensor(NRM[:, h % 2, :], QKV[:, h, :], QKV[:, h, :], ALU.mult).then_inc(sem("qk_squares"), 1)
            for c in range(NT):
                for lv in range(1, LEVELS):
                    for a in range(2):
                        pool.wait_ge(sem("delta_a"), 2 * c + a + 1)
                        if lv > 1:
                            pool.wait_ge(sem("delta_x_sum"), ((c * 6 + lv - 2) * 2 + a) + 1)
                        elif c:
                            pool.wait_ge(sem("state_sum"), 2 * c)
                        pool.tensor_tensor(ML[:, 4 * a:4 * a + 4, :], MT[:, 4 * a:4 * a + 4, :],
                                           b3m(CST[:, K_LV + lv * P:K_LV + (lv + 1) * P], 4), ALU.mult)\
                            .then_inc(sem("level_block"), 1)
                pool.wait_ge(sem("o_var"), c + 1)
                pool.tensor_tensor(PAR[:, RSO:RSO + 8], PAR[:, RSO:RSO + 8], PAR[:, HALF:HALF + 8], ALU.pow)\
                    .then_inc(sem("o_rstd"), 1)

        @block.tensor
        def _(pe):
            pe.wait_ge(sem("const_loaded"), 16)
            pe.wait_ge(sem("rows_loaded"), 16 * 18)
            for tile, n, to in ((0, N1, 0), (1, N2, 128), (2, N3, 256), (3, 64, 384)):
                mm = pe.transpose(PS[:, 4, to:to + n], PROW[0:n, tile, :], ID[0:n, 0:n])
            mm.then_inc(sem("params_T"), 1)
            pe.wait_ge(sem("x_loaded"), 16 * NT)
            for k in range(KD):
                if k >= 3:
                    pe.wait_ge(x_ready, k - 2)
                for n in range(NT):
                    mm = pe.transpose(PS[:, 5 + k % 3, n * P:n * P + P], XTOK[:, n, k * P:k * P + P], ID)
                mm.then_inc(sem("x_T"), 1)

            def rms_sum(r):
                for k in range(KD):
                    pe.wait_ge(sem("squares_ready"), 8 * r + k + 1)
                    if r == 0 and k == 0:
                        pe.wait_ge(sem("params_ready"), 1)
                    pe.matmul(PS[:, 4, :], ONES, SQ[:, k % 2, :], start=(k == 0), stop=(k == KD - 1))\
                      .then_inc(sem("square_sum"), 1)

            def tile_stage(name, rhi, rlo, kts=8, ready=None, ada=True):
                def body(pl):
                    a = ADA0.get(name, 0)
                    for k in range(pl.nb):
                        pe_tile(pe, pl, k, k, kts, rhi, rlo)
                        if ada and name in ADA:
                            for _ in range(ADA[name][k]):
                                a += 1
                                if a % 8 == 0:
                                    mod_sum(pl, a)
                stage(name, body)

            def stage(name, body):
                if INFO[name]["iters"] == 1:
                    body(Place(name, 0))
                else:
                    with pe.Fori(0, INFO[name]["iters"]) as i:
                        body(Place(name, i))

            def mod_sum(pl, a):
                pl.at_least(pe, sem("ada_used"), a, 0, 8)
                for j in range(8):
                    mm = pe.matmul(PS[:, 7, j:j + 1], ADAC[:, j * P:j * P + P], ONES[:, 0:1], start=True, stop=True)
                mm.then_inc(sem("mod_sum"), 1)

            def token_stage(name, halves, kts, width):
                pl = Place(name, 0)
                a = ADA0[name]
                per = 8 // kts
                for h in range(halves):
                    for c in range(per):
                        k = per * h + c
                        n = pl.chunk + k
                        pe.wait_ge(w_lo, n + 1)
                        for t in range(NT):
                            bank = pe_open(pe, pl, NT * h + t) if c == 0 else PS[:, pl.bank(NT * h + t), :]
                            for kk in range(kts):
                                w = slice(kk * width, kk * width + width)
                                kt, tok = kts * c + kk, slice(t * P, t * P + P)
                                o = bank[:, 0:width]
                                pe.matmul(o, HHI[:, kt, tok], WHI[:, n % 4, w], start=(kt == 0), stop=False)
                                pe.matmul(o, HHI[:, kt, tok], WLO[:, n % 4, w], start=False, stop=False)
                                mm = pe.matmul(o, HLO[:, kt, tok], WHI[:, n % 4, w], start=False, stop=(kt == 7))
                        mm.then_inc(chunk_done, 1)
                        for _ in range(ADA[name][k]):
                            a += 1
                            if a % 8 == 0:
                                mod_sum(pl, a)

            def merge_stage(name, ka, ahi, alo, kb, bhi, blo):
                def body(pl):
                    for f in range(2):
                        for q, (kts, rh, rl) in enumerate(((8, HHI, HLO), (8, HHI, HLO), (ka, ahi, alo), (kb, bhi, blo))):
                            pe_tile(pe, pl, 4 * f + q, 4 * f + q, kts, rh, rl)
                stage(name, body)

            def ffn_out(name):
                def body(pl):
                    for f in range(4):
                        for c, (k0, kn) in enumerate(((0, 8), (8, 8), (16, 6))):
                            pe_tile(pe, pl, 3 * f + c, f, kn, HIDHI, HIDLO, k0, c == 0, c == 2)
                stage(name, body)

            rms_sum(0)
            pe.wait_ge(h_ready, 8)
            token_stage("v1", 2, 2, 512)
            tile_stage("conv1", HHI, HLO)
            tile_stage("small1", HHI, HLO)
            tile_stage("nsa1", HHI, HLO)
            token_stage("vsw1", 1, 4, 256)

            pe.wait_ge(sem("packed_gates"), 1)
            pe.wait_ge(sem("packed_um"), 1)
            for n in range(NT):
                mm = pe.transpose(PS[:, 4, n * P:n * P + P], SM[:, n * P:n * P + P], ID)
            mm.then_inc(sem("packed_T"), 1)
            pe.wait_ge(sem("conv_ready"), 16)
            for h in range(MH):
                if h == 0:
                    pe.wait_ge(sem("packed_cols"), 1)
                else:
                    pe.wait_ge(sem("pv_used"), 4 * h)
                pe.matmul(PS[:, 4, :], ID[0:4, h:h + 1].to_broadcast([4, P]), ROW[4][0:4, :], start=True, stop=True)\
                  .then_inc(sem("m_bcast"), 1)
                for j in range(NT):
                    if 4 * h + j >= 2:
                        pe.wait_ge(sem("p_ready"), 4 * h + j - 1)
                    for e in range(2):
                        mm = pe.matmul(PS[:, 5 + j % 2, 0:T - j * P], QK1[:, 8 + 2 * h + e, j * P:j * P + P],
                                       QK1[:, 2 * h + e, j * P:T], start=(e == 0), stop=(e == 1))
                    mm.then_inc(sem("s_ready"), 1)
                for i in range(NT):
                    if h == 0 and i == 0:
                        pe.wait_ge(sem("v_ones"), 1)
                        pe.wait_ge(sem("mod_taken"), 7)
                    if 4 * h + i >= 2:
                        pe.wait_ge(sem("pv_used"), 4 * h + i - 1)
                    for j in range(i + 1):
                        pe.wait_ge(sem("p_ready"), 4 * h + j + 1)
                        o = (0, 512, 896, 1152)[j] + (i - j) * P
                        mm = pe.matmul(PS[:, 7 if i % 2 == 0 else 4, 0:MD + 1], DP[:, h % 2, o:o + P],
                                       VTOK[:, j, h, :], start=(j == 0), stop=(j == i))
                    mm.then_inc(sem("pv_ready"), 1)
            for f in range(8):
                pe.wait_ge(sem("h_normed"), 4 * (f // 2) + 4)
                if f >= 4:
                    pe.wait_ge(sem("mht_ready"), f - 3)
                for n in range(NT):
                    mm = pe.transpose(PS[:, 4 + f % 4, n * P:n * P + P],
                                      MTOK[:, f // 2, n, (f % 2) * P:(f % 2) * P + P], ID)
                mm.then_inc(sem("h_T"), 1)
            pe.wait_ge(sem("mht_ready"), 8)
            tile_stage("oz1", HHI, HLO)

            pe.wait_ge(sem("mod_taken"), 9)
            for t in range(6):
                if t >= 4:
                    pe.wait_ge(sem("roped"), t - 3)
                pe.matmul(PS[:, 4 + t % 4, :], CST[:, K_ROPE:K_ROPE + P], QRAW[:, t, :] if t < 4 else KVR[:, t - 2, :],
                          start=True, stop=True).then_inc(sem("rope_perm"), 1)
            for s in range(2):
                pe.wait_ge(sem("roped"), 5 + s)
                pe.matmul(PS[:, 6 + s, :], CST[:, K_SWAP:K_SWAP + P], KR[:, s, :], start=True, stop=True)\
                  .then_inc(sem("k_swap_sum"), 1)
            for s in range(2):
                pe.wait_ge(sem("w1_loaded"), 32 * (s + 1))
                pe.wait_ge(sem("cmp_blocks"), s + 1)
                if s:
                    pe.wait_ge(sem("hid_ready"), 1)
                for g in range(2):
                    r = slice(64 * g, 64 * g + 64)
                    for lt in range(CB):
                        mm = pe.matmul(PS[:, 4 + g, 0:NC], W1[r, lt, :], BLK[r, lt, :],
                                       start=(lt == 0), stop=(lt == CB - 1))
                mm.then_inc(sem("cmp_hid_sum"), 1)
                pe.wait_ge(sem("hid_ready"), s + 1)
                pe.wait_ge(sem("w2_loaded"), 64)
                if s == 0:
                    pe.wait_ge(sem("k_swapped"), 2)
                    for g in range(2):
                        mm = pe.matmul(PS[:, 6, 32 * g:32 * g + 32], W2[:, 0, :], HID[:, 2 * g, :], start=True, stop=True)
                else:
                    mm = pe.matmul(PS[:, 7, 0:DK], HID[:].rearrange("p q n -> p (q n)"), W2[:, 1, 0:DK],
                                   start=True, stop=True)
                mm.then_inc(sem("cmp_kv_sum"), 1)
            pe.wait_ge(sem("cmp_kv_ready"), 5)
            for i in range(NT):
                if i >= 2:
                    pe.wait_ge(sem("cmp_scored"), 2 * (i - 1))
                for p in range(2):
                    for q in range(4):
                        r = slice(64 * p, 64 * p + 64)
                        mm = pe.matmul(PS[:, 4 + 2 * (i % 2) + p, 32 * q:32 * q + 32], QRAW[r, q, i * P:i * P + P],
                                       PAR[r, KCT + 32 * (q // 2):KCT + 32 * (q // 2) + 32], start=True, stop=True)
                mm.then_inc(sem("cmp_s_sum"), 1)
            pe.wait_ge(sem("cmp_probs"), 1)
            for i in range(NT):
                for p in range(2):
                    o = (2 * (i % 2) + p) * P
                    mm = pe.transpose(PS[:, 4 + i // 2, o:o + P], SC[:, i, p].rearrange("p q n -> p (q n)"), ID)
            mm.then_inc(sem("cmp_probs_T"), 1)
            for i in range(NT):
                pe.wait_ge(sem("cmp_pt_ready"), i // 2 + 1)
                if i >= 2:
                    pe.wait_ge(sem("y_cmp"), 2 * (i - 1))
                for p in range(2):
                    mm = pe.matmul(PS[:, 6 + i % 2, 256 * p:256 * p + 256], PCT[:, i, p, :],
                                   VCB[:].rearrange("p q d -> p (q d)"), start=True, stop=True)
                mm.then_inc(sem("cmp_o_sum"), 1)
            pe.wait_ge(sem("y_cmp"), 8)
            units = [(i, g, b, hh) for i in range(NT) for g in range(NG) for b in range(2) for hh in range(4)]

            def score(u):
                i, g, b, hh = units[u]
                par = hh % 2
                r = slice(64 * par, 64 * par + 64)
                if u >= 2:
                    pe.wait_ge(sem("exp_done"), u - 1)
                k = KR[r, b + (0 if par == g else 2), 0:(i + 1) * P]
                pe.matmul(PS[:, 4 + par, 0:(i + 1) * P], QROPE[r, 2 * g + hh // 2, i * P:i * P + P], k,
                          start=True, stop=True).then_inc(sem("nsa_s"), 1)

            def turn(u):
                i = units[u][0]
                pe.wait_ge(sem("exp_done"), u + 1)
                if u >= 1:
                    pe.wait_ge(sem("pt_ready"), u)
                for j in range(i + 1):
                    mm = pe.transpose(PS[:, 6, j * P:j * P + P], PR[:, u % 2, j * P:j * P + P], ID)
                mm.then_inc(sem("probs_T"), 1)

            def apply_v(u):
                i, g, b, hh = units[u]
                pe.wait_ge(sem("pt_ready"), u + 1)
                if hh == 0 and u >= 4:
                    pe.wait_ge(sem("y_added"), u // 4)
                o = 256 * (u // 4 % 2) + 64 * hh
                for j in range(i + 1):
                    mm = pe.matmul(PS[:, 7, o:o + DK], PT[:, u % 2, j * P:j * P + P], VSW[:, j, b, 64 * g:64 * g + 64],
                                   start=(j == 0), stop=(j == i))
                mm.then_inc(sem("nsa_o"), 1)

            for u in range(len(units) + 2):
                if u < len(units):
                    score(u)
                if 1 <= u <= len(units):
                    turn(u - 1)
                if u >= 2:
                    apply_v(u - 2)
            pe.wait_ge(sem("y_added"), 16)
            for f in range(4):
                for n in range(NT):
                    mm = pe.transpose(PS[:, 4 + f, n * P:n * P + P], YTOK[:, n, f].rearrange("p a d -> p (a d)"), ID)
                mm.then_inc(sem("y_T"), 1)
            tile_stage("nz1", HHI, HLO)
            pe.wait_ge(u_lo, UNITS["merge1"])
            merge_stage("merge1", 8, YAHI, YALO, 4, YBHI, YBLO)
            pe.wait_ge(u_lo, UNITS["ffn1_in"])
            tile_stage("out1", MGHI, MGLO)

            rms_sum(1)
            rms_sum(2)
            pe.wait_ge(h_ready, 16)
            tile_stage("ffn1_in", HHI, HLO)
            pe.wait_ge(u_lo, UNITS["z2"])
            ffn_out("ffn1_out")
            rms_sum(3)
            pe.wait_ge(h_ready, 24)
            tile_stage("conv2", HHI, HLO)
            tile_stage("small2", HHI, HLO)

            for h in range(16):
                pe.wait_ge(sem("qk_squares"), h + 1)
                if h >= 2:
                    pe.wait_ge(sem("norm_root"), h - 1)
                pe.matmul(PS[:, 5 + h % 2, :], ONES, NRM[:, h % 2, :], start=True, stop=True).then_inc(sem("norm_sum"), 1)
            pe.wait_ge(sem("packed2"), 2)
            for n in range(NT):
                mm = pe.transpose(PS[:, 7, n * P:n * P + P], SM[:, n * P:n * P + P], ID)
            mm.then_inc(sem("packed_T"), 1)
            pe.wait_ge(sem("qk_normed"), 16)
            pe.wait_ge(sem("delta_cols"), 1)

            def heads(a):
                return range(4 * a, 4 * a + 4)

            for c in range(NT):
                tok = slice(c * P, c * P + P)
                k2 = 2 * c
                for a in range(2):
                    B0, B1 = 4 + 2 * a, 5 + 2 * a
                    if c:
                        pe.wait_ge(sem("state_new"), k2 - 1 + a)
                    for h in heads(a):
                        mm = pe.matmul(PS[:, B0, (h % 4) * P:(h % 4) * P + P], ID[0:8, h:h + 1].to_broadcast([8, P]),
                                       EROW[0][0:8, tok], start=True, stop=True)
                    mm.then_inc(sem("gc_bcast"), 1)
                    if c:
                        pe.wait_ge(sem("o_T_taken"), k2 - 1 + a)
                    for h in heads(a):
                        mm = pe.matmul(PS[:, B1, (h % 4) * P:(h % 4) * P + P], QKV[:, 8 + h, tok], QKV[:, 8 + h, tok],
                                       start=True, stop=True)
                    mm.then_inc(sem("kk_sum"), 1)
                for a in range(2):
                    B0, B1 = 4 + 2 * a, 5 + 2 * a
                    pe.wait_ge(sem("decay_arg"), k2 + a + 1)
                    for h in heads(a):
                        mm = pe.matmul(PS[:, B0, (h % 4) * P:(h % 4) * P + P], ID[0:8, h:h + 1].to_broadcast([8, P]),
                                       EROW[1][0:8, tok], start=True, stop=True)
                    mm.then_inc(sem("beta_bcast"), 1)
                    pe.wait_ge(sem("kk_decayed"), k2 + a + 1)
                    for h in heads(a):
                        mm = pe.matmul(PS[:, B1, (h % 4) * P:(h % 4) * P + P], QKV[:, 8 + h, tok], QKV[:, h, tok],
                                       start=True, stop=True)
                    mm.then_inc(sem("qk_sum"), 1)
                for lv in range(LEVELS):
                    for a in range(2):
                        B0, B1 = 4 + 2 * a, 5 + 2 * a
                        n = (c * 6 + lv - 1) * 2 + a
                        m = (c * 6 + lv) * 2 + a
                        if lv == 0:
                            pe.wait_ge(sem("qk_decayed"), k2 + a + 1)
                        else:
                            pe.wait_ge(sem("level_block"), n + 1)
                            pe.wait_ge(sem("inv_ready"), m - 2 + 1)
                            for h in heads(a):
                                mm = pe.matmul(PS[:, B0, (h % 4) * P:(h % 4) * P + P], ML[:, h, :], TI[:, h, :],
                                               start=True, stop=True)
                            mm.then_inc(sem("delta_x_sum"), 1)
                    for a in range(2):
                        B0, B1 = 4 + 2 * a, 5 + 2 * a
                        n = (c * 6 + lv - 1) * 2 + a
                        if lv:
                            pe.wait_ge(sem("delta_x"), n + 1)
                            for h in heads(a):
                                mm = pe.matmul(PS[:, B1, (h % 4) * P:(h % 4) * P + P], XX[:, h, :], TT[:, h, :],
                                               start=True, stop=True)
                            mm.then_inc(sem("inv_step"), 1)
                    for a in range(2):
                        B0 = 4 + 2 * a
                        if lv < LEVELS - 1:
                            pe.wait_ge(sem("inv_T_ready"), (c * LEVELS + lv) * 2 + a + 1)
                            for h in heads(a):
                                mm = pe.transpose(PS[:, B0, (h % 4) * P:(h % 4) * P + P], TT[:, h, :], ID)
                            mm.then_inc(sem("inv_back"), 1)
                for a in range(2):
                    B0, B1 = 4 + 2 * a, 5 + 2 * a
                    for h in heads(a):
                        mm = pe.transpose(PS[:, B0, (h % 4) * P:(h % 4) * P + P], QKV[:, 16 + h, tok], ID)
                    mm.then_inc(sem("v_T"), 1)
                    pe.wait_ge(sem("inv_T_ready"), (c * LEVELS + LEVELS - 1) * 2 + a + 1)
                    if c:
                        for h in heads(a):
                            mm = pe.matmul(PS[:, B1, (h % 4) * P:(h % 4) * P + P], QKV[:, 8 + h, tok], SS[:, h, :],
                                           start=True, stop=True)
                        mm.then_inc(sem("ks_sum"), 1)
                for a in range(2):
                    B0, B1 = 4 + 2 * a, 5 + 2 * a
                    pe.wait_ge(sem("rhs_ready"), k2 + a + 1)
                    for h in heads(a):
                        mm = pe.matmul(PS[:, B0, (h % 4) * P:(h % 4) * P + P], TT[:, h, :], RV[:, h, :],
                                       start=True, stop=True)
                    mm.then_inc(sem("v_new_sum"), 1)
                    for h in heads(a):
                        mm = pe.transpose(PS[:, B1, (h % 4) * P:(h % 4) * P + P], QKV[:, 8 + h, tok], ID)
                    mm.then_inc(sem("k_T"), 1)
                for a in range(2):
                    B0, B1 = 4 + 2 * a, 5 + 2 * a
                    pe.wait_ge(sem("v_new"), k2 + a + 1)
                    pe.wait_ge(sem("k_dec"), k2 + a + 1)
                    if c:
                        for h in heads(a):
                            mm = pe.matmul(PS[:, B0, (h % 4) * P:(h % 4) * P + P], QKV[:, h, tok], SS[:, h, :],
                                           start=True, stop=True)
                        mm.then_inc(sem("qs_sum"), 1)
                    for h in heads(a):
                        mm = pe.matmul(PS[:, B1, (h % 4) * P:(h % 4) * P + P], QKM[:, h, :], VN[:, h, :],
                                       start=True, stop=True)
                    mm.then_inc(sem("intra_sum"), 1)
                for a in range(2):
                    B0, B1 = 4 + 2 * a, 5 + 2 * a
                    if c:
                        pe.wait_ge(sem("o_inter"), k2 - 2 + a + 1)
                    for h in heads(a):
                        mm = pe.matmul(PS[:, B0, (h % 4) * P:(h % 4) * P + P], KDT[:, h, :], VN[:, h, :],
                                       start=True, stop=True)
                    mm.then_inc(sem("state_sum"), 1)
                for a in range(2):
                    B1 = 5 + 2 * a
                    pe.wait_ge(sem("o_normed"), c + 1)
                    for h in heads(a):
                        mm = pe.transpose(PS[:, B1, (h % 4) * P:(h % 4) * P + P], OO[:, h, :], ID)
                    mm.then_inc(sem("o_T"), 1)
            tile_stage("z2", HHI, HLO)
            pl = Place("pool2", 0)
            for k in range(4 + 2):
                if k < 4:
                    pe_tile(pe, pl, k, k, 8, HHI, HLO)
                if k >= 2:
                    g = k - 2
                    pe.wait_ge(product, UNITS["pool2"] + g + 1)
                    if g == 0:
                        pe.wait_ge(sem("pool_w_loaded"), 16)
                        pe.wait_ge(sem("o_T_taken"), 8)
                    pe.matmul(PS[:, 4 + g, :], PLW[:, g, :], PLS[:, 2, :], start=True, stop=True)\
                      .then_inc(sem("pool_sum"), 1)
            pe.wait_ge(u_lo, UNITS["merge2"])
            merge_stage("merge2", 4, PLHI, PLLO, 8, Y2HI, Y2LO)
            pe.wait_ge(u_lo, UNITS["ffn2_in"])
            tile_stage("out2", M2HI, M2LO)
            rms_sum(4)
            pe.wait_ge(h_ready, 32)
            tile_stage("ffn2_in", HHI, HLO)
            pe.wait_ge(u_lo, UNITS["ffn2_in"] + 22)
            ffn_out("ffn2_out")
            rms_sum(5)
            for n in range(NT):
                for q in range(2):
                    m = 2 * n + q
                    pe.wait_ge(sem("final_x"), 8)
                    if m >= 3:
                        pe.wait_ge(sem("out_tokens"), m - 2)
                    for k in range(4):
                        mm = pe.transpose(PS[:, 5 + m % 3, k * P:k * P + P], XT[:, 4 * q + k, n * P:n * P + P], ID)
                    mm.then_inc(sem("out_T"), 1)

        @block.scalar
        def _(act):
            cnt = Count(act, sem("act_step"))

            def copy(out_, in_, **kw):
                return act.activation(out_, in_, ACT.Copy, **kw)

            def stage(name, body):
                if INFO[name]["iters"] == 1:
                    body(Place(name, 0))
                else:
                    with act.Fori(0, INFO[name]["iters"]) as i:
                        body(Place(name, i))

            act.wait_ge(sem("params_T"), 1)
            act.wait_ge(sem("bias_zero"), 1)
            cnt.mark(copy(PAR[:, 0:N1], PS[:, 4, 0:N1]))
            cnt.mark(copy(PAR[:, G2:G2 + N2], PS[:, 4, 128:128 + N2]))
            cnt.mark(copy(PAR[:, ADAB:ADAB + N3], PS[:, 4, 256:256 + N3]))
            copy(PAR[:, POST:POST + 64], PS[:, 4, 384:448]).then_inc(sem("params_ready"), 1)
            cnt.wait()
            act.activation(PAR[:, SILC:SILC + 8], PAR[:, CVEC:CVEC + 8], ACT.Silu).then_inc(sem("silu_c"), 1)

            def squares(r):
                for k in range(KD):
                    act.wait_ge(x_ready, NORM_X[r] - 8 + k + 1)
                    if 8 * r + k >= 2:
                        act.wait_ge(sem("square_sum"), 8 * r + k - 1)
                    act.activation(SQ[:, k % 2, :], XT[:, k, :], ACT.Square).then_inc(sem("squares_ready"), 1)
                act.wait_ge(sem("mean_recip"), r + 1)
                act.activation(RMS[:], RMS[:], ACT.Sqrt).then_inc(sem("rms_ready"), 1)

            def norm_hi(r, idx, shift):
                for k in range(KD):
                    act.wait_ge(sem("normed"), 8 * idx + k + 1)
                    kw = {} if shift is None else dict(bias=col(shift + k))
                    act.activation(HHI[:, k, :], SQ[:, k % 2, :], ACT.Identity, **kw).then_inc(sem("h_hi"), 1)

            def conv_stage(name, tile0):
                def body(pl):
                    for k in range(pl.nb):
                        split_hi(act, pl, k + AHEAD)
                        tiles_ready(act, pl, k)
                        dst = QK1 if name == "conv1" else QKV
                        d = dst[:, ds(pl.i * 8 + k, 1), :]
                        src = PS[:, pl.bank(k):pl.bank(k) + 1, :]
                        if name == "conv1":
                            kw = dict(scale=PAR[:, ds(pl.i * 32 + (8 + 24 + k), 1)], bias=PAR[:, ds(pl.i * 8 + (CQB + k), 1)])
                        else:
                            kw = dict(scale=PAR[:, ds(pl.i * 8 + (CW2 + 72 + k), 1)])
                        waited(act, pl)
                        act.activation(d, src, ACT.Identity, **kw).then_inc(sem("conv_base"), 1)
                        pl.at_least(act, sem("conv_taps"), tile0 + k + 1, 0, 8)
                        waited(act, pl)
                        act.activation(d, d, ACT.Silu).then_inc(sem("conv_ready"), 1)
                stage(name, body)

            def unit_hi(pl, name, per, k, dst, src):
                at_least_unit(act, product, pl, name, per, k)
                waited(act, pl)
                act.activation(dst, src, ACT.Copy).then_inc(u_hi, 1)

            squares(0)
            norm_hi(0, 0, None)
            for n in range(AHEAD):
                act.wait_ge(w_loaded[n], 16)
                act.activation(WHI[:, n, :], RAW[:, n, :], ACT.Copy).then_inc(w_hi, 1)
            pl = Place("v1", 0)
            for k in range(8):
                split_hi(act, pl, k + AHEAD)
                if k % 4 == 3:
                    h = k // 4
                    tiles_ready(act, pl, k)
                    for t in range(NT):
                        src = PS[:, pl.bank(t), :].rearrange("p (h d) -> p h d", d=MD)
                        tile_used(copy(VTOK[:, t, 2 * h:2 * h + 2, 0:MD], src), pl, t)
            conv_stage("conv1", 0)
            pl = Place("small1", 0)
            split_hi(act, pl, AHEAD)
            tiles_ready(act, pl, 0)
            act.wait_ge(sem("biases_loaded"), 16 * 5)
            tile_used(act.activation(SMR[:], PS[:, pl.bank(0), :], ACT.Identity, bias=col(SMB)), pl, 0)
            pl = Place("nsa1", 0)
            for k in range(8):
                split_hi(act, pl, k + AHEAD)
                tiles_ready(act, pl, k)
                tile_used(copy(QRAW[:, k, :] if k < 4 else KVR[:, k - 4, :], PS[:, pl.bank(k), :]), pl, k)
            pl = Place("vsw1", 0)
            for k in range(2):
                split_hi(act, pl, k + AHEAD)
            tiles_ready(act, pl, 1)
            for t in range(NT):
                tile_used(copy(VSW[:, t].rearrange("p a d -> p (a d)"), PS[:, pl.bank(t), 0:256]), pl, t)

            act.wait_ge(bank_free[INFO["small1"]["tile"] % 4], INFO["small1"]["tile"] // 4 + 1)
            cnt.mark(copy(ROW[0][0:4, :], SMR[32:36, :]))
            act.wait_ge(sem("row_zero"), 2)
            act.activation(SM[64:88, :], SMR[64:88, :], ACT.Sigmoid).then_inc(sem("packed_gates"), 1)
            cnt.wait()
            cnt.mark(act.activation(ROW[1][0:4, :], ROW[0][0:4, :], ACT.Abs))
            cnt.wait()
            cnt.mark(act.activation(ROW[1][0:4, :], ROW[1][0:4, :], ACT.Exp, scale=-1.0))
            cnt.wait()
            act.activation(ROW[1][0:4, :], ROW[1][0:4, :], ACT.Ln, bias=1.0).then_inc(sem("log_f_parts"), 1)
            act.wait_ge(sem("packed_T"), 1)
            copy(SMT[:].rearrange("p n c -> p (n c)"), PS[:, 4, :]).then_inc(sem("packed_cols"), 1)
            act.wait_ge(sem("neg_m"), 1)
            act.activation(col(NE, 16), col(NE, 16), ACT.Exp, scale=-1.0).then_inc(sem("exp_neg_m"), 1)
            for h in range(MH):
                act.wait_ge(sem("m_bcast"), h + 1)
                if h:
                    act.wait_ge(sem("m_masked"), h)
                copy(ROW[0][:], PS[:, 4, :]).then_inc(sem("m_copied"), 1)
                act.wait_ge(sem("m_masked"), h + 1)
                for j in range(NT):
                    o = (0, 512, 896, 1152)[j]
                    if h >= 2 and j == 0:
                        act.wait_ge(sem("pv_ready"), 4 * (h - 1))
                    bias = SMT[:, j, h:h + 1]
                    e = act.activation(DP[:, h % 2, o:o + P], ROW[1][:, j * P:j * P + P], ACT.Exp, bias=bias, scale=-1.0)
                    if j < NT - 1:
                        e = act.activation(DP[:, h % 2, o + P:o + T - j * P], ROW[0][:, (j + 1) * P:T], ACT.Exp,
                                           bias=bias, scale=-1.0)
                    e.then_inc(sem("decay_ready"), 1)
            act.wait_ge(sem("ln_recip"), 1)
            act.activation(col(RST, 16), col(RST, 16), ACT.Sqrt).then_inc(sem("ln_rstd"), 1)
            for f in range(8):
                act.wait_ge(sem("h_T"), f + 1)
                copy(MHT[:, f, :], PS[:, 4 + f % 4, :], scale=col(MHG + f)).then_inc(sem("mht_ready"), 1)

            def oz(pl):
                for f in range(4):
                    for q in range(2):
                        k = 2 * f + q
                        split_hi(act, pl, k + AHEAD)
                        tiles_ready(act, pl, k)
                        a = act.activation(ROW[2 * (f % 2) + q][:], PS[:, pl.bank(k), :], ACT.Sigmoid)
                        if q == 0:
                            tile_used(a, pl, k)
                        else:
                            a.then_inc(nonlin, 1)
                    unit_hi(pl, "oz1", 4, f, YAHI[:, ds(pl.i * 4 + f, 1), :], ROW[2 * (f % 2)][:].unsqueeze(1))
            stage("oz1", oz)

            act.wait_ge(sem("angles"), 1)
            act.activation(RSIN[:], ANG[:], ACT.Sin)
            act.activation(RTMP[:], ANG[:], ACT.Sin, scale=0.5).then_inc(sem("sines"), 1)
            for s in range(2):
                act.wait_ge(sem("k_swap_sum"), s + 1)
                copy(KR[:, 2 + s, :], PS[:, 6 + s, :]).then_inc(sem("k_swapped"), 1)
            act.wait_ge(sem("hid_zero"), 2)
            for s in range(2):
                act.wait_ge(sem("cmp_hid_sum"), s + 1)
                if s:
                    act.wait_ge(sem("cmp_kv_sum"), 1)
                for q in range(4):
                    e = act.activation(HID[:, q, 0:NC], PS[:, 4 + q // 2, 0:NC], ACT.Gelu_apprx_tanh)
                e.then_inc(sem("hid_ready"), 1)
                act.wait_ge(sem("cmp_kv_sum"), s + 1)
                if s == 0:
                    copy(col(KCT, 64), PS[:, 6, 0:64]).then_inc(sem("cmp_kv_ready"), 1)
                else:
                    for q in range(4):
                        r = slice(32 * q, 32 * q + 32)
                        copy(VCB[r, q, :], PS[r, 7, 0:DK]).then_inc(sem("cmp_kv_ready"), 1)
            act.wait_ge(sem("cmp_shifted"), 1)
            act.activation(SC[:], SC[:], ACT.Exp).then_inc(sem("cmp_exp"), 1)
            act.wait_ge(sem("cmp_probs_T"), 1)
            for i in range(2):
                copy(PCT[:, 2 * i:2 * i + 2].rearrange("p a b n -> p (a b n)"), PS[:, 4 + i, :]).then_inc(sem("cmp_pt_ready"), 1)
            act.wait_ge(sem("y_cmp"), 8)
            units = [(i, g, b, hh) for i in range(NT) for g in range(NG) for b in range(2) for hh in range(4)]

            def turned(u):
                act.wait_ge(sem("probs_T"), u + 1)
                if u >= 2:
                    act.wait_ge(sem("nsa_o"), u - 1)
                n = (units[u][0] + 1) * P
                copy(PT[:, u % 2, 0:n], PS[:, 6, 0:n]).then_inc(sem("pt_ready"), 1)

            for u, (i, g, b, hh) in enumerate(units):
                act.wait_ge(sem("max_ready"), u + 1)
                if u >= 2:
                    act.wait_ge(sem("probs_T"), u - 1)
                n = (i + 1) * P
                if hh == 0 and u >= 8:
                    act.wait_ge(sem("y_added"), u // 4 - 1)
                act.activation(PR[:, u % 2, 0:n], PS[:, 4 + hh % 2, 0:n], ACT.Exp, bias=col(MX + 4 + u % 4),
                               accum_out=col(SUM + 4 * (u // 4 % 2) + hh)).then_inc(sem("exp_done"), 1)
                if u >= 1:
                    turned(u - 1)
            turned(len(units) - 1)
            for f in range(4):
                act.wait_ge(sem("y_T"), f + 1)
                copy(YT[:, f, :], PS[:, 4 + f, :]).then_inc(sem("yt_ready"), 1)
            pl = Place("nz1", 0)
            for f in range(4):
                split_hi(act, pl, f + AHEAD)
                tiles_ready(act, pl, f)
                if f >= 2:
                    act.wait_ge(u_lo, UNITS["nz1"] + f - 1)
                act.activation(NZS[:, f % 2, :], PS[:, pl.bank(f), :], ACT.Sigmoid).then_inc(nonlin, 1)
                unit_hi(pl, "nz1", 4, f, YBHI[:, f, :], NZS[:, f % 2, :])

            def merge(name, gates, hi):
                def body(pl):
                    for f in range(2):
                        for q in range(2):
                            k = 4 * f + q
                            split_hi(act, pl, k + AHEAD)
                            tiles_ready(act, pl, k)
                            a = act.activation(gates[:, 2 * f + q, :], PS[:, pl.bank(k), :], ACT.Sigmoid)
                            tile_used(a, pl, k)
                        for q in range(2, 4):
                            split_hi(act, pl, 4 * f + q + AHEAD)
                        unit_hi(pl, name, 2, f, hi[:, ds(pl.i * 2 + f, 1), :], gates[:, 2 * f:2 * f + 1, :])
                stage(name, body)

            def splits_only(name):
                def body(pl):
                    for k in range(pl.nb):
                        split_hi(act, pl, k + AHEAD)
                stage(name, body)

            def ffn_in(name):
                def body(pl):
                    for f in range(2):
                        split_hi(act, pl, 2 * f + AHEAD)
                        tiles_ready(act, pl, 2 * f)
                        act.activation(FS[:, f, :], PS[:, pl.bank(2 * f), :], ACT.Silu)\
                           .then_inc(bank_free[pl.bank(2 * f)], 1)
                        split_hi(act, pl, 2 * f + 1 + AHEAD)
                        unit_hi(pl, name, 2, f, HIDHI[:, ds(pl.i * 2 + f, 1), :], FS[:, f:f + 1, :])
                stage(name, body)

            merge("merge1", GT, MGHI)
            splits_only("out1")

            squares(1)
            squares(2)
            norm_hi(2, 1, MOD)
            ffn_in("ffn1_in")
            splits_only("ffn1_out")
            squares(3)
            norm_hi(3, 2, MOD + 24)
            conv_stage("conv2", 16)
            pl = Place("small2", 0)
            split_hi(act, pl, AHEAD)
            tiles_ready(act, pl, 0)
            act.activation(EROW[1][0:8, :], PS[0:8, pl.bank(0), :], ACT.Sigmoid).then_inc(sem("beta_rows"), 1)
            act.activation(EROW[0][0:8, :], PS[32:40, pl.bank(0), :], ACT.Identity, bias=PAR[0:8, DTB:DTB + 1])\
               .then_inc(bank_free[pl.bank(0)], 1)
            act.wait_ge(bank_free[pl.bank(0)], INFO["small2"]["tile"] // 4 + 1)
            cnt.mark(act.activation(LPR[0:8, 0, :], EROW[0][0:8, :], ACT.Abs))
            cnt.wait()
            cnt.mark(act.activation(LPR[0:8, 0, :], LPR[0:8, 0, :], ACT.Exp, scale=-1.0))
            cnt.mark(act.activation(PAR[0:8, ALOG:ALOG + 1], PAR[0:8, ALOG:ALOG + 1], ACT.Exp))
            cnt.wait()
            cnt.mark(act.activation(LPR[0:8, 2, :], LPR[0:8, 0, :], ACT.Identity, bias=1.0))
            cnt.wait()
            act.activation(LPR[0:8, 1, :], LPR[0:8, 2, :], ACT.Ln).then_inc(sem("softplus_parts"), 1)
            for h in range(16):
                act.wait_ge(sem("norm_sum"), h + 1)
                if h >= 2:
                    act.wait_ge(sem("qk_normed"), h - 1)
                act.activation(NRT[:, h % 2, :], PS[:, 5 + h % 2, :], ACT.Sqrt, bias=EPS).then_inc(sem("norm_root"), 1)
            act.wait_ge(sem("packed_T"), 2)
            cnt.mark(copy(SMT[:].rearrange("p n c -> p (n c)"), PS[:, 7, :]))
            cnt.wait()
            act.activation(col(EG, 32).rearrange("p (c h) -> p c h", h=8), SMT[:, :, 32:40], ACT.Exp)
            cnt.mark(act.activation(col(EKD, 32).rearrange("p (c h) -> p c h", h=8), SMT[:, :, 64:72], ACT.Exp))
            cnt.wait()
            act.activation(col(QEG, 32), col(EG, 32), ACT.Copy, scale=float(128 ** -0.5)).then_inc(sem("delta_cols"), 1)

            def ps4(b):
                return PS[:, b, :].rearrange("p (h n) -> p h n", n=P)

            for c in range(NT):
                k2 = 2 * c
                for a in range(2):
                    h4 = slice(4 * a, 4 * a + 4)
                    act.wait_ge(sem("gc_bcast"), k2 + a + 1)
                    if c:
                        act.wait_ge(sem("state_new"), k2 - 1 + a)
                    act.activation(PAR[:, EGL + 4 * a:EGL + 4 * a + 4].unsqueeze(2), ps4(4 + 2 * a)[:, :, P - 1:P], ACT.Exp)\
                       .then_inc(sem("end_decay"), 1)
                    act.wait_ge(sem("decay_masked"), k2 + a + 1)
                    act.activation(DD[:, h4, :], DD[:, h4, :], ACT.Exp).then_inc(sem("decay_exp"), 1)
                for lv in range(LEVELS):
                    for a in range(2):
                        n = (c * 6 + lv - 1) * 2 + a
                        h4 = slice(4 * a, 4 * a + 4)
                        if lv:
                            act.wait_ge(sem("delta_x_sum"), n + 1)
                            copy(XX[:, h4, :], ps4(4 + 2 * a)).then_inc(sem("delta_x"), 1)
                    for a in range(2):
                        h4 = slice(4 * a, 4 * a + 4)
                        if lv < LEVELS - 1:
                            act.wait_ge(sem("inv_back"), (c * 6 + lv) * 2 + a + 1)
                            copy(TI[:, h4, :], ps4(4 + 2 * a)).then_inc(sem("inv_ready"), 1)
                for a in range(2):
                    h4 = slice(4 * a, 4 * a + 4)
                    act.wait_ge(sem("v_T"), k2 + a + 1)
                    copy(RV[:, h4, :], ps4(4 + 2 * a)).then_inc(sem("v_tokens"), 1)
                for a in range(2):
                    h4 = slice(4 * a, 4 * a + 4)
                    act.wait_ge(sem("v_new_sum"), k2 + a + 1)
                    copy(VN[:, h4, :], ps4(4 + 2 * a)).then_inc(sem("v_new"), 1)
                for a in range(2):
                    act.wait_ge(sem("o_T"), k2 + a + 1)
                    act.activation(QKV[:, 16 + 4 * a:20 + 4 * a, c * P:c * P + P], ps4(5 + 2 * a), ACT.Copy,
                                   scale=col(DNG)).then_inc(sem("o_T_taken"), 1)

            def z2(pl):
                for f in range(4):
                    split_hi(act, pl, f + AHEAD)
                    tiles_ready(act, pl, f)
                    act.activation(TMP2[:, f, :], PS[:, pl.bank(f), :], ACT.Sigmoid).then_inc(nonlin, 1)
                    unit_hi(pl, "z2", 4, f, Y2HI[:, ds(pl.i * 4 + f, 1), :], TMP2[:, f:f + 1, :])
            stage("z2", z2)
            pl = Place("pool2", 0)
            for g in range(4):
                split_hi(act, pl, g + AHEAD)
                act.wait_ge(sem("pool_sum"), g + 1)
                if g:
                    act.wait_ge(u_lo, UNITS["pool2"] + g)
                cnt.mark(copy(PLT[:], PS[:, 4 + g, :], scale=col(PSC + g)))
                cnt.wait()
                copy(PLHI[:, g, :], PLT[:]).then_inc(u_hi, 1)
            merge("merge2", GT2, M2HI)
            splits_only("out2")
            squares(4)
            norm_hi(4, 3, MOD + 48)
            ffn_in("ffn2_in")
            for i in range(INFO["ffn2_out"]["iters"]):
                pl = Place("ffn2_out", 0)
                pl.chunk += pl.nb * i
                pl.iters = 1
                for k in range(pl.nb):
                    split_hi(act, pl, k + AHEAD)
            squares(5)
            for m in range(2 * NT):
                act.wait_ge(sem("out_T"), m + 1)
                copy(YTOK2[:, m // 2, (m % 2) * T:(m % 2) * T + T], PS[:, 5 + m % 3, :]).then_inc(sem("out_tokens"), 1)

        @block.vector
        def _(dve):
            cnt = Count(dve, sem("dve_step"))

            def chained(ins):
                cnt.mark(ins)
                cnt.wait()

            def tt(o, a, b, op):
                return dve.tensor_tensor(o, a, b, op)

            def stt(o, a, s, b, op0, op1):
                return dve.scalar_tensor_tensor(o, a, s, b, op0, op1)

            def ts(o, a, s1, s2, op0, op1=None):
                return dve.tensor_scalar(o, a, s1, s2, op0) if op1 is None else dve.tensor_scalar(o, a, s1, s2, op0, op1)

            def stage(name, step, body):
                stage_loop(cnt, name, step, body)

            for k in range(KD):
                dve.wait_ge(sem("x_T"), k + 1)
                dve.tensor_copy(XT[:, k, :], PS[:, 5 + k % 3, :]).then_inc(x_ready, 1)

            def rms(r, coef, dst=None, shift=None, idx=0):
                dve.wait_ge(sem("square_sum"), 8 * r + 8)
                chained(ts(RMS[:], PS[:, 4, :], 1.0 / D, EPS, ALU.mult, ALU.add))
                dve.reciprocal(RMS[:], RMS[:]).then_inc(sem("mean_recip"), 1)
                dve.wait_ge(sem("rms_ready"), r + 1)
                for k in range(KD):
                    if dst is not None:
                        stt(dst[:, k, :], XT[:, k, :], col(coef + k), RMS[:], ALU.mult, ALU.mult)\
                            .then_inc(sem("final_x") if r == 5 else x_ready, 1)
                        continue
                    stt(SQ[:, k % 2, :], XT[:, k, :], col(coef + k), RMS[:], ALU.mult, ALU.mult)\
                        .then_inc(sem("normed"), 1)
                    dve.wait_ge(sem("h_hi"), 8 * idx + k + 1)
                    hi = HHI[:, k, :].bitcast(F32)
                    if shift is None:
                        tt(HLO[:, k, :], SQ[:, k % 2, :], hi, ALU.subtract).then_inc(h_ready, 1)
                    else:
                        stt(HLO[:, k, :], SQ[:, k % 2, :], col(shift + k), hi, ALU.add, ALU.subtract)\
                            .then_inc(h_ready, 1)

            def ada(pl, name, k, a0):
                a = a0
                for _ in range(ADA[name][k]):
                    pl.at_least(dve, sem(f"ada_loaded{a % 2}"), 16 * (a // 2 + 1), 0, 64)
                    kt = a % 8
                    if kt == 0:
                        dve.wait_ge(sem("silu_c"), 1)
                        ins = ts(ADAC[:], ADAW[:, a % 2, :], col(SILC), None, ALU.mult)
                    else:
                        pl.at_least(dve, sem("ada_used"), a, 0, 8)
                        ins = stt(ADAC[:], ADAW[:, a % 2, :], col(SILC + kt), ADAC[:], ALU.mult, ALU.add)
                    ins.then_inc(sem("ada_used"), 1)
                    a += 1
                    if a % 8 == 0:
                        g = a // 8 - 1
                        pl.at_least(dve, sem("mod_sum"), g + 1, 0, 1)
                        if pl.iters == 1:
                            o, b = PAR[:, MOD + 8 * g:MOD + 8 * g + 8], PAR[:, ADAB + 8 * g:ADAB + 8 * g + 8]
                        else:
                            o, b = PAR[:, ds(pl.i * 8 + (MOD + 8 * g), 8)], PAR[:, ds(pl.i * 8 + (ADAB + 8 * g), 8)]
                        tt(o, PS[:, 7, 0:8], b, ALU.add).then_inc(sem("mod_taken"), 1)
                return a

            def conv_stage(name, tile0):
                def body(pl):
                    a = ADA0["conv1"]
                    for k in range(pl.nb):
                        split_lo(dve, pl, k + AHEAD)
                        if name == "conv1" and k < pl.nb - 1:
                            a = ada(pl, name, k, a)
                        pl.at_least(dve, sem("conv_base"), tile0 + k + 1, 0, 8)
                        dst = QK1 if name == "conv1" else QKV
                        for s in range(1, 4):
                            w = (PAR[:, ds(pl.i * 32 + (8 + 8 * (3 - s) + k), 1)] if name == "conv1"
                                 else PAR[:, ds(pl.i * 8 + (CW2 + 24 * (3 - s) + k), 1)])
                            o = dst[:, ds(pl.i * 8 + k, 1), s:T]
                            ins = stt(o, PS[:, pl.bank(k):pl.bank(k) + 1, 0:T - s], w, o, ALU.mult, ALU.add)
                            if s < 3:
                                chained(ins)
                        cnt.mark(ins)
                        cnt.wait()
                        dve.sem_inc(sem("conv_taps"), 1)
                        dve.sem_inc(bank_free[pl.bank(k)], 1)
                        if name == "conv1" and k == pl.nb - 1:
                            a = ada(pl, name, k, a)
                stage(name, 8 * 3, body)

            def unit_lo(pl, name, per, k, dst, src, hi):
                at_least_unit(dve, u_hi, pl, name, per, k)
                tt(dst, src, hi.bitcast(F32), ALU.subtract).then_inc(u_lo, 1)

            dve.wait_ge(sem("params_ready"), 1)
            dve.wait_ge(sem("half_set"), 1)
            rms(0, G1, idx=0)
            for n in range(AHEAD):
                dve.wait_ge(w_hi, n + 1)
                tt(WLO[:, n, :], RAW[:, n, :], WHI[:, n, :].bitcast(F32), ALU.subtract).then_inc(w_lo, 1)
            for name in ("v1", "conv1", "small1", "nsa1", "vsw1"):
                if name == "conv1":
                    conv_stage("conv1", 0)
                    continue
                pl = Place(name, 0)
                a = ADA0[name]
                for k in range(pl.nb):
                    split_lo(dve, pl, k + AHEAD)
                    a = ada(pl, name, k, a)

            dve.wait_ge(sem("log_f_parts"), 1)
            dve.wait_ge(sem("row_zero"), 2)
            r0, r1, r2, r3, r4 = (ROW[k][0:4, :] for k in range(5))
            chained(ts(r0, r0, 0.0, None, ALU.min))
            chained(tt(r0, r0, r1, ALU.subtract))
            chained(dve.tensor_tensor_scan(r2, r0, r3, 0.0, ALU.add, ALU.add))
            chained(tt(SM[0:4, :], SMR[0:4, :], r2, ALU.subtract))
            chained(dve.tensor_tensor_scan(r4, SM[0:4, :], r3, 0.0, ALU.max, ALU.add))
            tt(SM[32:36, :], r2, r4, ALU.add).then_inc(sem("packed_um"), 1)
            dve.wait_ge(sem("packed_cols"), 1)
            ts(col(NE, 16).rearrange("p (n h) -> p n h", h=4), SMT[:, :, 32:36], -87.0, None, ALU.max)\
                .then_inc(sem("neg_m"), 1)
            dve.wait_ge(sem("exp_neg_m"), 1)
            for h in range(MH):
                dve.wait_ge(sem("m_copied"), h + 1)
                if h:
                    dve.wait_ge(sem("decay_ready"), 4 * h)
                tt(ROW[1][:].rearrange("p (n t) -> p n t", t=P), ROW[0][:].rearrange("p (n t) -> p n t", t=P),
                   b3m(CST[:, K_CMT:K_CMT + P], NT), ALU.subtract).then_inc(sem("m_masked"), 1)
                for j in range(NT):
                    o, n = (0, 512, 896, 1152)[j], T - j * P
                    dve.wait_ge(sem("decay_ready"), 4 * h + j + 1)
                    dve.wait_ge(sem("s_ready"), 4 * h + j + 1)
                    stt(DP[:, h % 2, o:o + n], PS[:, 5 + j % 2, 0:n], 0.0625, DP[:, h % 2, o:o + n], ALU.mult, ALU.mult)\
                        .then_inc(sem("p_ready"), 1)
                for i in range(NT):
                    dve.wait_ge(sem("pv_ready"), 4 * h + i + 1)
                    ps = PS[:, 7 if i % 2 == 0 else 4, :]
                    chained(ts(col(DEN), ps[:, MD:MD + 1], -1.0, col(NE + 4 * i + h), ALU.mult, ALU.max))
                    chained(ts(col(DEN), ps[:, MD:MD + 1], col(DEN), None, ALU.max))
                    chained(dve.reciprocal(col(DEN + 1), col(DEN)))
                    chained(ts(MTOK[:, h, i, :], ps[:, 0:MD], col(DEN + 1), None, ALU.mult))
                    chained(dve.bn_stats(col(BST, 6), MTOK[:, h, i, :]))
                    dve.bn_aggr(col(MVS + 2 * (4 * h + i), 2), col(BST, 6)).then_inc(sem("pv_used"), 1)
            dve.wait_ge(sem("pv_used"), 16)
            mv = col(MVS, 32).rearrange("p (n c) -> p n c", c=2)
            chained(ts(col(RST, 16).unsqueeze(2), mv[:, :, 1:2], EPS, None, ALU.add))
            dve.reciprocal(col(RST, 16), col(RST, 16)).then_inc(sem("ln_recip"), 1)
            dve.wait_ge(sem("ln_rstd"), 1)
            for h in range(MH):
                for i in range(NT):
                    m = 4 * h + i
                    ts(MTOK[:, h, i, :], MTOK[:, h, i, :], col(MVS + 2 * m), col(RST + m), ALU.subtract, ALU.mult)\
                        .then_inc(sem("h_normed"), 1)

            def oz(pl):
                a = 56
                for f in range(4):
                    for q in range(2):
                        k = 2 * f + q
                        split_lo(dve, pl, k + AHEAD)
                        if k < 7:
                            a = ada(pl, "oz1", k, a)
                    so, sz = ROW[2 * (f % 2)], ROW[2 * (f % 2) + 1]
                    fk = ds(pl.i * 4 + f, 1)
                    if f == 0:
                        dve.wait_ge(sem("mht_ready"), 8)
                    pl.at_least(dve, nonlin, GATES["oz1"] + f + 1, 0, 4)
                    chained(tt(so[:].unsqueeze(1), so[:].unsqueeze(1), MHT[:, fk, :], ALU.mult))
                    cnt.mark(tt(sz[:], sz[:], PS[:, pl.bank(2 * f + 1), :], ALU.mult))
                    cnt.wait()
                    dve.sem_inc(bank_free[pl.bank(2 * f + 1)], 1)
                    tt(so[:], so[:], sz[:], ALU.mult).then_inc(product, 1)
                    unit_lo(pl, "oz1", 4, f, YALO[:, fk, :], so[:].unsqueeze(1), YAHI[:, fk, :])
                    if f == 3:
                        a = ada(pl, "oz1", 7, a)
            stage("oz1", 8, oz)

            two_pi = 2 * np.pi
            c1 = float(np.float32(np.round(two_pi * 64) / 64))
            c2 = float(np.float32(np.round((two_pi - c1) * 2.0 ** 16) / 2.0 ** 16))
            c3 = float(np.float32(two_pi - c1 - c2))
            magic = float(1.5 * 2 ** 23)
            dve.wait_ge(sem("pos_loaded"), 16)
            chained(dve.tensor_copy(ANG[:], POSI[:]))
            chained(ts(ANG[:], ANG[:], CST[:, K_INV:K_INV + 1], None, ALU.mult))
            chained(ts(TRN[:], ANG[:], 1.0 / two_pi, magic, ALU.mult, ALU.add))
            chained(ts(TRN[:], TRN[:], magic, None, ALU.subtract))
            for c in (c1, c2, c3):
                chained(stt(ANG[:], TRN[:], -c, ANG[:], ALU.mult, ALU.add))
            ts(ANG[:], ANG[:], 3.1415925, -3.1415925, ALU.min, ALU.max).then_inc(sem("angles"), 1)
            dve.wait_ge(sem("sines"), 1)
            chained(tt(RCOS[:], RTMP[:], RTMP[:], ALU.mult))
            ts(RCOS[:], RCOS[:], -2.0, 1.0, ALU.mult, ALU.add).then_inc(sem("rope_tables"), 1)
            for t in range(6):
                dst = QROPE[:, t, :] if t < 4 else KR[:, t - 4, :]
                dve.wait_ge(sem("rope_perm"), t + 1)
                if t:
                    dve.wait_ge(sem("roped"), t)
                chained(tt(RTMP[:], PS[:, 4 + t % 4, :], RSIN[:], ALU.mult))
                dve.wait_ge(sem("rope_cos_part"), t + 1)
                tt(dst, dst, RTMP[:], ALU.add).then_inc(sem("roped"), 1)
            dve.wait_ge(sem("roped"), 6)
            for s in range(2):
                if s:
                    dve.wait_ge(sem("cmp_hid_sum"), 1)
                for h in range(2):
                    src = KVR[:, s, CS * h:CS * h + CS * NC].rearrange("p (n b) -> p b n", b=CS)
                    pos = col(POST + 32 * s + CS * h, CS)
                    ins = tt(BLK[:, CS * h:CS * h + CS, :], src, b3(pos, NC), ALU.add)
                    chained(ins) if h == 0 else ins.then_inc(sem("cmp_blocks"), 1)
            for i in range(NT):
                dve.wait_ge(sem("cmp_s_sum"), i + 1)
                if i == 0:
                    dve.wait_ge(sem("w1_loaded"), 64)
                    dve.wait_ge(sem("cmp_hid_sum"), 2)
                for p in range(2):
                    stt(SC[:, i, p], PS[:, 4 + 2 * (i % 2) + p, 0:P].rearrange("p (q n) -> p q n", n=32), DK ** -0.5,
                        b3m(CST[:, K_CA + 32 * i:K_CA + 32 * i + 32], 4), ALU.mult, ALU.add).then_inc(sem("cmp_scored"), 1)
            dve.wait_ge(sem("cmp_scored"), 8)
            sc = SC[:].rearrange("p i a q n -> p (i a q) n")
            mx, sm = col(CMX, 32), col(CMX + 32, 32)
            chained(dve.tensor_reduce(mx, sc, AX, ALU.max))
            tt(sc, sc, b3(mx, 32), ALU.subtract).then_inc(sem("cmp_shifted"), 1)
            dve.wait_ge(sem("cmp_exp"), 1)
            chained(dve.tensor_reduce(sm, sc, AX, ALU.add))
            chained(dve.reciprocal(sm, sm))
            chained(tt(sc, sc, b3(sm, 32), ALU.mult))
            for i in range(NT):
                v = SC[:, i].rearrange("p a q n -> p (a q) n")
                ins = tt(v, v, b3m(CST[:, K_CK + 32 * i:K_CK + 32 * i + 32], 8), ALU.mult)
                chained(ins) if i < NT - 1 else ins.then_inc(sem("cmp_probs"), 1)

            def gate(i, first, n, step):
                return SMT[:, i, 64 + first:64 + first + step * (n - 1) + 1:step]

            for i in range(NT):
                dve.wait_ge(sem("cmp_o_sum"), i + 1)
                for p in range(2):
                    tt(YTOK[:, i, :, p, :], PS[:, 6 + i % 2, 256 * p:256 * p + 256].rearrange("p (q d) -> p q d", d=DK),
                       b3(gate(i, 3 * p, 4, 6), DK), ALU.mult).then_inc(sem("y_cmp"), 1)
            dve.wait_ge(sem("y_cmp"), 8)
            units = [(i, g, b, hh) for i in range(NT) for g in range(NG) for b in range(2) for hh in range(4)]

            def add_branch(w):
                i, g, b, _ = units[4 * w]
                dve.wait_ge(sem("exp_done"), 4 * w + 4)
                chained(dve.reciprocal(col(AG, 4), col(SUM + 4 * (w % 2), 4)))
                chained(tt(col(AG + 4, 4), col(AG, 4), gate(i, 12 * g + 1 + b, 4, 3), ALU.mult))
                dve.wait_ge(sem("nsa_o"), 4 * w + 4)
                o = OTMP[:, 0:256].rearrange("p (h d) -> p h d", d=DK)
                chained(tt(o, PS[:, 7, 256 * (w % 2):256 * (w % 2) + 256].rearrange("p (h d) -> p h d", d=DK),
                           b3(col(AG + 4, 4), DK), ALU.mult))
                y = YTOK[:, i, 2 * g:2 * g + 2].rearrange("p q a d -> p (q a) d")
                tt(y, y, o, ALU.add).then_inc(sem("y_added"), 1)

            for u, (i, g, b, hh) in enumerate(units):
                n = (i + 1) * P
                dve.wait_ge(sem("nsa_s"), u + 1)
                ps = PS[:, 4 + hh % 2, 0:n]
                if u >= 4:
                    dve.wait_ge(sem("exp_done"), u - 3)
                chained(dve.tensor_tensor_reduce(out=ps, in0=ps, in1=CST[:, K_CM + 512 - n:K_CM + 512], scale=DK ** -0.5,
                                                 scalar=-3.0e38, op0=ALU.add, op1=ALU.max, accum_out=col(MX + u % 4)))
                ts(col(MX + 4 + u % 4), col(MX + u % 4), -1.0, None, ALU.mult).then_inc(sem("max_ready"), 1)
                if u >= 6 and (u - 6) % 4 == 0:
                    add_branch((u - 6) // 4)
            for w in range((len(units) - 7) // 4 + 1, 16):
                add_branch(w)
            pl = Place("nz1", 0)
            for f in range(4):
                split_lo(dve, pl, f + AHEAD)
                pl.at_least(dve, nonlin, GATES["nz1"] + f + 1, 0, 4)
                dve.wait_ge(sem("yt_ready"), f + 1)
                s = NZS[:, f % 2, :]
                chained(tt(s, s, PS[:, pl.bank(f), :], ALU.mult))
                tt(s, s, YT[:, f, :], ALU.mult).then_inc(product, 1)
                dve.sem_inc(bank_free[pl.bank(f)], 1)
                unit_lo(pl, "nz1", 4, f, YBLO[:, f, :], s, YBHI[:, f, :])

            def merge(name, gates, hi, lo):
                def body(pl):
                    for f in range(2):
                        for q in range(4):
                            split_lo(dve, pl, 4 * f + q + AHEAD)
                            if q >= 2:
                                tiles_ready(dve, pl, 4 * f + q)
                                g = gates[:, 2 * f + q - 2, :]
                                cnt.mark(tt(g, g, PS[:, pl.bank(4 * f + q), :], ALU.mult))
                        cnt.wait()
                        for q in (2, 3):
                            dve.sem_inc(bank_free[pl.bank(4 * f + q)], 1)
                        tt(gates[:, 2 * f, :], gates[:, 2 * f, :], gates[:, 2 * f + 1, :], ALU.add).then_inc(product, 1)
                        fk = ds(pl.i * 2 + f, 1)
                        unit_lo(pl, name, 2, f, lo[:, fk, :], gates[:, 2 * f:2 * f + 1, :], hi[:, fk, :])
                stage(name, 4, body)

            def residual(name, per_tile, gate_col, last=False):
                def body(pl):
                    for f in range(4):
                        for c in range(per_tile):
                            split_lo(dve, pl, per_tile * f + c + AHEAD)
                        tiles_ready(dve, pl, per_tile * f + per_tile - 1)
                        fk = ds(pl.i * 4 + f, 1)
                        ps = PS[:, pl.bank(f):pl.bank(f) + 1, :]
                        xt = XT[:, fk, :]
                        if gate_col is None:
                            ins = tt(xt, ps, xt, ALU.add)
                        else:
                            ins = stt(xt, ps, PAR[:, ds(pl.i * 4 + (gate_col + f), 1)], xt, ALU.mult, ALU.add)
                        cnt.mark(ins)
                        cnt.wait()
                        dve.sem_inc(x_ready, 1)
                        dve.sem_inc(bank_free[pl.bank(f)], 1)
                stage(name, 4, body)

            def ffn_in(name):
                def body(pl):
                    for f in range(2):
                        split_lo(dve, pl, 2 * f + AHEAD)
                        split_lo(dve, pl, 2 * f + 1 + AHEAD)
                        tiles_ready(dve, pl, 2 * f + 1)
                        pl.at_least(dve, bank_free[pl.bank(2 * f)], (pl.tile + 2 * f) // 4 + 1, 0, pl.tb // 4)
                        cnt.mark(tt(FS[:, f, :], FS[:, f, :], PS[:, pl.bank(2 * f + 1), :], ALU.mult))
                        cnt.wait()
                        dve.sem_inc(product, 1)
                        dve.sem_inc(bank_free[pl.bank(2 * f + 1)], 1)
                        fk = ds(pl.i * 2 + f, 1)
                        unit_lo(pl, name, 2, f, HIDLO[:, fk, :], FS[:, f:f + 1, :], HIDHI[:, fk, :])
                stage(name, 2, body)

            def coef(sub):
                chained(stt(col(COEF, 8), col(MOD + 24 * sub + 8, 8), 1.0, col(G2 + 8 * sub, 8), ALU.add, ALU.mult))

            merge("merge1", GT, MGHI, MGLO)
            residual("out1", 1, None)

            for sub in (0, 2):
                chained(ts(col(MOD + 24 * sub + 16, 8), col(MOD + 24 * sub + 16, 8), 0.5, None, ALU.mult))
            rms(1, FNG, dst=XT)
            coef(0)
            rms(2, COEF, shift=MOD, idx=1)
            ffn_in("ffn1_in")
            residual("ffn1_out", 3, MOD + 16)
            coef(1)
            rms(3, COEF, shift=MOD + 24, idx=2)
            conv_stage("conv2", 16)
            pl = Place("small2", 0)
            split_lo(dve, pl, AHEAD)

            e0, e1, e2 = (EROW[k][0:8, :] for k in range(3))
            l0, l1, l2 = (LPR[0:8, k, :] for k in range(3))
            dve.wait_ge(sem("softplus_parts"), 1)
            dve.wait_ge(sem("row_zero"), 5)
            chained(stt(SM[0:8, :], l2, 1.0, l0, ALU.is_equal, ALU.mult))
            chained(ts(l2, l2, -1.0, 2.0 ** -24, ALU.add, ALU.max))
            chained(dve.reciprocal(l2, l2))
            chained(tt(l2, l2, l0, ALU.mult))
            chained(tt(l1, l1, l2, ALU.mult))
            chained(tt(l1, l1, SM[0:8, :], ALU.add))
            chained(ts(e0, e0, 0.0, None, ALU.max))
            chained(tt(e0, e0, l1, ALU.add))
            chained(ts(e0, e0, PAR[0:8, ALOG:ALOG + 1], -1.0, ALU.mult, ALU.mult))
            chained(dve.tensor_tensor_scan(l0, e2, e0, 0.0, ALU.mult, ALU.add))
            cnt.mark(dve.tensor_copy(e0, l0))
            cnt.mark(dve.tensor_copy(SM[32:40, :], l0))
            g3 = l0.rearrange("p (c t) -> p c t", t=P)
            cnt.mark(tt(SM[64:72, :].rearrange("p (c t) -> p c t", t=P), g3[:, :, P - 1:P].to_broadcast([8, NT, P]), g3,
                        ALU.subtract))
            dve.wait_ge(sem("beta_rows"), 1)
            cnt.mark(dve.tensor_copy(SM[0:8, :], e1))
            cnt.wait()
            dve.sem_inc(sem("packed2"), 2)
            for h in range(16):
                dve.wait_ge(sem("norm_root"), h + 1)
                r = NRT[:, h % 2, :]
                chained(dve.reciprocal(r, r))
                tt(QKV[:, h, :], QKV[:, h, :], r, ALU.mult).then_inc(sem("qk_normed"), 1)
            dve.wait_ge(sem("delta_cols"), 1)

            def ps4(bk):
                return PS[:, bk, :].rearrange("p (h n) -> p h n", n=P)

            def ccol(base, c, a):
                return b3(PAR[:, base + 8 * c + 4 * a:base + 8 * c + 4 * a + 4], P)

            id4 = b3m(ID, 4)
            for c in range(NT):
                k2 = 2 * c
                for a in range(2):
                    h4 = slice(4 * a, 4 * a + 4)
                    dve.wait_ge(sem("end_decay"), k2 + a + 1)
                    if c and a == 0:
                        dve.wait_ge(sem("intra_sum"), 2 * c)
                    tt(DD[:, h4, :], ps4(4 + 2 * a), b3(SMT[:, c, 32 + 4 * a:36 + 4 * a], P), ALU.subtract)\
                        .then_inc(sem("decay_arg"), 1)
                    dve.wait_ge(sem("decay_arg"), k2 + a + 1)
                    tt(DD[:, h4, :], DD[:, h4, :], b3m(CST[:, K_CMT:K_CMT + P], 4), ALU.add)\
                        .then_inc(sem("decay_masked"), 1)
                for a in range(2):
                    h4 = slice(4 * a, 4 * a + 4)
                    dve.wait_ge(sem("decay_exp"), k2 + a + 1)
                    dve.wait_ge(sem("kk_sum"), k2 + a + 1)
                    tt(MT[:, h4, :], ps4(5 + 2 * a), DD[:, h4, :], ALU.mult).then_inc(sem("kk_decayed"), 1)
                for a in range(2):
                    h4 = slice(4 * a, 4 * a + 4)
                    dve.wait_ge(sem("kk_decayed"), k2 + a + 1)
                    dve.wait_ge(sem("beta_bcast"), k2 + a + 1)
                    tt(MT[:, h4, :], ps4(4 + 2 * a), MT[:, h4, :], ALU.mult).then_inc(sem("delta_a"), 1)
                    dve.wait_ge(sem("qk_sum"), k2 + a + 1)
                    stt(QKM[:, h4, :], ps4(5 + 2 * a), float(128 ** -0.5), DD[:, h4, :], ALU.mult, ALU.mult)\
                        .then_inc(sem("qk_decayed"), 1)
                for a in range(2):
                    h4 = slice(4 * a, 4 * a + 4)
                    dve.wait_ge(sem("delta_a"), k2 + a + 1)
                    chained(tt(TT[:, h4, :], MT[:, h4, :], b3m(CST[:, K_LV:K_LV + P], 4), ALU.mult))
                    tt(TT[:, h4, :], id4, TT[:, h4, :], ALU.subtract).then_inc(sem("inv_T_ready"), 1)
                for lv in range(1, LEVELS):
                    for a in range(2):
                        h4 = slice(4 * a, 4 * a + 4)
                        dve.wait_ge(sem("inv_step"), (c * 6 + lv - 1) * 2 + a + 1)
                        dve.wait_ge(sem("inv_T_ready"), (c * LEVELS + lv - 1) * 2 + a + 1)
                        tt(TT[:, h4, :], TT[:, h4, :], ps4(5 + 2 * a), ALU.subtract).then_inc(sem("inv_T_ready"), 1)
                for a in range(2):
                    h4 = slice(4 * a, 4 * a + 4)
                    r = RV[:, h4, :]
                    dve.wait_ge(sem("v_tokens"), k2 + a + 1)
                    if c:
                        dve.wait_ge(sem("ks_sum"), k2 - 2 + a + 1)
                        chained(tt(DD[:, h4, :], ps4(5 + 2 * a), ccol(EG, c, a), ALU.mult))
                        chained(tt(r, r, DD[:, h4, :], ALU.subtract))
                    tt(r, r, b3(SMT[:, c, 4 * a:4 * a + 4], P), ALU.mult).then_inc(sem("rhs_ready"), 1)
                for a in range(2):
                    h4 = slice(4 * a, 4 * a + 4)
                    dve.wait_ge(sem("k_T"), k2 + a + 1)
                    tt(KDT[:, h4, :], ps4(5 + 2 * a), ccol(EKD, c, a), ALU.mult).then_inc(sem("k_dec"), 1)
                for a in range(2):
                    h4 = slice(4 * a, 4 * a + 4)
                    o = OO[:, h4, :]
                    if c:
                        dve.wait_ge(sem("qs_sum"), k2 - 2 + a + 1)
                        tt(o, ps4(4 + 2 * a), ccol(QEG, c, a), ALU.mult).then_inc(sem("o_inter"), 1)
                        dve.wait_ge(sem("o_inter"), k2 - 2 + a + 1)
                    dve.wait_ge(sem("intra_sum"), k2 + a + 1)
                    if c:
                        chained(tt(o, ps4(5 + 2 * a), o, ALU.add))
                    else:
                        chained(dve.tensor_copy(o, ps4(5 + 2 * a)))
                for a in range(2):
                    h4 = slice(4 * a, 4 * a + 4)
                    s = SS[:, h4, :]
                    dve.wait_ge(sem("state_sum"), k2 + a + 1)
                    if c:
                        chained(tt(s, s, b3(PAR[:, EGL + 4 * a:EGL + 4 * a + 4], P), ALU.mult))
                        tt(s, s, ps4(4 + 2 * a), ALU.add).then_inc(sem("state_new"), 1)
                    else:
                        dve.tensor_copy(s, ps4(4 + 2 * a)).then_inc(sem("state_new"), 1)
                chained(tt(RV[:], OO[:], OO[:], ALU.mult))
                chained(dve.tensor_reduce(col(RSO, 8), RV[:], AX, ALU.add))
                ts(col(RSO, 8), col(RSO, 8), 1.0 / P, EPS, ALU.mult, ALU.add).then_inc(sem("o_var"), 1)
                dve.wait_ge(sem("o_rstd"), c + 1)
                tt(OO[:], OO[:], b3(col(RSO, 8), P), ALU.mult).then_inc(sem("o_normed"), 1)

            def z2(pl):
                for f in range(4):
                    split_lo(dve, pl, f + AHEAD)
                    pl.at_least(dve, nonlin, GATES["z2"] + f + 1, 0, 4)
                    if f == 0:
                        dve.wait_ge(sem("o_T_taken"), 8)
                    g = TMP2[:, f:f + 1, :]
                    fk = ds(pl.i * 4 + f, 1)
                    chained(tt(g, g, PS[:, pl.bank(f):pl.bank(f) + 1, :], ALU.mult))
                    tt(g, g, QKV[:, ds(pl.i * 4 + (16 + f), 1), :], ALU.mult).then_inc(product, 1)
                    dve.sem_inc(bank_free[pl.bank(f)], 1)
                    unit_lo(pl, "z2", 4, f, Y2LO[:, fk, :], g, Y2HI[:, fk, :])
            stage("z2", 4, z2)

            pl = Place("pool2", 0)
            for g in range(4):
                split_lo(dve, pl, g + AHEAD)
                tiles_ready(dve, pl, g)
                if g:
                    dve.wait_ge(sem("pool_sum"), g)
                ps = PS[:, pl.bank(g), :]
                chained(dve.tensor_copy(PLS[:, 0, :], ps))
                cur = 0
                for lv in range(g + 1):
                    b = 1 << lv
                    nxt = 1 - cur
                    cnt.mark(dve.tensor_copy(PLS[:, nxt, 0:b], PLS[:, cur, 0:b]))
                    chained(tt(PLS[:, nxt, b:T], PLS[:, cur, b:T], PLS[:, cur, 0:T - b], ALU.add))
                    cur = nxt
                s = PLS[:, cur, :]
                chained(tt(s[:, 0:16], s[:, 0:16], CST[:, K_FIX + 16 * g:K_FIX + 16 * g + 16], ALU.mult))
                chained(ts(PLS[:, 2, :], s, 1.0 / (2 << g), None, ALU.mult))
                cnt.mark(tt(PLS[:, 2, :], PLS[:, 2, :], ps, ALU.subtract))
                cnt.wait()
                dve.sem_inc(product, 1)
                dve.sem_inc(bank_free[pl.bank(g)], 1)
                dve.wait_ge(u_hi, UNITS["pool2"] + g + 1)
                tt(PLLO[:, g, :], PLT[:], PLHI[:, g, :].bitcast(F32), ALU.subtract).then_inc(u_lo, 1)
            merge("merge2", GT2, M2HI, M2LO)
            residual("out2", 1, MOD + 24 + 16)
            coef(2)
            rms(4, COEF, shift=MOD + 48, idx=3)
            ffn_in("ffn2_in")
            for i in range(INFO["ffn2_out"]["iters"]):
                pl = Place("ffn2_out", 0)
                pl.chunk += pl.nb * i
                pl.tile += pl.tb * i
                pl.iters = 1
                for f in range(4):
                    for q in range(3):
                        split_lo(dve, pl, 3 * f + q + AHEAD)
                    tiles_ready(dve, pl, 3 * f + 2)
                    xt = XT[:, 4 * i + f, :]
                    chained(stt(xt, PS[:, pl.bank(f), :], col(MOD + 48 + 16 + 4 * i + f), xt, ALU.mult, ALU.add))
                    dve.sem_inc(x_ready, 1)
                    dve.sem_inc(bank_free[pl.bank(f)], 1)
            rms(5, FG2, dst=XT)


_INS = ["x", "positions", "norm_g", "w_in", "conv_q_w", "conv_q_b", "conv_k_w", "conv_k_b", "b_igate", "b_fgate",
        "mh_norm_g", "cmp_pos_k", "cmp_w1_k", "cmp_w2_k", "cmp_pos_v", "cmp_w1_v", "cmp_w2_v", "b_nsa_gate",
        "w_branch_a", "w_branch_b", "w_out", "final_norm_g", "c_2", "ada_w_2", "ada_b_2", "norm_g_2",
        "ffn1_w_in_2", "ffn1_w_out_2", "ffn2_w_in_2", "ffn2_w_out_2", "mix_w_in_2", "conv_w_2", "a_log_2",
        "dt_bias_2", "dn_norm_g_2", "pool_w_2", "pool_scale_2", "pool_proj_2", "dn_proj_2", "mix_w_out_2",
        "final_g_2"]


def kernel(**inputs):
    import concourse.bacc as bacc
    from concourse.bass_utils import run_bass_kernel_spmd

    nc = bacc.Bacc("TRN2", target_bir_lowering=False, num_devices=1)
    arrays = {"in_constants": constants()}
    arrays.update({f"in_{n}": np.ascontiguousarray(inputs[n]) for n in _INS})
    args = [nc.dram_tensor(n, a.shape, mybir.dt.from_np(a.dtype), kind="ExternalInput").ap()
            for n, a in arrays.items()]
    out = nc.dram_tensor("out", (1, T, D), F32, kind="ExternalOutput").ap()
    two_blocks(nc, *args, out)
    return run_bass_kernel_spmd(nc, [arrays], core_ids=[0]).results[0]["out"]
```

```python
from contextlib import ExitStack

import numpy as np

import concourse.bass as bass
from concourse import mybir

F32 = mybir.dt.float32
F32R = mybir.dt.float32r
I32 = mybir.dt.int32
ALU = mybir.AluOpType
ACT = mybir.ActivationFunctionType
AX = mybir.AxisListType.X
ds = bass.ds

P = 128
T = 512
NT = T // P
D = 1024
KD = D // P
EPS = 1e-6
NEG = -1e30

MH, MD = 4, 256
NHD, NG, DK = 8, 2, 64
C_Q, C_K, C_V, C_O, C_Z = 0, 1024, 2048, 3072, 4096
C_I, C_F = 5120, 5124
C_NQ, C_KC, C_VC, C_KS, C_VS, C_KW, C_VW = 5128, 5640, 5768, 5896, 6024, 6152, 6280
C_NG, C_NZ, C_GA, C_GB = 6408, 6432, 6944, 7968
CB, CS, CH = 32, 16, 128
NC = (T - CB) // CS + 1
ROPE_HALF = 8
X_P, X_Q, X_Z, X_B, X_A, X_GP, X_GD = 0, 512, 3584, 4608, 4616, 4624, 5648
DH = 8
FF = 2816
NF = FF // P
LEVELS = 7

K_ID, K_ONE, K_CM, K_CMT, K_ROPE, K_SWAP, K_LV = 0, 128, 256, 768, 896, 1024, 1152
K_CA = K_LV + LEVELS * P
K_CK = K_CA + 128
K_FIX = K_CK + 128
K_INV = K_FIX + 64
K_SEL = K_INV + 1
K_ALL = K_SEL + 31


def constants():
    c = np.zeros((P, K_ALL), np.float32)
    r = np.arange(P)
    c[:, K_ID:K_ID + P] = np.eye(P)
    c[:, K_ONE:K_ONE + P] = 1
    c[:, K_CM + 384:K_CM + 512] = np.where(r[None, :] <= r[:, None], 0, NEG)
    c[:, K_CMT:K_CMT + P] = np.where(r[None, :] >= r[:, None], 0, NEG)
    for k in range(P):
        d = k % DK
        if d < ROPE_HALF:
            c[k, K_ROPE + k + ROPE_HALF] = 1
            c[k, K_INV] = np.power(np.float32(500000.0), np.float32(-d * (2.0 / 16)))
        elif d < 2 * ROPE_HALF:
            c[k, K_ROPE + k - ROPE_HALF] = -1
            c[k, K_INV] = np.power(np.float32(500000.0), np.float32(-(d - ROPE_HALF) * (2.0 / 16)))
        c[k, K_SWAP + (k + DK) % P] = 1
    c[:, K_SEL + 15] = 1
    for lv in range(LEVELS):
        b = 1 << lv
        i, j = r[None, :], r[:, None]
        c[:, K_LV + lv * P:K_LV + lv * P + P] = (i // (2 * b) == j // (2 * b)) & (i // b % 2 == 1) & (j // b % 2 == 0)
    t = (np.arange(NT)[None, :, None] * P + r[:, None, None])
    n = np.arange(32)[None, None, :]
    ok = (n * CS + CB - 1 <= t) & (n < NC)
    c[:, K_CA:K_CA + 128] = np.where(ok, 0, NEG).reshape(P, 128)
    c[:, K_CK:K_CK + 128] = ok.reshape(P, 128)
    for g in range(4):
        w = 2 << g
        c[:, K_FIX + 16 * g:K_FIX + 16 * g + 16] = w / np.minimum(np.arange(1, 17), w)
    return c


G1, CQW, CQB, MHG, FNG = 0, 8, 72, 88, 96
N1 = 104
G2, CW2 = N1, N1 + 24
N2 = 120
ADAB, DNG, PSC, FG2, CVEC = N1 + N2, N1 + N2 + 72, N1 + N2 + 73, N1 + N2 + 77, N1 + N2 + 85
N3 = 93
MOD = N1 + N2 + N3
COEF = MOD + 72
SILC = COEF + 8
SMB = SILC + 8
ALOG, DTB = SMB + 1, SMB + 2
POST = SMB + 3
MVS = POST + 64
RST = MVS + 32
NE = RST + 16
DEN = NE + 16
BST = DEN + 32
MX = BST + 24
SUM = MX + 8
AG = SUM + 8
KCT = AG + 8
CMX = KCT + 128
EG = CMX + 64
EKD = EG + 32
QEG = EKD + 32
EGL = QEG + 32
RSO = EGL + 8
HALF = RSO + 8
RCOL = HALF + 8
FCOEF = RCOL + 8
PAR_ALL = FCOEF + 8


class Count:

    def __init__(self, eng, sem):
        self.eng, self.sem, self.n, self.i, self.step = eng, sem, 0, 0, 0

    def mark(self, ins):
        ins.then_inc(self.sem, 1)
        self.n += 1
        return self.n

    def wait(self, n=None):
        n = self.n if n is None else n
        self.eng.wait_ge(self.sem, self.i * self.step + n if self.step else n)

    def loop(self, times, step, body):
        start, self.step = self.n, step
        with self.eng.Fori(0, times) as i:
            self.i = i
            body(i)
            assert self.n - start == step, (self.n - start, step)
        self.i, self.step = 0, 0
        self.n = start + times * step


def two_blocks(nc, cst, x, positions, norm_g, w_in, conv_q_w, conv_q_b, conv_k_w, conv_k_b, b_igate,
               b_fgate, mh_norm_g, cmp_pos_k, cmp_w1_k, cmp_w2_k, cmp_pos_v, cmp_w1_v, cmp_w2_v,
               b_nsa_gate, w_branch_a, w_branch_b, w_out, final_norm_g, c_2, ada_w_2, ada_b_2,
               norm_g_2, ffn1_w_in_2, ffn1_w_out_2, ffn2_w_in_2, ffn2_w_out_2, mix_w_in_2, conv_w_2,
               a_log_2, dt_bias_2, dn_norm_g_2, pool_w_2, pool_scale_2, pool_proj_2, dn_proj_2,
               mix_w_out_2, final_g_2, out):
    ctx = ExitStack()
    with ctx:
        BASE = 16512
        assert nc.sbuf_base <= BASE
        at = [BASE]
        KB = 1024

        def fixed(name, shape, dt=F32):
            t = nc.alloc_sbuf_tensor_at(name, [P, *shape], dt, offset=at[0])
            at[0] += -(-int(np.prod(shape)) * 4 // 32) * 32
            return t

        XT = fixed("residual", [KD, T])
        HHI, HLO = fixed("act_hi", [KD, T], F32R), fixed("act_lo", [KD, T], F32R)
        RAW = fixed("w_raw", [4, 1024])
        WHI, WLO = fixed("w_hi", [4, 1024], F32R), fixed("w_lo", [4, 1024], F32R)
        CST = fixed("constants", [K_ALL])
        PAR = fixed("params", [PAR_ALL])
        PH = at[0]

        def phase(name, kb, shape, dt=F32):
            off = PH + int(kb * KB)
            assert off + int(np.prod(shape)) * 4 <= 229344, (name, off, shape)
            return nc.alloc_sbuf_tensor_at(name, [P, *shape], dt, offset=off)

        XTOK = phase("x_tokens", 0, [NT, D])
        PROW = phase("param_rows", 16, [4, P])
        SQ = phase("squares", 88, [4, T])
        RDIAG = phase("rms_diagonal", 96, [NT, P])
        RDIAG2 = phase("rms_diagonal2", 48, [NT, P])
        QK1 = phase("mlstm_qk_T", 0, [16, T])
        MTOK = phase("mlstm_h_tokens", 0, [MH, NT, MD])
        VTOK = phase("mlstm_v_tokens", 32, [NT, MH, MD + 1])
        MHT = phase("mlstm_h_T", 32, [KD, T])
        YAHI, YALO = phase("ya_hi", 0, [KD, T], F32R), phase("ya_lo", 16, [KD, T], F32R)
        QRAW = phase("nsa_q_T", 48.25, [4, T])
        KVR = phase("nsa_kv_T", 56.25, [4, T])
        YBHI, YBLO = phase("yb_hi", 48, [4, T], F32R), phase("yb_lo", 56, [4, T], F32R)
        ADAW = phase("ada_w", 66, [4, D])
        ADAC = [phase("ada_sum0", 82.5, [D]), phase("ada_sum1", 86.5, [D])]
        DP = phase("mlstm_decay_probs", 66, [2, 1280])
        VSW = phase("nsa_v_tokens", 78, [NT, 2, P])
        ROW = [phase(f"rows{i}", 82.5 + 2 * i, [T]) for i in range(4)] + [phase("rows4", 92, [T])]
        SMR = phase("gate_rows", 96, [T])
        SM = phase("packed_rows", 94, [T])
        SMT = phase("packed_cols", 96, [NT, P])
        QROPE = phase("nsa_q_rope", 66, [4, T])
        KR = phase("nsa_k_rope", 82.5, [4, T])
        RSIN, RTMP, RCOS = phase("rope_sin", 74, [T]), phase("rope_tmp", 76, [T]), phase("rope_cos", 92, [T])
        HID = phase("cmp_hidden", 90.5, [4, 32])
        VCB = phase("cmp_v_blocks", 94, [4, DK])
        POSI = phase("positions", 76, [T], I32)
        ANG, TRN = phase("angles", 84.5, [T]), phase("turns", 86.5, [T])
        W1 = phase("cmp_w1", 0, [CB, CH])
        W2 = phase("cmp_w2", 92, [2, P])
        BLK = phase("cmp_blocks", 24, [CB, NG, NC])
        SC = phase("cmp_scores", 16, [NT, 2, 4, 32])
        PCT = phase("cmp_probs_T", 20, [NT, 2, P])
        PR = phase("nsa_probs", 56.25, [2, T])
        PT = phase("nsa_probs_T", 60.25, [2, T])
        YTOK = phase("nsa_y_tokens", 48.25, [NT, 4, 2, DK])
        OTMP = phase("nsa_o_tmp", 74, [T // 2])
        OGATE = [phase("o_gate0", 91, [T]), phase("o_gate1", 93, [T])]
        ZGATE = phase("z_gate", 75.5, [T])
        YT = phase("nsa_y_T", 66, [4, T])
        MGHI, MGLO = phase("merged_hi", 72, [KD, T], F32R), phase("merged_lo", 32, [KD, T], F32R)
        GT = phase("merge_gates", 64, [4, T])
        NZS = phase("nz_gates", 74, [2, T])
        HIDHI, HIDLO = phase("ffn_hi", 0, [NF, T], F32R), phase("ffn_lo", 44, [NF, T], F32R)
        FS = phase("ffn_tmp", 88, [4, T])
        QKV = phase("delta_qkv_T", 0, [24, T])
        DD, MT, TT, TI = (phase(n, 48 + 4 * i, [DH, P]) for i, n in enumerate(
            ["delta_decay", "delta_a_T", "delta_inv_T", "delta_inv"]))
        XX, QKM, KDT, RV = (phase(n, 64 + 4 * i, [DH, P]) for i, n in enumerate(
            ["delta_x", "delta_qk_T", "delta_k_dec", "delta_rhs"]))
        VN, SS = phase("delta_v_new", 80, [DH, P]), phase("delta_state", 84, [DH, P])
        ML = phase("delta_level", 80, [DH, P])
        OO = phase("delta_o", 76, [DH, P])
        EROW = [phase(f"delta_rows{i}", 88 + 2 * i, [T]) for i in range(3)]
        NRM, NRT = phase("delta_squares", 56, [16, T]), phase("delta_roots", 54, [T])
        LPR = phase("softplus_rows", 48, [3, T])
        Y2HI, Y2LO = phase("yb2_hi", 48, [KD, T], F32R), phase("yb2_lo", 64, [KD, T], F32R)
        PLHI, PLLO = phase("pool_hi", 80, [4, T], F32R), phase("pool_lo", 40, [4, T], F32R)
        PLS = phase("pool_sums", 92, [2, T])
        PLW = phase("pool_w", 88, [4, P])
        GT2 = phase("merge2_gates", 0, [4, T])
        M2HI, M2LO = phase("merged2_hi", 8, [KD, T], F32R), phase("merged2_lo", 24, [KD, T], F32R)
        YTOK2 = phase("out_tokens", 0, [NT, D])

        PS = ctx.enter_context(nc.psum_tensor("psum", [P, 8, 512], F32))
        block = ctx.enter_context(nc.Block())

        names = {}

        def sem(name):
            if name not in names:
                names[name] = ctx.enter_context(nc.semaphore(name))
            return names[name]

        w_loaded = [sem(f"w_loaded{k}") for k in range(4)]
        w_hi, w_lo, chunk_done = sem("w_hi_ready"), sem("w_lo_ready"), sem("chunk_done")
        bank_free = [sem(f"bank_free{k}") for k in range(4)]

        ID = CST[:, K_ID:K_ID + P]
        ONES = CST[:, K_ONE:K_ONE + P]

        def col(n, k=1):
            return PAR[:, n:n + k]

        def wchunk(w, kt0, kts, c0, cols):
            return w[0].rearrange("(kt p) n -> p kt n", p=P)[:, kt0:kt0 + kts, c0:c0 + cols]

        def wdyn(w, kt0, kts, c0, cols):
            return w[0].rearrange("(kt p) n -> p kt n", p=P)[:, kt0:kt0 + kts, ds(c0, cols)]

        def merge_body(wg, ca, cb, wa, ka, wb, kb, nf):
            return lambda i: [c for f in range(nf) for c in (
                (wg, 0, 8, i * (P * nf) + (ca + P * f), P), (wg, 0, 8, i * (P * nf) + (cb + P * f), P),
                (wa, 0, ka, i * (P * nf) + P * f, P), (wb, 0, kb, i * (P * nf) + P * f, P))]

        def cols_body(w, c0, n):
            return lambda i: [(w, 0, 8, i * (P * n) + (c0 + P * f), P) for f in range(n)]

        def ffn_in_body(w):
            return lambda i: [c for f in range(2) for c in (
                (w, 0, 8, i * 256 + P * f, P), (w, 0, 8, i * 256 + (FF + P * f), P))]

        def ffn_out_body(w):
            return lambda i: [(w, k0, kn, i * 512 + P * f, P)
                              for f in range(4) for k0, kn in ((0, 8), (8, 8), (16, 6))]

        STAGES = [
            ("v1", 1, lambda i: [(w_in, 2 * k, 2, C_V + 512 * h, 512) for h in range(2) for k in range(4)], 8),
            ("conv1", 2, cols_body(w_in, C_Q, 8), 8),
            ("small1", 1, lambda i: ["small1"], 1),
            ("nsa1", 1, lambda i: [(w_in, 0, 8, c, P) for c in
                                   [C_NQ + P * f for f in range(4)] + [C_KC, C_VC, C_KS, C_KW]], 8),
            ("vsw1", 1, lambda i: ["vsw0", "vsw1"], 4),
            ("oz1", 1, lambda i: [(w_in, 0, 8, c + P * f, P) for f in range(8) for c in (C_O, C_Z)], 16),
            ("nz1", 1, cols_body(w_in, C_NZ, 4), 4),
            ("merge1", 4, merge_body(w_in, C_GA, C_GB, w_branch_a, 8, w_branch_b, 4, 2), 8),
            ("out1", 2, cols_body(w_out, 0, 4), 4),
            ("ffn1_in", 11, ffn_in_body(ffn1_w_in_2), 4),
            ("ffn1_out", 2, ffn_out_body(ffn1_w_out_2), 4),
            ("conv2", 2, cols_body(mix_w_in_2, X_Q, 8), 8),
            ("small2", 1, lambda i: ["small2"], 1),
            ("v2", 1, cols_body(mix_w_in_2, X_Q + 2048, 8), 8),
            ("pool2", 1, cols_body(mix_w_in_2, X_P, 4), 4),
            ("z2", 1, cols_body(mix_w_in_2, X_Z, 8), 8),
            ("merge2", 4, merge_body(mix_w_in_2, X_GP, X_GD, pool_proj_2, 4, dn_proj_2, 8, 2), 8),
            ("out2", 2, cols_body(mix_w_out_2, 0, 4), 4),
            ("ffn2_in", 11, ffn_in_body(ffn2_w_in_2), 4),
            ("ffn2_out", 2, ffn_out_body(ffn2_w_out_2), 4),
        ]
        INFO, c0, t0 = {}, 0, 0
        for name, iters, body, tiles in STAGES:
            nb = len(body(0))
            INFO[name] = dict(iters=iters, body=body, nb=nb, tb=tiles, chunk=c0, tile=t0)
            c0 += iters * nb
            t0 += iters * tiles
        N_CHUNKS = c0
        PV_BANK = (7, (INFO["oz1"]["tile"] + 2) % 4)
        AHEAD = 2

        class Place:

            def __init__(self, name, i):
                stage = INFO[name]
                self.iters, self.nb, self.tb = stage["iters"], stage["nb"], stage["tb"]
                self.chunk, self.tile, self.i = stage["chunk"], stage["tile"], i

            def at_least(self, eng, s, v, per):
                if self.iters > 1 and per:
                    v = self.i * per + v
                eng.wait_ge(s, v)

            def bank(self, t):
                return (self.tile + t) % 4

        def waited(eng, pl):
            if pl.iters > 1:
                eng.sem_inc(sem("loop_waits"), 1)

        def split_hi(act, pl, k):
            n = pl.chunk + k
            if n >= N_CHUNKS:
                return
            pl.at_least(act, w_loaded[n % 4], 16 * (n // 4 + 1), 4 * pl.nb)
            if n >= 4:
                pl.at_least(act, chunk_done, n - 3, pl.nb)
            act.activation(WHI[:, n % 4, :], RAW[:, n % 4, :], ACT.Copy).then_inc(w_hi, 1)

        def split_lo(dve, pl, k):
            n = pl.chunk + k
            if n >= N_CHUNKS:
                return
            pl.at_least(dve, w_hi, n + 1, pl.nb)
            dve.tensor_tensor(WLO[:, n % 4, :], RAW[:, n % 4, :], WHI[:, n % 4, :].bitcast(F32),
                              ALU.subtract).then_inc(w_lo, 1)

        def tile_used(ins, pl, t):
            ins.then_inc(bank_free[pl.bank(t)], 1)

        def load_chunk(sp, pl, k, desc):
            n = pl.chunk + k
            if n >= 4:
                pl.at_least(sp, w_lo, n - 3, pl.nb)
            slot = RAW[:, n % 4, :]
            if desc in ("small1", "small2"):
                wi = (w_in if desc == "small1" else mix_w_in_2)[0].rearrange("(kt p) n -> p kt n", p=P)
                v = slot.rearrange("p (k c) -> p k c", c=P)
                parts = ([(C_I, 4, 0), (C_F, 4, 32), (C_NG, 24, 64)] if desc == "small1"
                         else [(X_B, 8, 0), (X_A, 8, 32)])
                first = desc == "small1"
                for q, (c, m, to) in enumerate(parts):
                    d = sp.dma_start(v[:, :, to:to + m], wi[:, :, c:c + m])
                    if q < len(parts) - 1:
                        d.then_inc(sem("part_loaded"), 16)
                        sp.wait_ge(sem("part_loaded"), 16 * (q + 1 + (0 if first else 4)))
                    else:
                        d.then_inc(w_loaded[n % 4], 16)
                return
            if desc in ("vsw0", "vsw1"):
                h = int(desc[-1])
                v = slot.rearrange("p (k c) -> p k c", c=256)
                sp.dma_start(v[:, :, 0:P], wchunk(w_in, 4 * h, 4, C_VS, P)).then_inc(sem("part_loaded"), 16)
                sp.wait_ge(sem("part_loaded"), 16 * (3 + h))
                sp.dma_start(v[:, :, P:256], wchunk(w_in, 4 * h, 4, C_VW, P)).then_inc(w_loaded[n % 4], 16)
                return
            w, kt0, kts, c, cols = desc
            src = wchunk(w, kt0, kts, c, cols) if isinstance(c, int) else wdyn(w, kt0, kts, c, cols)
            waited(sp, pl)
            sp.dma_start(slot[:, 0:kts * cols].rearrange("p (k c) -> p k c", c=cols), src)\
              .then_inc(w_loaded[n % 4], 16)

        def mm3(pe, out, whi, wlo, hhi, hlo, start, stop):
            pe.matmul(out, whi, hhi, start=start, stop=False)
            pe.matmul(out, whi, hlo, start=False, stop=False)
            return pe.matmul(out, wlo, hhi, start=False, stop=stop)

        def pe_open(pe, pl, t):
            m = pl.tile + t
            if m >= 4:
                pl.at_least(pe, bank_free[m % 4], m // 4, pl.tb // 4)
            return PS[:, m % 4, :]

        def pe_tile(pe, pl, k, t, kts, rhi, rlo, k0=0, first=True, last=True, act_ready=None):
            n = pl.chunk + k
            bank = pe_open(pe, pl, t) if first else PS[:, (pl.tile + t) % 4, :]
            pl.at_least(pe, w_lo, n + 1, pl.nb)
            for kk in range(kts):
                if act_ready is not None:
                    act_ready(kk)
                a = slice(kk * P, kk * P + P)
                mm = mm3(pe, bank, WHI[:, n % 4, a], WLO[:, n % 4, a], rhi[:, k0 + kk, :], rlo[:, k0 + kk, :],
                         first and kk == 0, last and kk == kts - 1)
            mm.then_inc(chunk_done, 1)

        def stage_loop(cnt, name, step, body):
            it = INFO[name]["iters"]
            if it == 1:
                start = cnt.n
                body(Place(name, 0))
                assert cnt.n - start == step, (name, cnt.n - start, step)
            else:
                cnt.loop(it, step, lambda i: body(Place(name, i)))

        def tiles_ready(eng, pl, k):
            pl.at_least(eng, chunk_done, pl.chunk + k + 1, pl.nb)

        UNITS, u0 = {}, 0
        for name, per in (("oz1", 8), ("nz1", 4), ("merge1", 8), ("ffn1_in", 22), ("z2", 8), ("pool2", 4),
                          ("merge2", 8), ("ffn2_in", 22)):
            UNITS[name] = u0
            u0 += per
        def waiting(t):
            return QKV[:, 4 * (t % 4):4 * (t % 4) + 4, P * (t // 4):P * (t // 4) + P]

        def by_chunk(ap):
            return ap.rearrange("p (c t) -> p c t", t=P)

        def side_place(t):
            return (Place("v2", 0), t) if t < 8 else (Place("pool2", 0), t - 8) if t < 12 else (Place("z2", 0), t - 12)

        GATES = {"oz1": 0, "nz1": 8, "z2": 12}
        nonlin, product = sem("gate_ready"), sem("product_ready")
        u_hi, u_lo = sem("result_hi_ready"), sem("result_lo_ready")
        N_MOD = 9
        ADA = {"v1": [3] * 4 + [2] * 4, "conv1": [2, 1, 1, 1, 1, 1, 1, 0], "small1": [3], "nsa1": [3] * 8, "vsw1": [3, 2]}
        ADA0 = {"v1": 4, "conv1": 24, "small1": 40, "nsa1": 43, "vsw1": 67}
        MOD_AT = {("v1", 2): 0, ("v1", 5): 1, ("v1", 7): 2, ("conv1", 7): 3, ("nsa1", 2): 5, ("nsa1", 5): 6,
                  ("nsa1", 7): 7, ("last", 0): 8}
        SUM_AT = [0, 1, 0, 1, 1, 0, 1, 0, 1]
        NORM_X = [8, 16, 32, 40, 48]
        DOUBLE = 1
        x_ready, h_ready = sem("residual_ready"), sem("h_ready")

        def at_least_unit(eng, s, pl, name, per, k):
            pl.at_least(eng, s, UNITS[name] + k + 1, per)

        def b3(ap, n):
            return ap.unsqueeze(2).to_broadcast([ap.shape[0], ap.shape[1], n])

        def b3m(ap, n):
            return ap.unsqueeze(1).to_broadcast([ap.shape[0], n, ap.shape[1]])

        @block.sync
        def _(sp):
            sp.dma_start(CST[:], cst).then_inc(sem("x_loaded"), 16)
            xv = x[0].rearrange("(n p) d -> p n d", p=P)
            for n in range(NT):
                sp.dma_start(XTOK[:, n, :], xv[:, n, :]).then_inc(sem("x_loaded"), 16)
            rows = [(0, norm_g, 0), (0, conv_q_w, 8), (0, conv_k_w, 40), (0, conv_q_b, 72),
                    (0, conv_k_b, 80), (0, mh_norm_g, 88), (0, final_norm_g, 96),
                    (1, norm_g_2, 0), (1, conv_w_2, 24),
                    (2, ada_b_2, 0), (2, dn_norm_g_2, 72), (2, pool_scale_2, 73), (2, final_g_2, 77), (2, c_2, 85)]
            for tile, w, r in rows:
                nd = len(w.shape)
                flat = w if nd == 1 else w.rearrange("a b -> (a b)") if nd == 2 else w.rearrange("a b c -> (a b c)")
                n = flat.shape[0] // P
                sp.dma_start(PROW[r:r + n, tile, :], flat.rearrange("(r q) -> r q", q=P))\
                  .then_inc(sem("rows_loaded"), 16)
            for s, pos in enumerate((cmp_pos_k, cmp_pos_v)):
                for half in range(2):
                    sp.dma_start(PROW[32 * s:32 * s + 32, 3, 64 * half:64 * half + 64], pos[0])\
                      .then_inc(sem("rows_loaded"), 16)
            sp.wait_ge(sem("params_set"), 3)
            for w, r, m, c in ((b_igate, 0, 4, SMB), (b_fgate, 32, 4, SMB), (b_nsa_gate, 64, 24, SMB),
                               (a_log_2, 0, 8, ALOG), (dt_bias_2, 0, 8, DTB)):
                sp.dma_start(PAR[r:r + m, c:c + 1], w[0].rearrange("(p a) -> p a", a=1))\
                  .then_inc(sem("biases_loaded"), 16)
            def load_attention():
                sp.wait_ge(sem("ada_used"), 8 * N_MOD)
                sp.dma_start(POSI[:], positions.to_broadcast([P, T])).then_inc(sem("side_loaded"), 16)
                sp.wait_ge(sem("mht_ready"), 8)
                for s, w1 in enumerate((cmp_w1_k, cmp_w1_v)):
                    if s:
                        sp.wait_ge(sem("cmp_hid_sum"), 1)
                    for half in range(2):
                        sp.dma_start(W1[64 * half:64 * half + 64], w1[0].rearrange("(l d) h -> d l h", d=DK))\
                          .then_inc(sem("w1_loaded"), 16)
                    if s == 0:
                        sp.wait_ge(sem("roped"), 6)
                        for q, w2 in enumerate((cmp_w2_k, cmp_w2_v)):
                            for half in range(2):
                                sp.dma_start(W2[:, q, 64 * half:64 * half + 64], w2[0])\
                                  .then_inc(sem("w2_loaded"), 16)

            for name, iters, body, _ in STAGES:
                if name == "merge2":
                    sp.wait_ge(sem("beta_bcast"), 2 * NT)
                    sp.dma_start(PLW[:], pool_w_2[0].rearrange("g c d -> c g d")).then_inc(sem("side_loaded"), 16)
                if iters == 1:
                    for k, desc in enumerate(body(0)):
                        if name == "oz1" and k == 4:
                            load_attention()
                        load_chunk(sp, Place(name, 0), k, desc)
                else:
                    with sp.Fori(0, iters) as i:
                        for k, desc in enumerate(body(i)):
                            load_chunk(sp, Place(name, i), k, desc)
            ov = out[0].rearrange("(n p) d -> p n d", p=P)
            for n in range(NT):
                sp.wait_ge(sem("out_tokens"), 2 * n + 2)
                sp.dma_start(ov[:, n, :], YTOK2[:, n, :]).then_inc(sem("stored"), 16)
            sp.wait_ge(sem("stored"), 16 * NT)

        @block.gpsimd
        def _(pool):
            pool.memset(PAR[:, SMB:SMB + 3], 0.0).then_inc(sem("params_set"), 1)
            pool.memset(PAR[:, HALF:HALF + 8], -0.5).then_inc(sem("params_set"), 1)
            pool.memset(PAR[:, RCOL:RCOL + 8], 1.0).then_inc(sem("params_set"), 1)

            pool.wait_ge(sem("x_loaded"), 16 * (NT + 1))
            for k in range(8):
                if k >= 4:
                    pool.wait_ge(sem("ada_used"), k - 3)
                pool.dma_start(ADAW[:, k % 4, :], ada_w_2[0, k * P:(k + 1) * P, 0:D]).then_inc(sem(f"ada_loaded{k % 4}"), 16)
            with pool.Fori(0, N_MOD - 1) as g:
                for k in range(8):
                    pool.wait_ge(sem("ada_used"), g * 8 + (8 + k - 3))
                    pool.dma_start(ADAW[:, k % 4, :], ada_w_2[0, k * P:(k + 1) * P, ds(g * D + D, D)])\
                        .then_inc(sem(f"ada_loaded{k % 4}"), 16)
            pool.wait_ge(h_ready, 8)
            pool.wait_ge(sem("mod_sum"), 7)
            pool.memset(VTOK[:, :, :, MD:MD + 1], 1.0).then_inc(sem("v_ones"), 1)
            pool.memset(SM[:], 0.0).then_inc(sem("row_zero"), 1)
            pool.wait_ge(sem("mod_sum"), 9)
            pool.memset(ROW[3][0:8, :], 0.0).then_inc(sem("row_zero"), 1)
            pool.wait_ge(sem("mht_ready"), 8)
            pool.memset(BLK[:], 0.0).then_inc(sem("hid_zero"), 1)
            pool.wait_ge(sem("rope_tables"), 1)
            for t in range(6):
                src = QRAW[:, t, :] if t < 4 else KVR[:, t - 2, :]
                dst = QROPE[:, t, :] if t < 4 else KR[:, t - 4, :]
                pool.tensor_tensor(dst, src, RCOS[:], ALU.mult).then_inc(sem("rope_cos_part"), 1)
            pool.wait_ge(sem("roped"), 6)
            pool.memset(HID[:], 0.0).then_inc(sem("hid_zero"), 1)
            pool.memset(VCB[:], 0.0).then_inc(sem("hid_zero"), 1)
            pool.memset(col(KCT, 128), 0.0).then_inc(sem("hid_zero"), 1)
            steps = Count(pool, sem("pool_step"))

            def step(ins):
                steps.mark(ins)
                steps.wait()

            def pool_windows(groups):
                for g in groups:
                    pool.wait_ge(sem("xp_stored"), g + 1)
                    step(pool.tensor_copy(by_chunk(PLS[:, 0, :]), waiting(g)))
                    cur = 0
                    for lv in range(g + 1):
                        b = 1 << lv
                        step(pool.tensor_copy(PLS[:, 1 - cur, 0:b], PLS[:, cur, 0:b]))
                        step(pool.tensor_tensor(PLS[:, 1 - cur, b:T], PLS[:, cur, b:T], PLS[:, cur, 0:T - b], ALU.add))
                        cur = 1 - cur
                    s = PLS[:, cur, :]
                    step(pool.tensor_tensor(s[:, 0:16], s[:, 0:16], CST[:, K_FIX + 16 * g:K_FIX + 16 * g + 16], ALU.mult))
                    step(pool.tensor_scalar(s, s, 1.0 / (2 << g), None, ALU.mult))
                    pool.tensor_tensor(waiting(g), by_chunk(s), waiting(g), ALU.subtract)\
                        .then_inc(sem("pooled"), 1)

            for h in range(16):
                pool.wait_ge(sem("conv_ready"), 16 + h + 1)
                pool.tensor_tensor(NRM[:, h, :], QKV[:, h, :], QKV[:, h, :], ALU.mult).then_inc(sem("qk_squares"), 1)
            pool.memset(SM[:], 0.0).then_inc(sem("row_zero"), 1)
            pool.memset(EROW[2][0:8, :], 1.0).then_inc(sem("row_zero"), 1)
            pool.wait_ge(sem("row_zero"), 4)
            pool.memset(EROW[2][0:8, :].rearrange("p (c t) -> p c t", t=P)[:, :, 0:1], 0.0).then_inc(sem("row_zero"), 1)
            for c in range(NT):
                for lv in range(1, LEVELS):
                    for a in range(2):
                        pool.wait_ge(sem("delta_a"), 2 * c + a + 1)
                        if lv > 1:
                            pool.wait_ge(sem("delta_x_sum"), ((c * 6 + lv - 2) * 2 + a) + 1)
                        elif c:
                            pool.wait_ge(sem("state_sum"), 2 * c)
                        pool.tensor_tensor(ML[:, 4 * a:4 * a + 4, :], MT[:, 4 * a:4 * a + 4, :],
                                           b3m(CST[:, K_LV + lv * P:K_LV + (lv + 1) * P], 4), ALU.mult)\
                            .then_inc(sem("level_block"), 1)
                pool_windows(((), (0, 1), (2,), (3,))[c])
                pool.wait_ge(sem("o_var"), c + 1)
                pool.tensor_tensor(PAR[:, RSO:RSO + 8], PAR[:, RSO:RSO + 8], PAR[:, HALF:HALF + 8], ALU.pow)\
                    .then_inc(sem("o_rstd"), 1)

        @block.tensor
        def _(pe):
            pe.wait_ge(sem("x_loaded"), 16 * (NT + 1))
            for k in range(KD):
                if k >= 3:
                    pe.wait_ge(x_ready, k - 2)
                for n in range(NT):
                    mm = pe.transpose(PS[:, 5 + k % 3, n * P:n * P + P], XTOK[:, n, k * P:k * P + P], ID)
                mm.then_inc(sem("x_T"), 1)
            pe.wait_ge(sem("rows_loaded"), 16 * 18)
            for tile, n, to in ((0, N1, 0), (1, N2, 128), (2, N3, 256), (3, 64, 384)):
                mm = pe.transpose(PS[:, 4, to:to + n], PROW[0:n, tile, :], ID[0:n, 0:n])
            mm.then_inc(sem("params_T"), 1)

            def rms_sum(r):
                for k in range(KD):
                    pe.wait_ge(sem("squares_ready"), 8 * r + k + 1)
                    if r == 0 and k == 0:
                        pe.wait_ge(sem("params_ready"), 1)
                    sums = 2 if r == DOUBLE else 1
                    for n in range(sums * NT):
                        slot = (sums * k + n // NT) % 4
                        mm = pe.matmul(PS[:, 4, n:n + 1], SQ[:, slot, n % NT * P:n % NT * P + P], ONES[:, 0:1],
                                       start=(k == 0 and n == 0), stop=(k == KD - 1 and n == sums * NT - 1))
                    mm.then_inc(sem("square_sum"), 1)
                pe.wait_ge(sem("rms_diagonal"), r + 1)
                for n in range(NT):
                    mm = pe.matmul(PS[:, 5, n * P:n * P + P], ONES, RDIAG[:, n, :], start=True, stop=True)
                mm.then_inc(sem("rms_spread"), 1)
                if r == DOUBLE:
                    for n in range(NT):
                        mm = pe.matmul(PS[:, 6, n * P:n * P + P], ONES, RDIAG2[:, n, :], start=True, stop=True)
                    mm.then_inc(sem("x_T"), 1)

            def mods(name, k, pl):
                g = MOD_AT.get((name, k))
                if g is None:
                    return
                pl.at_least(pe, sem("ada_used"), 8 * (g + 1), 8)
                for j in range(8):
                    o = PS[:, 7, 8 * g + j:8 * g + j + 1] if pl.iters == 1 else PS[:, 7, ds(pl.i * 8 + (8 * g + j), 1)]
                    mm = pe.matmul(o, ADAC[SUM_AT[g]][:, j * P:j * P + P], ONES[:, 0:1], start=True, stop=True)
                mm.then_inc(sem("mod_sum"), 1)

            def counted(s, base):
                return lambda kk: pe.wait_ge(s, base + kk + 1)

            def tile_stage(name, rhi, rlo, kts=8, ready=None, first=0):
                def body(pl):
                    for k in range(first, pl.nb):
                        pe_tile(pe, pl, k, k, kts, rhi, rlo, act_ready=ready if k == 0 else None)
                        mods(name, k, pl)
                stage(name, body)

            def stage(name, body):
                if INFO[name]["iters"] == 1:
                    body(Place(name, 0))
                else:
                    with pe.Fori(0, INFO[name]["iters"]) as i:
                        body(Place(name, i))

            def token_stage(name, halves, kts, width):
                pl = Place(name, 0)
                per = 8 // kts
                for h in range(halves):
                    for c in range(per):
                        k = per * h + c
                        n = pl.chunk + k
                        pe.wait_ge(w_lo, n + 1)
                        if h == 0:
                            pe.wait_ge(h_ready, kts * (c + 1))
                        for t in range(NT):
                            bank = pe_open(pe, pl, NT * h + t) if c == 0 else PS[:, pl.bank(NT * h + t), :]
                            for kk in range(kts):
                                w = slice(kk * width, kk * width + width)
                                kt, tok = kts * c + kk, slice(t * P, t * P + P)
                                o = bank[:, 0:width]
                                pe.matmul(o, HHI[:, kt, tok], WHI[:, n % 4, w], start=(kt == 0), stop=False)
                                pe.matmul(o, HHI[:, kt, tok], WLO[:, n % 4, w], start=False, stop=False)
                                mm = pe.matmul(o, HLO[:, kt, tok], WHI[:, n % 4, w], start=False, stop=(kt == 7))
                        mm.then_inc(chunk_done, 1)
                        mods(name, k, pl)

            def merge_stage(name, ka, ahi, alo, kb, bhi, blo):
                def body(pl):
                    for f in range(2):
                        for q, (kts, rh, rl) in enumerate(((8, HHI, HLO), (8, HHI, HLO), (ka, ahi, alo), (kb, bhi, blo))):
                            if q == 2 and f == 0:
                                pe.wait_ge(u_lo, UNITS[name])
                            pe_tile(pe, pl, 4 * f + q, 4 * f + q, kts, rh, rl)
                stage(name, body)

            def ffn_out(name):
                def body(pl):
                    for f in range(4):
                        for c, (k0, kn) in enumerate(((0, 8), (8, 8), (16, 6))):
                            pe_tile(pe, pl, 3 * f + c, f, kn, HIDHI, HIDLO, k0, c == 0, c == 2,
                                    counted(u_lo, UNITS[name[:-3] + "in"] + k0) if f == 0 else None)
                stage(name, body)

            def quarter(pl, k, q):
                n = pl.chunk + k
                if q == 0:
                    pe_open(pe, pl, k)
                    pe.wait_ge(w_lo, n + 1)
                for kk in (2 * q, 2 * q + 1):
                    a = slice(kk * P, kk * P + P)
                    mm = mm3(pe, PS[:, pl.bank(k), :], WHI[:, n % 4, a], WLO[:, n % 4, a], HHI[:, kk, :], HLO[:, kk, :],
                             kk == 0, kk == 7)
                if q == 3:
                    mm.then_inc(chunk_done, 1)

            def side(m):
                pl, k = side_place(m // 4)
                quarter(pl, k, m % 4)

            def oz(m):
                quarter(Place("oz1", 0), m // 4, m % 4)

            rms_sum(0)
            token_stage("v1", 2, 2, 512)
            tile_stage("conv1", HHI, HLO)
            tile_stage("small1", HHI, HLO)
            tile_stage("nsa1", HHI, HLO)
            token_stage("vsw1", 1, 4, 256)

            for m in range(8):
                oz(m)
                if m == 3:
                    mods("last", 0, Place("vsw1", 0))
            pe.wait_ge(sem("packed_gates"), 1)
            pe.wait_ge(sem("packed_um"), 1)
            for n in range(NT):
                mm = pe.transpose(PS[:, 4, n * P:n * P + P], SM[:, n * P:n * P + P], ID)
            mm.then_inc(sem("packed_T"), 1)
            pe.wait_ge(sem("conv_ready"), 16)
            def spread_m(h):
                if h == 0:
                    pe.wait_ge(sem("packed_cols"), 1)
                else:
                    pe.wait_ge(sem("m_copied"), h)
                pe.matmul(PS[:, 4, :], ID[0:4, h:h + 1].to_broadcast([4, P]), ROW[4][0:4, :], start=True, stop=True)\
                  .then_inc(sem("m_bcast"), 1)

            spread_m(0)
            for h in range(MH):
                for j in range(NT):
                    if 4 * h + j >= 2:
                        pe.wait_ge(sem("p_ready"), 4 * h + j - 1)
                    for e in range(2):
                        mm = pe.matmul(PS[:, 5 + j % 2, 0:T - j * P], QK1[:, 8 + 2 * h + e, j * P:j * P + P],
                                       QK1[:, 2 * h + e, j * P:T], start=(e == 0), stop=(e == 1))
                    mm.then_inc(sem("s_ready"), 1)
                if h < MH - 1:
                    spread_m(h + 1)
                for i in range(NT):
                    if h == 0 and i == 0:
                        pe.wait_ge(sem("v_ones"), 1)
                        pe.wait_ge(sem("mod_taken"), 1)
                    if 4 * h + i >= 2:
                        pe.wait_ge(sem("pv_used"), 4 * h + i - 1)
                    for j in range(i + 1):
                        pe.wait_ge(sem("p_ready"), 4 * h + j + 1)
                        o = (0, 512, 896, 1152)[j] + (i - j) * P
                        mm = pe.matmul(PS[:, PV_BANK[i % 2], 0:MD + 1], DP[:, h % 2, o:o + P],
                                       VTOK[:, j, h, :], start=(j == 0), stop=(j == i))
                    mm.then_inc(sem("pv_ready"), 1)
            for f in range(8):
                pe.wait_ge(sem("h_normed"), 4 * (f // 2) + 4)
                if f >= 4:
                    pe.wait_ge(sem("mht_ready"), f - 3)
                for n in range(NT):
                    mm = pe.transpose(PS[:, 4 + f % 4, n * P:n * P + P],
                                      MTOK[:, f // 2, n, (f % 2) * P:(f % 2) * P + P], ID)
                mm.then_inc(sem("h_T"), 1)
            pe.wait_ge(sem("mht_ready"), 8)
            for t in range(6):
                if t >= 4:
                    pe.wait_ge(sem("roped"), t - 3)
                if t == 4:
                    oz(8)
                    oz(9)
                pe.matmul(PS[:, 4 + t % 4, :], CST[:, K_ROPE:K_ROPE + P], QRAW[:, t, :] if t < 4 else KVR[:, t - 2, :],
                          start=True, stop=True).then_inc(sem("rope_perm"), 1)
            for m in range(4):
                oz(10 + m)
            for s in range(2):
                pe.wait_ge(sem("roped"), 5 + s)
                pe.matmul(PS[:, 6 + s, :], CST[:, K_SWAP:K_SWAP + P], KR[:, s, :], start=True, stop=True)\
                  .then_inc(sem("k_swap_sum"), 1)
            for s in range(2):
                pe.wait_ge(sem("w1_loaded"), 32 * (s + 1))
                pe.wait_ge(sem("cmp_blocks"), s + 1)
                if s:
                    pe.wait_ge(sem("hid_ready"), 1)
                for lt in range(CB):
                    mm = pe.matmul(PS[:, 4, 0:NG * NC], W1[:, lt, :], BLK[:, lt].rearrange("p g n -> p (g n)"),
                                   start=(lt == 0), stop=(lt == CB - 1))
                mm.then_inc(sem("cmp_hid_sum"), 1)
                pe.wait_ge(sem("hid_ready"), s + 1)
                pe.wait_ge(sem("w2_loaded"), 64)
                if s == 0:
                    pe.wait_ge(sem("k_swapped"), 2)
                    for g in range(2):
                        mm = pe.matmul(PS[:, 6, 32 * g:32 * g + 32], W2[:, 0, :], HID[:, 2 * g, :], start=True, stop=True)
                else:
                    mm = pe.matmul(PS[:, 7, 0:DK], HID[:].rearrange("p q n -> p (q n)"), W2[:, 1, 0:DK],
                                   start=True, stop=True)
                mm.then_inc(sem("cmp_kv_sum"), 1)
            pe.wait_ge(sem("cmp_kv_ready"), 6)
            for i in range(NT):
                if i >= 2:
                    pe.wait_ge(sem("cmp_scored"), 2 * (i - 1))
                for q in range(4):
                    mm = pe.matmul(PS[:, 4 + i % 2, 64 * q:64 * q + 64], QRAW[:, q, i * P:i * P + P],
                                   col(KCT + 64 * (q // 2), 64), start=True, stop=True)
                mm.then_inc(sem("cmp_s_sum"), 1)
            oz(14)
            oz(15)
            pe.wait_ge(sem("cmp_probs"), 1)
            for i in range(NT):
                for p in range(2):
                    o = (2 * (i % 2) + p) * P
                    mm = pe.transpose(PS[:, 4 + i // 2, o:o + P], SC[:, i, p].rearrange("p q n -> p (q n)"), ID)
            mm.then_inc(sem("cmp_probs_T"), 1)
            for i in range(NT):
                pe.wait_ge(sem("cmp_pt_ready"), i // 2 + 1)
                if i >= 2:
                    pe.wait_ge(sem("y_cmp"), 2 * (i - 1))
                for p in range(2):
                    mm = pe.matmul(PS[:, 6 + i % 2, 256 * p:256 * p + 256], PCT[:, i, p, :],
                                   VCB[:].rearrange("p q d -> p (q d)"), start=True, stop=True)
                mm.then_inc(sem("cmp_o_sum"), 1)
            pe.wait_ge(sem("y_cmp"), 8)
            units = [(i, g, b, hh) for i in range(NT) for g in range(NG) for b in range(2) for hh in range(4)]

            def score(u):
                i, g, b, hh = units[u]
                par = hh % 2
                r = slice(64 * par, 64 * par + 64)
                if u >= 2:
                    pe.wait_ge(sem("exp_done"), u - 1)
                k = KR[r, b + (0 if par == g else 2), 0:(i + 1) * P]
                pe.matmul(PS[:, 4 + par, 0:(i + 1) * P], QROPE[r, 2 * g + hh // 2, i * P:i * P + P], k,
                          start=True, stop=True).then_inc(sem("nsa_s"), 1)

            def turn(u):
                i = units[u][0]
                pe.wait_ge(sem("exp_done"), u + 1)
                if u >= 1:
                    pe.wait_ge(sem("pt_ready"), u)
                for j in range(i + 1):
                    mm = pe.transpose(PS[:, 6, j * P:j * P + P], PR[:, u % 2, j * P:j * P + P], ID)
                mm.then_inc(sem("probs_T"), 1)

            def apply_v(u):
                i, g, b, hh = units[u]
                pe.wait_ge(sem("pt_ready"), u + 1)
                if hh == 0 and u >= 4:
                    pe.wait_ge(sem("y_added"), u // 4)
                o = 256 * (u // 4 % 2) + 64 * hh
                for j in range(i + 1):
                    mm = pe.matmul(PS[:, 7, o:o + DK], PT[:, u % 2, j * P:j * P + P], VSW[:, j, b, 64 * g:64 * g + 64],
                                   start=(j == 0), stop=(j == i))
                mm.then_inc(sem("nsa_o"), 1)

            for u in range(len(units) + 2):
                if u < len(units):
                    score(u)
                if 8 <= u < 56:
                    oz(u + 8)
                elif 56 <= u < 64:
                    quarter(Place("nz1", 0), (u - 56) // 4, u % 4)
                if 1 <= u <= len(units):
                    turn(u - 1)
                if u >= 2:
                    apply_v(u - 2)
            pe.wait_ge(sem("y_added"), 16)
            for f in range(4):
                for n in range(NT):
                    mm = pe.transpose(PS[:, 4 + f, n * P:n * P + P], YTOK[:, n, f].rearrange("p a d -> p (a d)"), ID)
                mm.then_inc(sem("y_T"), 1)
            tile_stage("nz1", HHI, HLO, first=2)
            merge_stage("merge1", 8, YAHI, YALO, 4, YBHI, YBLO)
            tile_stage("out1", MGHI, MGLO, ready=counted(u_lo, UNITS["merge1"]))

            rms_sum(1)
            tile_stage("ffn1_in", HHI, HLO, ready=counted(h_ready, 8))
            ffn_out("ffn1_out")
            rms_sum(2)
            tile_stage("conv2", HHI, HLO, ready=counted(h_ready, 16))
            tile_stage("small2", HHI, HLO)

            for h in range(16):
                pe.wait_ge(sem("qk_squares"), h + 1)
                pe.matmul(PS[0:16, 5, :], CST[:, K_SEL + 15 - h:K_SEL + 31 - h], NRM[:, h, :], start=(h == 0),
                          stop=(h == 15)).then_inc(sem("norm_sum"), 1)
                if h % 2:
                    side(h // 2)
            for h in range(16):
                if h == 0:
                    pe.wait_ge(sem("lengths"), 1)
                if h >= 2:
                    pe.wait_ge(sem("qk_normed"), h - 1)
                pe.matmul(PS[:, 5 + h % 2, :], ID[0:16, h:h + 1].to_broadcast([16, P]), NRT[0:16, :], start=True,
                          stop=True).then_inc(sem("length_spread"), 1)
                if h % 4 == 3:
                    side(8 + h // 4)
            pe.wait_ge(sem("packed2"), 2)
            for n in range(NT):
                mm = pe.transpose(PS[:, 7, n * P:n * P + P], SM[:, n * P:n * P + P], ID)
            mm.then_inc(sem("packed_T"), 1)
            pe.wait_ge(sem("qk_normed"), 16)
            pe.wait_ge(sem("delta_cols"), 1)

            def heads(a):
                return range(4 * a, 4 * a + 4)

            def outputs_back(c, a):
                pe.wait_ge(sem("o_normed"), c + 1)
                for h in heads(a):
                    mm = pe.transpose(PS[:, 5 + 2 * a, (h % 4) * P:(h % 4) * P + P], OO[:, h, :], ID)
                mm.then_inc(sem("o_T"), 1)

            for c in range(NT):
                tok = slice(c * P, c * P + P)
                k2 = 2 * c
                for a in range(2):
                    B0, B1 = 4 + 2 * a, 5 + 2 * a
                    if c:
                        pe.wait_ge(sem("state_new"), k2 - 1 + a)
                    for h in heads(a):
                        mm = pe.matmul(PS[:, B0, (h % 4) * P:(h % 4) * P + P], ID[0:8, h:h + 1].to_broadcast([8, P]),
                                       EROW[0][0:8, tok], start=True, stop=True)
                    mm.then_inc(sem("gc_bcast"), 1)
                    for h in heads(a):
                        mm = pe.matmul(PS[:, B1, (h % 4) * P:(h % 4) * P + P], QKV[:, 8 + h, tok], QKV[:, 8 + h, tok],
                                       start=True, stop=True)
                    mm.then_inc(sem("kk_sum"), 1)
                for a in range(2):
                    B0, B1 = 4 + 2 * a, 5 + 2 * a
                    pe.wait_ge(sem("decay_arg"), k2 + a + 1)
                    for h in heads(a):
                        mm = pe.matmul(PS[:, B0, (h % 4) * P:(h % 4) * P + P], ID[0:8, h:h + 1].to_broadcast([8, P]),
                                       EROW[1][0:8, tok], start=True, stop=True)
                    mm.then_inc(sem("beta_bcast"), 1)
                    pe.wait_ge(sem("kk_decayed"), k2 + a + 1)
                    for h in heads(a):
                        mm = pe.matmul(PS[:, B1, (h % 4) * P:(h % 4) * P + P], QKV[:, 8 + h, tok], QKV[:, h, tok],
                                       start=True, stop=True)
                    mm.then_inc(sem("qk_sum"), 1)
                for lv in range(LEVELS):
                    beside = 1 <= lv <= (5 if c == 0 else 4)
                    m0 = 12 + 4 * (lv - 1) if c == 0 else 32 + 16 * (c - 1) + 4 * (lv - 1)
                    for a in range(2):
                        B0, B1 = 4 + 2 * a, 5 + 2 * a
                        n = (c * 6 + lv - 1) * 2 + a
                        m = (c * 6 + lv) * 2 + a
                        if beside:
                            side(m0 + a)
                        if lv == 0:
                            pe.wait_ge(sem("qk_decayed"), k2 + a + 1)
                            if c:
                                outputs_back(c - 1, a)
                        else:
                            pe.wait_ge(sem("level_block"), n + 1)
                            pe.wait_ge(sem("inv_ready"), m - 2 + 1)
                            for h in heads(a):
                                mm = pe.matmul(PS[:, B0, (h % 4) * P:(h % 4) * P + P], ML[:, h, :], TI[:, h, :],
                                               start=True, stop=True)
                            mm.then_inc(sem("delta_x_sum"), 1)
                    for a in range(2):
                        B0, B1 = 4 + 2 * a, 5 + 2 * a
                        n = (c * 6 + lv - 1) * 2 + a
                        if beside and a == 0:
                            side(m0 + 2)
                        if lv:
                            pe.wait_ge(sem("delta_x"), n + 1)
                            if c and lv == 1:
                                pe.wait_ge(sem("o_T_taken"), 2 * (c - 1) + a + 1)
                            for h in heads(a):
                                mm = pe.matmul(PS[:, B1, (h % 4) * P:(h % 4) * P + P], XX[:, h, :], TT[:, h, :],
                                               start=True, stop=True)
                            mm.then_inc(sem("inv_step"), 1)
                    for a in range(2):
                        B0 = 4 + 2 * a
                        if beside and a == 0:
                            side(m0 + 3)
                        if lv < LEVELS - 1:
                            pe.wait_ge(sem("inv_T_ready"), (c * LEVELS + lv) * 2 + a + 1)
                            for h in heads(a):
                                mm = pe.transpose(PS[:, B0, (h % 4) * P:(h % 4) * P + P], TT[:, h, :], ID)
                            mm.then_inc(sem("inv_back"), 1)
                for a in range(2):
                    B0, B1 = 4 + 2 * a, 5 + 2 * a
                    if c == 0:
                        pe.wait_ge(sem("conv_ready"), 16 + 20 + 4 * a)
                    for h in heads(a):
                        mm = pe.transpose(PS[:, B0, (h % 4) * P:(h % 4) * P + P], QKV[:, 16 + h, tok], ID)
                    mm.then_inc(sem("v_T"), 1)
                    pe.wait_ge(sem("inv_T_ready"), (c * LEVELS + LEVELS - 1) * 2 + a + 1)
                    if c:
                        for h in heads(a):
                            mm = pe.matmul(PS[:, B1, (h % 4) * P:(h % 4) * P + P], QKV[:, 8 + h, tok], SS[:, h, :],
                                           start=True, stop=True)
                        mm.then_inc(sem("ks_sum"), 1)
                for a in range(2):
                    B0, B1 = 4 + 2 * a, 5 + 2 * a
                    pe.wait_ge(sem("rhs_ready"), k2 + a + 1)
                    for h in heads(a):
                        mm = pe.matmul(PS[:, B0, (h % 4) * P:(h % 4) * P + P], TT[:, h, :], RV[:, h, :],
                                       start=True, stop=True)
                    mm.then_inc(sem("v_new_sum"), 1)
                    if c < NT - 1:
                        for h in heads(a):
                            mm = pe.transpose(PS[:, B1, (h % 4) * P:(h % 4) * P + P], QKV[:, 8 + h, tok], ID)
                        mm.then_inc(sem("k_T"), 1)
                for a in range(2):
                    B0, B1 = 4 + 2 * a, 5 + 2 * a
                    pe.wait_ge(sem("v_new"), k2 + a + 1)
                    if c < NT - 1:
                        pe.wait_ge(sem("k_dec"), k2 + a + 1)
                    if c:
                        for h in heads(a):
                            mm = pe.matmul(PS[:, B0, (h % 4) * P:(h % 4) * P + P], QKV[:, h, tok], SS[:, h, :],
                                           start=True, stop=True)
                        mm.then_inc(sem("qs_sum"), 1)
                    for h in heads(a):
                        mm = pe.matmul(PS[:, B1, (h % 4) * P:(h % 4) * P + P], QKM[:, h, :], VN[:, h, :],
                                       start=True, stop=True)
                    mm.then_inc(sem("intra_sum"), 1)
                for a in range(2 if c < NT - 1 else 0):
                    B0, B1 = 4 + 2 * a, 5 + 2 * a
                    if c:
                        pe.wait_ge(sem("o_inter"), k2 - 2 + a + 1)
                    for h in heads(a):
                        mm = pe.matmul(PS[:, B0, (h % 4) * P:(h % 4) * P + P], KDT[:, h, :], VN[:, h, :],
                                       start=True, stop=True)
                    mm.then_inc(sem("state_sum"), 1)
            for a in range(2):
                outputs_back(NT - 1, a)
            for g in range(4):
                pe.wait_ge(sem("pooled"), g + 1)
                if g == 0:
                    pe.wait_ge(sem("side_loaded"), 32)
                    pe.wait_ge(sem("o_T_taken"), 8)
                pe.matmul(PS[:, 4 + g, :], PLW[:, g, :], waiting(g), start=True, stop=True).then_inc(sem("pool_sum"), 1)
            merge_stage("merge2", 4, PLHI, PLLO, 8, Y2HI, Y2LO)
            tile_stage("out2", M2HI, M2LO, ready=counted(u_lo, UNITS["merge2"]))
            rms_sum(3)
            tile_stage("ffn2_in", HHI, HLO, ready=counted(h_ready, 24))
            ffn_out("ffn2_out")
            rms_sum(4)
            for n in range(NT):
                for q in range(2):
                    m = 2 * n + q
                    pe.wait_ge(sem("final_x"), 8)
                    if m >= 3:
                        pe.wait_ge(sem("out_tokens"), m - 2)
                    for k in range(4):
                        mm = pe.transpose(PS[:, 5 + m % 3, k * P:k * P + P], XT[:, 4 * q + k, n * P:n * P + P], ID)
                    mm.then_inc(sem("out_T"), 1)

        @block.scalar
        def _(act):
            cnt = Count(act, sem("act_step"))

            def copy(out_, in_, **kw):
                return act.activation(out_, in_, ACT.Copy, **kw)

            def stage(name, body):
                if INFO[name]["iters"] == 1:
                    body(Place(name, 0))
                else:
                    with act.Fori(0, INFO[name]["iters"]) as i:
                        body(Place(name, i))

            act.wait_ge(sem("params_T"), 1)
            act.wait_ge(sem("params_set"), 3)
            cnt.mark(copy(PAR[:, 0:N1], PS[:, 4, 0:N1]))
            cnt.mark(copy(PAR[:, G2:G2 + N2], PS[:, 4, 128:128 + N2]))
            cnt.mark(copy(PAR[:, ADAB:ADAB + N3], PS[:, 4, 256:256 + N3]))
            copy(PAR[:, POST:POST + 64], PS[:, 4, 384:448]).then_inc(sem("params_ready"), 1)
            cnt.wait()
            act.activation(PAR[:, SILC:SILC + 8], PAR[:, CVEC:CVEC + 8], ACT.Silu).then_inc(sem("silu_c"), 1)

            def first_weights():
                for n in range(AHEAD):
                    act.wait_ge(w_loaded[n], 16)
                    act.activation(WHI[:, n, :], RAW[:, n, :], ACT.Copy).then_inc(w_hi, 1)

            def squares(r, between=None):
                ahead = 2 if r == DOUBLE else 4
                for k in range(KD):
                    act.wait_ge(x_ready, NORM_X[r] - 8 + k + 1)
                    if k >= ahead:
                        act.wait_ge(sem("square_sum"), 8 * r + k - ahead + 1)
                    if r == DOUBLE:
                        act.activation(SQ[:, 2 * k % 4, :], XT[:, k, :], ACT.Square)
                        e = act.activation(SQ[:, (2 * k + 1) % 4, :], XT[:, k, :], ACT.Square, scale=col(FNG + k))
                    else:
                        e = act.activation(SQ[:, k % 4, :], XT[:, k, :], ACT.Square)
                    e.then_inc(sem("squares_ready"), 1)
                if between:
                    between()
                act.wait_ge(sem("mean_recip"), r + 1)
                act.activation(col(RCOL, 8), col(RCOL, 8), ACT.Sqrt).then_inc(sem("rms_ready"), 1)

            def norm_hi(r, idx, shift):
                for k in range(KD):
                    act.wait_ge(sem("normed"), 8 * idx + k + 1)
                    kw = {} if shift is None else dict(bias=col(shift + k))
                    act.activation(HHI[:, k, :], SQ[:, k % 4, :], ACT.Identity, **kw).then_inc(sem("h_hi"), 1)

            def conv_stage(name, tile0):
                def body(pl):
                    dst = QK1 if name == "conv1" else QKV

                    def silu(k):
                        pl.at_least(act, sem("conv_taps"), tile0 + k + 1, 8)
                        waited(act, pl)
                        d = dst[:, ds(pl.i * 8 + k, 1), :]
                        act.activation(d, d, ACT.Silu).then_inc(sem("conv_ready"), 1)

                    for k in range(pl.nb):
                        split_hi(act, pl, k + AHEAD)
                        tiles_ready(act, pl, k)
                        waited(act, pl)
                        src = PS[:, pl.bank(k):pl.bank(k) + 1, :]
                        if name == "conv1":
                            kw = dict(scale=PAR[:, ds(pl.i * 32 + (8 + 24 + k), 1)], bias=PAR[:, ds(pl.i * 8 + (CQB + k), 1)])
                        else:
                            kw = dict(scale=PAR[:, ds(pl.i * 8 + (CW2 + 72 + k), 1)])
                        act.activation(dst[:, ds(pl.i * 8 + k, 1), :], src, ACT.Identity, **kw)\
                           .then_inc(sem("conv_base"), 1)
                        if k:
                            silu(k - 1)
                    silu(pl.nb - 1)
                stage(name, body)

            def unit_hi(pl, name, per, k, dst, src):
                at_least_unit(act, product, pl, name, per, k)
                waited(act, pl)
                act.activation(dst, src, ACT.Copy).then_inc(u_hi, 1)

            squares(0, first_weights)
            norm_hi(0, 0, None)
            pl = Place("v1", 0)
            for k in range(8):
                split_hi(act, pl, k + AHEAD)
                if k % 4 == 3:
                    h = k // 4
                    tiles_ready(act, pl, k)
                    for t in range(NT):
                        src = PS[:, pl.bank(t), :].rearrange("p (h d) -> p h d", d=MD)
                        tile_used(copy(VTOK[:, t, 2 * h:2 * h + 2, 0:MD], src), pl, t)
            conv_stage("conv1", 0)
            pl = Place("small1", 0)
            split_hi(act, pl, AHEAD)
            tiles_ready(act, pl, 0)
            act.wait_ge(sem("biases_loaded"), 16 * 5)
            tile_used(act.activation(SMR[:], PS[:, pl.bank(0), :], ACT.Identity, bias=col(SMB)), pl, 0)
            pl = Place("nsa1", 0)
            for k in range(8):
                split_hi(act, pl, k + AHEAD)
                tiles_ready(act, pl, k)
                tile_used(copy(QRAW[:, k, :] if k < 4 else KVR[:, k - 4, :], PS[:, pl.bank(k), :]), pl, k)
            pl = Place("vsw1", 0)
            for k in range(2):
                split_hi(act, pl, k + AHEAD)
            tiles_ready(act, pl, 1)
            act.wait_ge(sem("ada_used"), 8 * N_MOD)
            for t in range(NT):
                tile_used(copy(VSW[:, t].rearrange("p a d -> p (a d)"), PS[:, pl.bank(t), 0:256]), pl, t)

            for k in (2, 3):
                split_hi(act, Place("oz1", 0), k)

            act.wait_ge(bank_free[INFO["small1"]["tile"] % 4], INFO["small1"]["tile"] // 4 + 1)
            cnt.mark(copy(ROW[0][0:4, :], SMR[32:36, :]))
            act.wait_ge(sem("row_zero"), 2)
            act.activation(SM[64:88, :], SMR[64:88, :], ACT.Sigmoid).then_inc(sem("packed_gates"), 1)
            cnt.wait()
            cnt.mark(act.activation(ROW[1][0:4, :], ROW[0][0:4, :], ACT.Abs))
            cnt.wait()
            cnt.mark(act.activation(ROW[1][0:4, :], ROW[1][0:4, :], ACT.Exp, scale=-1.0))
            cnt.wait()
            act.activation(ROW[1][0:4, :], ROW[1][0:4, :], ACT.Ln, bias=1.0).then_inc(sem("log_f_parts"), 1)
            act.wait_ge(sem("packed_T"), 1)
            copy(SMT[:].rearrange("p n c -> p (n c)"), PS[:, 4, :]).then_inc(sem("packed_cols"), 1)
            act.wait_ge(sem("stats_ready"), 1)
            act.activation(col(NE, 16), col(NE, 16), ACT.Exp, scale=-1.0).then_inc(sem("stats_done"), 1)
            def decays(h):
                m, masked = ROW[2 * (h % 2)], ROW[2 * (h % 2) + 1]
                act.wait_ge(sem("m_bcast"), h + 1)
                copy(m[:], PS[:, 4, :]).then_inc(sem("m_copied"), 1)
                act.wait_ge(sem("m_masked"), h + 1)
                for j in range(NT):
                    o = (0, 512, 896, 1152)[j]
                    if h >= 2 and j == 0:
                        act.wait_ge(sem("pv_ready"), 4 * (h - 1))
                    bias = SMT[:, j, h:h + 1]
                    e = act.activation(DP[:, h % 2, o:o + P], masked[:, j * P:j * P + P], ACT.Exp, bias=bias, scale=-1.0)
                    if j < NT - 1:
                        e = act.activation(DP[:, h % 2, o + P:o + T - j * P], m[:, (j + 1) * P:T], ACT.Exp,
                                           bias=bias, scale=-1.0)
                    e.then_inc(sem("decay_ready"), 1)

            decays(0)
            for h in range(MH):
                if h < MH - 1:
                    decays(h + 1)
                for i in range(NT):
                    act.wait_ge(sem("pv_ready"), 4 * h + i + 1)
                    ps = PS[:, PV_BANK[i % 2], :]
                    copy(MTOK[:, h, i, :], ps[:, 0:MD])
                    copy(col(DEN + 4 * h + i), ps[:, MD:MD + 1]).then_inc(sem("pv_used"), 1)
            act.wait_ge(sem("stats_ready"), 2)
            act.activation(col(RST, 16), col(RST, 16), ACT.Sqrt).then_inc(sem("stats_done"), 1)
            for f in range(8):
                act.wait_ge(sem("h_T"), f + 1)
                copy(MHT[:, f, :], PS[:, 4 + f % 4, :], scale=col(MHG + f)).then_inc(sem("mht_ready"), 1)

            act.wait_ge(sem("angles"), 1)
            act.activation(RSIN[:], ANG[:], ACT.Sin)
            act.activation(RTMP[:], ANG[:], ACT.Sin, scale=0.5).then_inc(sem("sines"), 1)
            for s in range(2):
                act.wait_ge(sem("k_swap_sum"), s + 1)
                copy(KR[:, 2 + s, :], PS[:, 6 + s, :]).then_inc(sem("k_swapped"), 1)
            act.wait_ge(sem("hid_zero"), 4)
            for s in range(2):
                act.wait_ge(sem("cmp_hid_sum"), s + 1)
                if s:
                    act.wait_ge(sem("cmp_kv_sum"), 1)
                for q in range(4):
                    e = act.activation(HID[:, q, 0:NC], PS[:, 4, NC * (q // 2):NC * (q // 2) + NC],
                                       ACT.Gelu_apprx_tanh)
                e.then_inc(sem("hid_ready"), 1)
                act.wait_ge(sem("cmp_kv_sum"), s + 1)
                if s == 0:
                    for half in range(2):
                        r = slice(64 * half, 64 * half + 64)
                        copy(PAR[r, KCT:KCT + 128].rearrange("p (g a n) -> p g a n", g=NG, a=2)[:, :, half, :],
                             PS[r, 6, 0:64].rearrange("p (g n) -> p g n", g=NG)).then_inc(sem("cmp_kv_ready"), 1)
                else:
                    for q in range(4):
                        r = slice(32 * q, 32 * q + 32)
                        copy(VCB[r, q, :], PS[r, 7, 0:DK]).then_inc(sem("cmp_kv_ready"), 1)
            act.wait_ge(sem("cmp_shifted"), 1)
            act.activation(SC[:], SC[:], ACT.Exp).then_inc(sem("cmp_exp"), 1)
            act.wait_ge(sem("cmp_probs_T"), 1)
            for i in range(2):
                copy(PCT[:, 2 * i:2 * i + 2].rearrange("p a b n -> p (a b n)"), PS[:, 4 + i, :]).then_inc(sem("cmp_pt_ready"), 1)
            act.wait_ge(sem("y_cmp"), 8)
            units = [(i, g, b, hh) for i in range(NT) for g in range(NG) for b in range(2) for hh in range(4)]

            def side(w):
                pl = Place("oz1", 0)
                if w < 14:
                    split_hi(act, pl, w + 4)
                f = w // 2
                if w % 2 == 0 and w:
                    act.wait_ge(product, UNITS["oz1"] + f)
                    copy(YAHI[:, f - 1, :], OGATE[(f - 1) % 2][:]).then_inc(u_hi, 1)
                if w % 2:
                    tiles_ready(act, pl, w)
                    if f >= 2:
                        act.wait_ge(u_lo, UNITS["oz1"] + f - 1)
                    o = act.activation(OGATE[f % 2][:], PS[:, pl.bank(w - 1), :], ACT.Sigmoid)
                    tile_used(o, pl, w - 1)
                    act.activation(ZGATE[:], PS[:, pl.bank(w), :], ACT.Sigmoid).then_inc(nonlin, 1)

            def turned(u):
                act.wait_ge(sem("probs_T"), u + 1)
                if u >= 2:
                    act.wait_ge(sem("nsa_o"), u - 1)
                n = (units[u][0] + 1) * P
                copy(PT[:, u % 2, 0:n], PS[:, 6, 0:n]).then_inc(sem("pt_ready"), 1)

            for u, (i, g, b, hh) in enumerate(units):
                if hh == 0:
                    side(u // 4)
                act.wait_ge(sem("max_ready"), u + 1)
                if u >= 2:
                    act.wait_ge(sem("probs_T"), u - 1)
                n = (i + 1) * P
                if hh == 0 and u >= 8:
                    act.wait_ge(sem("y_added"), u // 4 - 1)
                act.activation(PR[:, u % 2, 0:n], PS[:, 4 + hh % 2, 0:n], ACT.Exp, bias=col(MX + 4 + u % 4),
                               accum_out=col(SUM + 4 * (u // 4 % 2) + hh)).then_inc(sem("exp_done"), 1)
                if u >= 1:
                    turned(u - 1)
            turned(len(units) - 1)
            side(16)
            for f in range(4):
                act.wait_ge(sem("y_T"), f + 1)
                copy(YT[:, f, :], PS[:, 4 + f, :]).then_inc(sem("yt_ready"), 1)
            pl = Place("nz1", 0)
            for f in range(4):
                split_hi(act, pl, f + AHEAD)
                tiles_ready(act, pl, f)
                if f >= 2:
                    act.wait_ge(u_lo, UNITS["nz1"] + f - 1)
                act.activation(NZS[:, f % 2, :], PS[:, pl.bank(f), :], ACT.Sigmoid).then_inc(nonlin, 1)
                unit_hi(pl, "nz1", 4, f, YBHI[:, f, :], NZS[:, f % 2, :])

            def merge(name, gates, hi):
                def body(pl):
                    for f in range(2):
                        for q in range(2):
                            k = 4 * f + q
                            split_hi(act, pl, k + AHEAD)
                            tiles_ready(act, pl, k)
                            a = act.activation(gates[:, 2 * f + q, :], PS[:, pl.bank(k), :], ACT.Sigmoid)
                            tile_used(a, pl, k)
                        for q in range(2, 4):
                            split_hi(act, pl, 4 * f + q + AHEAD)
                        unit_hi(pl, name, 2, f, hi[:, ds(pl.i * 2 + f, 1), :], gates[:, 2 * f:2 * f + 1, :])
                stage(name, body)

            def splits_only(name):
                def body(pl):
                    for k in range(pl.nb):
                        split_hi(act, pl, k + AHEAD)
                stage(name, body)

            def ffn_in(name):
                def body(pl):
                    for f in range(2):
                        split_hi(act, pl, 2 * f + AHEAD)
                        tiles_ready(act, pl, 2 * f)
                        act.activation(FS[:, f, :], PS[:, pl.bank(2 * f), :], ACT.Silu)\
                           .then_inc(bank_free[pl.bank(2 * f)], 1)
                        split_hi(act, pl, 2 * f + 1 + AHEAD)
                        unit_hi(pl, name, 2, f, HIDHI[:, ds(pl.i * 2 + f, 1), :], FS[:, f:f + 1, :])
                stage(name, body)

            merge("merge1", GT, MGHI)
            splits_only("out1")

            squares(1)
            norm_hi(1, 1, MOD)
            ffn_in("ffn1_in")
            splits_only("ffn1_out")
            squares(2)
            norm_hi(2, 2, MOD + 24)
            conv_stage("conv2", 16)
            def side(n):
                if n < 20:
                    split_hi(act, Place("v2", 0), n + AHEAD)
                if n == 0:
                    return
                pl, k = side_place(n - 1)
                ps = PS[:, pl.bank(k), :]
                if n <= 8:
                    tiles_ready(act, pl, k)
                    act.activation(QKV[:, 16 + k, :], ps, ACT.Identity, scale=col(CW2 + 72 + 16 + k))\
                       .then_inc(sem("conv_base"), 1)
                    for t in {0: (), 7: (6, 7)}.get(k, (k - 1,)):
                        act.wait_ge(sem("conv_taps"), 32 + t + 1)
                        act.activation(QKV[:, 16 + t, :], QKV[:, 16 + t, :], ACT.Silu).then_inc(sem("conv_ready"), 1)
                elif n > 12:
                    tiles_ready(act, pl, k)
                    act.activation(waiting(4 + k), by_chunk(ps), ACT.Sigmoid).then_inc(nonlin, 1)
                else:
                    tiles_ready(act, pl, k)
                    cnt.mark(copy(waiting(k), by_chunk(ps)))
                    cnt.wait()
                    act.sem_inc(bank_free[pl.bank(k)], 1)
                    act.sem_inc(sem("xp_stored"), 1)

            pl = Place("small2", 0)
            split_hi(act, pl, AHEAD)
            tiles_ready(act, pl, 0)
            side(0)
            act.activation(EROW[1][0:8, :], PS[0:8, pl.bank(0), :], ACT.Sigmoid).then_inc(sem("beta_rows"), 1)
            act.activation(EROW[0][0:8, :], PS[32:40, pl.bank(0), :], ACT.Identity, bias=PAR[0:8, DTB:DTB + 1])\
               .then_inc(bank_free[pl.bank(0)], 1)
            act.wait_ge(bank_free[pl.bank(0)], INFO["small2"]["tile"] // 4 + 1)
            cnt.mark(act.activation(LPR[0:8, 0, :], EROW[0][0:8, :], ACT.Abs))
            cnt.wait()
            cnt.mark(act.activation(LPR[0:8, 0, :], LPR[0:8, 0, :], ACT.Exp, scale=-1.0))
            cnt.mark(act.activation(PAR[0:8, ALOG:ALOG + 1], PAR[0:8, ALOG:ALOG + 1], ACT.Exp))
            cnt.wait()
            cnt.mark(act.activation(LPR[0:8, 2, :], LPR[0:8, 0, :], ACT.Identity, bias=1.0))
            cnt.wait()
            act.activation(LPR[0:8, 1, :], LPR[0:8, 2, :], ACT.Ln).then_inc(sem("softplus_parts"), 1)
            side(1)
            act.wait_ge(sem("norm_sum"), 16)
            act.activation(NRT[0:16, :], PS[0:16, 5, :], ACT.Sqrt, bias=EPS).then_inc(sem("norm_root"), 1)
            side(2)
            act.wait_ge(sem("packed_T"), 2)
            cnt.mark(copy(SMT[:].rearrange("p n c -> p (n c)"), PS[:, 7, :]))
            cnt.wait()
            act.activation(col(EG, 32).rearrange("p (c h) -> p c h", h=8), SMT[:, :, 32:40], ACT.Exp)
            cnt.mark(act.activation(col(EKD, 32).rearrange("p (c h) -> p c h", h=8), SMT[:, :, 64:72], ACT.Exp))
            cnt.wait()
            act.activation(col(QEG, 32), col(EG, 32), ACT.Copy, scale=float(128 ** -0.5)).then_inc(sem("delta_cols"), 1)

            def ps4(b):
                return PS[:, b, :].rearrange("p (h n) -> p h n", n=P)

            def outputs_taken(c, a):
                act.wait_ge(sem("o_T"), 2 * c + a + 1)
                act.activation(QKV[:, 16 + 4 * a:20 + 4 * a, c * P:c * P + P], ps4(5 + 2 * a), ACT.Copy,
                               scale=col(DNG)).then_inc(sem("o_T_taken"), 1)

            for c in range(NT):
                k2 = 2 * c
                for a in range(2):
                    h4 = slice(4 * a, 4 * a + 4)
                    act.wait_ge(sem("gc_bcast"), k2 + a + 1)
                    if c:
                        act.wait_ge(sem("state_new"), k2 - 1 + a)
                    act.activation(PAR[:, EGL + 4 * a:EGL + 4 * a + 4].unsqueeze(2), ps4(4 + 2 * a)[:, :, P - 1:P], ACT.Exp)\
                       .then_inc(sem("end_decay"), 1)
                    act.wait_ge(sem("decay_masked"), k2 + a + 1)
                    act.activation(DD[:, h4, :], DD[:, h4, :], ACT.Exp).then_inc(sem("decay_exp"), 1)
                for lv in range(LEVELS):
                    if c and lv == 0:
                        for a in range(2):
                            outputs_taken(c - 1, a)
                    if c == 0 and 1 <= lv <= 6:
                        side(lv + 2)
                    elif c and 1 <= lv <= 5:
                        if lv <= 4 and c + lv > 2:
                            side(8 + 4 * (c - 1) + lv - 1)
                        elif c == 3:
                            side(20)
                    for a in range(2):
                        n = (c * 6 + lv - 1) * 2 + a
                        h4 = slice(4 * a, 4 * a + 4)
                        if lv:
                            act.wait_ge(sem("delta_x_sum"), n + 1)
                            copy(XX[:, h4, :], ps4(4 + 2 * a)).then_inc(sem("delta_x"), 1)
                    for a in range(2):
                        h4 = slice(4 * a, 4 * a + 4)
                        if lv < LEVELS - 1:
                            act.wait_ge(sem("inv_back"), (c * 6 + lv) * 2 + a + 1)
                            copy(TI[:, h4, :], ps4(4 + 2 * a)).then_inc(sem("inv_ready"), 1)
                for a in range(2):
                    h4 = slice(4 * a, 4 * a + 4)
                    act.wait_ge(sem("v_T"), k2 + a + 1)
                    copy(RV[:, h4, :], ps4(4 + 2 * a)).then_inc(sem("v_tokens"), 1)
                for a in range(2):
                    h4 = slice(4 * a, 4 * a + 4)
                    act.wait_ge(sem("v_new_sum"), k2 + a + 1)
                    copy(VN[:, h4, :], ps4(4 + 2 * a)).then_inc(sem("v_new"), 1)
            for a in range(2):
                outputs_taken(NT - 1, a)
            for f in range(8):
                act.wait_ge(product, UNITS["z2"] + f + 1)
                act.activation(by_chunk(Y2HI[:, f, :]), waiting(4 + f), ACT.Copy).then_inc(u_hi, 1)
            for g in range(4):
                act.wait_ge(sem("pool_sum"), g + 1)
                act.activation(PLHI[:, g, :], PS[:, 4 + g, :], ACT.Copy, scale=col(PSC + g)).then_inc(u_hi, 1)
            merge("merge2", GT2, M2HI)
            splits_only("out2")
            squares(3)
            norm_hi(3, 3, MOD + 48)
            ffn_in("ffn2_in")
            for i in range(INFO["ffn2_out"]["iters"]):
                pl = Place("ffn2_out", 0)
                pl.chunk += pl.nb * i
                pl.iters = 1
                for k in range(pl.nb):
                    split_hi(act, pl, k + AHEAD)
            squares(4)
            for m in range(2 * NT):
                act.wait_ge(sem("out_T"), m + 1)
                copy(YTOK2[:, m // 2, (m % 2) * T:(m % 2) * T + T], PS[:, 5 + m % 3, :]).then_inc(sem("out_tokens"), 1)

        @block.vector
        def _(dve):
            cnt = Count(dve, sem("dve_step"))

            def chained(ins):
                cnt.mark(ins)
                cnt.wait()

            def tt(o, a, b, op):
                return dve.tensor_tensor(o, a, b, op)

            def stt(o, a, s, b, op0, op1):
                return dve.scalar_tensor_tensor(o, a, s, b, op0, op1)

            def ts(o, a, s1, s2, op0, op1=None):
                return dve.tensor_scalar(o, a, s1, s2, op0) if op1 is None else dve.tensor_scalar(o, a, s1, s2, op0, op1)

            def stage(name, step, body):
                stage_loop(cnt, name, step, body)

            for k in range(KD):
                dve.wait_ge(sem("x_T"), k + 1)
                dve.tensor_copy(XT[:, k, :], PS[:, 5 + k % 3, :]).then_inc(x_ready, 1)

            def norm_lo(k, idx, shift):
                dve.wait_ge(sem("h_hi"), 8 * idx + k + 1)
                hi = HHI[:, k, :].bitcast(F32)
                if shift is None:
                    ins = tt(HLO[:, k, :], SQ[:, k % 4, :], hi, ALU.subtract)
                else:
                    ins = stt(HLO[:, k, :], SQ[:, k % 4, :], col(shift + k), hi, ALU.add, ALU.subtract)
                ins.then_inc(h_ready, 1)

            def ada(pl, n, a):
                for _ in range(n):
                    pl.at_least(dve, sem(f"ada_loaded{a % 4}"), 16 * (a // 4 + 1), 32)
                    g, kt = a // 8, a % 8
                    acc = ADAC[SUM_AT[g]]
                    if kt == 0:
                        before = [q for q in range(g) if SUM_AT[q] == SUM_AT[g]]
                        if before:
                            pl.at_least(dve, sem("mod_sum"), before[-1] + 1, 2)
                        ins = ts(acc[:], ADAW[:, a % 4, :], col(SILC), None, ALU.mult)
                    else:
                        pl.at_least(dve, sem("ada_used"), a, 8)
                        ins = stt(acc[:], ADAW[:, a % 4, :], col(SILC + kt), acc[:], ALU.mult, ALU.add)
                    ins.then_inc(sem("ada_used"), 1)
                    a += 1
                return a

            def rms(r, coef, dst=None, idx=0, shift=None):
                dve.wait_ge(sem("square_sum"), 8 * r + 8)
                chained(ts(col(RCOL, 4), PS[:, 4, 0:NT], 1.0 / D, EPS, ALU.mult, ALU.add))
                if r == DOUBLE:
                    chained(dve.reciprocal(col(RCOL, 4), col(RCOL, 4)))
                    chained(stt(col(RCOL + 4, 4), PS[:, 4, NT:2 * NT], 1.0 / D, col(RCOL, 4), ALU.mult, ALU.mult))
                    chained(ts(col(RCOL + 4, 4), col(RCOL + 4, 4), EPS, None, ALU.add))
                    dve.reciprocal(col(RCOL + 4, 4), col(RCOL + 4, 4)).then_inc(sem("mean_recip"), 1)
                    dve.wait_ge(sem("rms_ready"), r + 1)
                    chained(tt(col(RCOL + 4, 4), col(RCOL + 4, 4), col(RCOL, 4), ALU.mult))
                    cnt.mark(tt(RDIAG[:], b3m(ID, NT), b3(col(RCOL + 4, 4), P), ALU.mult))
                    tt(RDIAG2[:], b3m(ID, NT), b3(col(RCOL, 4), P), ALU.mult).then_inc(sem("rms_diagonal"), 1)
                else:
                    dve.reciprocal(col(RCOL, 4), col(RCOL, 4)).then_inc(sem("mean_recip"), 1)
                    dve.wait_ge(sem("rms_ready"), r + 1)
                    tt(RDIAG[:], b3m(ID, NT), b3(col(RCOL, 4), P), ALU.mult).then_inc(sem("rms_diagonal"), 1)
                dve.wait_ge(sem("rms_spread"), r + 1)
                for k in range(KD):
                    if dst is not None:
                        stt(dst[:, k, :], XT[:, k, :], col(coef + k), PS[:, 5, :], ALU.mult, ALU.mult)\
                            .then_inc(sem("final_x"), 1)
                        continue
                    if k >= 4:
                        dve.wait_ge(h_ready, 8 * idx + k - 3)
                    stt(SQ[:, k % 4, :], XT[:, k, :], col(coef + k), PS[:, 5, :], ALU.mult, ALU.mult)\
                        .then_inc(sem("normed"), 1)
                    if k:
                        norm_lo(k - 1, idx, shift)
                if dst is None:
                    norm_lo(KD - 1, idx, shift)

            def conv_stage(name, tile0):
                def body(pl):
                    a = ADA0["conv1"]
                    for k in range(pl.nb):
                        split_lo(dve, pl, k + AHEAD)
                        if name == "conv1":
                            a = ada(pl, ADA[name][k], a)
                        pl.at_least(dve, sem("conv_base"), tile0 + k + 1, 8)
                        dst = QK1 if name == "conv1" else QKV
                        for s in range(1, 4):
                            w = (PAR[:, ds(pl.i * 32 + (8 + 8 * (3 - s) + k), 1)] if name == "conv1"
                                 else PAR[:, ds(pl.i * 8 + (CW2 + 24 * (3 - s) + k), 1)])
                            o = dst[:, ds(pl.i * 8 + k, 1), s:T]
                            ins = stt(o, PS[:, pl.bank(k):pl.bank(k) + 1, 0:T - s], w, o, ALU.mult, ALU.add)
                            if s < 3:
                                chained(ins)
                        cnt.mark(ins)
                        cnt.wait()
                        dve.sem_inc(sem("conv_taps"), 1)
                        dve.sem_inc(bank_free[pl.bank(k)], 1)
                stage(name, 8 * 3, body)

            def unit_lo(pl, name, per, k, dst, src, hi):
                at_least_unit(dve, u_hi, pl, name, per, k)
                tt(dst, src, hi.bitcast(F32), ALU.subtract).then_inc(u_lo, 1)

            dve.wait_ge(sem("params_ready"), 1)
            dve.wait_ge(sem("params_set"), 3)
            dve.wait_ge(sem("silu_c"), 1)
            ada(Place("v1", 0), 4, 0)
            for n in range(AHEAD):
                dve.wait_ge(w_hi, n + 1)
                tt(WLO[:, n, :], RAW[:, n, :], WHI[:, n, :].bitcast(F32), ALU.subtract).then_inc(w_lo, 1)
            rms(0, G1, idx=0)
            for name in ("v1", "conv1", "small1", "nsa1", "vsw1"):
                if name == "conv1":
                    conv_stage("conv1", 0)
                    continue
                pl, a = Place(name, 0), ADA0[name]
                for k in range(pl.nb):
                    split_lo(dve, pl, k + AHEAD)
                    a = ada(pl, ADA[name][k], a)
            for k in (2, 3):
                split_lo(dve, Place("oz1", 0), k)

            dve.wait_ge(sem("log_f_parts"), 1)
            dve.wait_ge(sem("row_zero"), 2)
            r0, r1, r2, r3, r4 = (ROW[k][0:4, :] for k in range(5))
            chained(ts(r0, r0, 0.0, None, ALU.min))
            chained(tt(r0, r0, r1, ALU.subtract))
            chained(dve.tensor_tensor_scan(r2, r0, r3, 0.0, ALU.add, ALU.add))
            chained(tt(SM[0:4, :], SMR[0:4, :], r2, ALU.subtract))
            chained(dve.tensor_tensor_scan(r4, SM[0:4, :], r3, 0.0, ALU.max, ALU.add))
            tt(SM[32:36, :], r2, r4, ALU.add).then_inc(sem("packed_um"), 1)
            dve.wait_ge(sem("packed_cols"), 1)
            ts(col(NE, 16).rearrange("p (n h) -> p n h", h=4), SMT[:, :, 32:36], -87.0, None, ALU.max)\
                .then_inc(sem("stats_ready"), 1)
            dve.wait_ge(sem("stats_done"), 1)
            def masked_m(h):
                m, masked = ROW[2 * (h % 2)], ROW[2 * (h % 2) + 1]
                dve.wait_ge(sem("m_copied"), h + 1)
                if h >= 2:
                    dve.wait_ge(sem("decay_ready"), 4 * (h - 1))
                tt(masked[:].rearrange("p (n t) -> p n t", t=P), m[:].rearrange("p (n t) -> p n t", t=P),
                   b3m(CST[:, K_CMT:K_CMT + P], NT), ALU.subtract).then_inc(sem("m_masked"), 1)

            def probs(h):
                for j in range(NT):
                    o, n = (0, 512, 896, 1152)[j], T - j * P
                    dve.wait_ge(sem("decay_ready"), 4 * h + j + 1)
                    dve.wait_ge(sem("s_ready"), 4 * h + j + 1)
                    stt(DP[:, h % 2, o:o + n], PS[:, 5 + j % 2, 0:n], 0.0625, DP[:, h % 2, o:o + n], ALU.mult, ALU.mult)\
                        .then_inc(sem("p_ready"), 1)

            dve.wait_ge(sem("mod_sum"), N_MOD)
            tt(col(MOD, 8 * N_MOD), PS[:, 7, 0:8 * N_MOD], col(ADAB, 8 * N_MOD), ALU.add).then_inc(sem("mod_taken"), 1)
            masked_m(0)
            probs(0)
            for h in range(MH):
                if h < MH - 1:
                    masked_m(h + 1)
                    probs(h + 1)
                dve.wait_ge(sem("pv_used"), 4 * h + 4)
                for i in range(NT):
                    cnt.mark(dve.bn_stats(col(BST + 6 * i, 6), MTOK[:, h, i, :]))
                cnt.wait()
                for i in range(NT):
                    cnt.mark(dve.bn_aggr(col(MVS + 2 * (4 * h + i), 2), col(BST + 6 * i, 6)))
                cnt.wait()
            mv = col(MVS, 32).rearrange("p (n c) -> p n c", c=2)
            den, rec = col(DEN, 16), col(DEN + 16, 16)
            chained(stt(rec.rearrange("p (h n) -> p h n", n=NT), den.rearrange("p (h n) -> p h n", n=NT), -1.0,
                        col(NE, 16).rearrange("p (n h) -> p h n", h=MH), ALU.mult, ALU.max))
            chained(tt(rec, rec, den, ALU.max))
            chained(dve.reciprocal(rec, rec))
            chained(tt(col(RST, 16).unsqueeze(2), mv[:, :, 1:2], rec.unsqueeze(2), ALU.mult))
            chained(tt(col(RST, 16), col(RST, 16), rec, ALU.mult))
            chained(ts(col(RST, 16), col(RST, 16), EPS, None, ALU.add))
            dve.reciprocal(col(RST, 16), col(RST, 16)).then_inc(sem("stats_ready"), 1)
            dve.wait_ge(sem("stats_done"), 2)
            chained(tt(col(RST, 16), col(RST, 16), rec, ALU.mult))
            for h in range(MH):
                for i in range(NT):
                    m = 4 * h + i
                    ts(MTOK[:, h, i, :], MTOK[:, h, i, :], col(MVS + 2 * m), col(RST + m), ALU.subtract, ALU.mult)\
                        .then_inc(sem("h_normed"), 1)

            two_pi = 2 * np.pi
            c1 = float(np.float32(np.round(two_pi * 64) / 64))
            c2 = float(np.float32(np.round((two_pi - c1) * 2.0 ** 16) / 2.0 ** 16))
            c3 = float(np.float32(two_pi - c1 - c2))
            magic = float(1.5 * 2 ** 23)
            dve.wait_ge(sem("side_loaded"), 16)
            chained(dve.tensor_copy(ANG[:], POSI[:]))
            chained(ts(ANG[:], ANG[:], CST[:, K_INV:K_INV + 1], None, ALU.mult))
            chained(ts(TRN[:], ANG[:], 1.0 / two_pi, magic, ALU.mult, ALU.add))
            chained(ts(TRN[:], TRN[:], magic, None, ALU.subtract))
            for c in (c1, c2, c3):
                chained(stt(ANG[:], TRN[:], -c, ANG[:], ALU.mult, ALU.add))
            ts(ANG[:], ANG[:], 3.1415925, -3.1415925, ALU.min, ALU.max).then_inc(sem("angles"), 1)
            dve.wait_ge(sem("sines"), 1)
            chained(tt(RCOS[:], RTMP[:], RTMP[:], ALU.mult))
            ts(RCOS[:], RCOS[:], -2.0, 1.0, ALU.mult, ALU.add).then_inc(sem("rope_tables"), 1)
            for t in range(6):
                dst = QROPE[:, t, :] if t < 4 else KR[:, t - 4, :]
                dve.wait_ge(sem("rope_perm"), t + 1)
                if t:
                    dve.wait_ge(sem("roped"), t)
                chained(tt(RTMP[:], PS[:, 4 + t % 4, :], RSIN[:], ALU.mult))
                dve.wait_ge(sem("rope_cos_part"), t + 1)
                tt(dst, dst, RTMP[:], ALU.add).then_inc(sem("roped"), 1)
            dve.wait_ge(sem("roped"), 6)
            for s in range(2):
                if s:
                    dve.wait_ge(sem("cmp_hid_sum"), 1)
                if s == 0:
                    dve.wait_ge(sem("hid_zero"), 1)
                for g in range(NG):
                    r = slice(64 * g, 64 * g + 64)
                    for h in range(2):
                        src = KVR[r, s, CS * h:CS * h + CS * NC].rearrange("p (n b) -> p b n", b=CS)
                        pos = PAR[r, POST + 32 * s + CS * h:POST + 32 * s + CS * h + CS]
                        ins = tt(BLK[r, CS * h:CS * h + CS, g, :], src, b3(pos, NC), ALU.add)
                        cnt.mark(ins)
                cnt.wait()
                dve.sem_inc(sem("cmp_blocks"), 1)
            for i in range(NT):
                dve.wait_ge(sem("cmp_s_sum"), i + 1)
                if i == 0:
                    dve.wait_ge(sem("w1_loaded"), 64)
                    dve.wait_ge(sem("cmp_hid_sum"), 2)
                for p in range(2):
                    stt(SC[:, i, p], PS[:, 4 + i % 2, 0:256].rearrange("p (q n) -> p q n", n=64)[:, :, 32 * p:32 * p + 32], DK ** -0.5,
                        b3m(CST[:, K_CA + 32 * i:K_CA + 32 * i + 32], 4), ALU.mult, ALU.add).then_inc(sem("cmp_scored"), 1)
            dve.wait_ge(sem("cmp_scored"), 8)
            sc = SC[:].rearrange("p i a q n -> p (i a q) n")
            mx, sm = col(CMX, 32), col(CMX + 32, 32)
            chained(dve.tensor_reduce(mx, sc, AX, ALU.max))
            tt(sc, sc, b3(mx, 32), ALU.subtract).then_inc(sem("cmp_shifted"), 1)
            dve.wait_ge(sem("cmp_exp"), 1)
            chained(dve.tensor_reduce(sm, sc, AX, ALU.add))
            chained(dve.reciprocal(sm, sm))
            chained(tt(sc, sc, b3(sm, 32), ALU.mult))
            for i in range(NT):
                v = SC[:, i].rearrange("p a q n -> p (a q) n")
                ins = tt(v, v, b3m(CST[:, K_CK + 32 * i:K_CK + 32 * i + 32], 8), ALU.mult)
                chained(ins) if i < NT - 1 else ins.then_inc(sem("cmp_probs"), 1)

            def gate(i, first, n, step):
                return SMT[:, i, 64 + first:64 + first + step * (n - 1) + 1:step]

            for i in range(NT):
                dve.wait_ge(sem("cmp_o_sum"), i + 1)
                for p in range(2):
                    tt(YTOK[:, i, :, p, :], PS[:, 6 + i % 2, 256 * p:256 * p + 256].rearrange("p (q d) -> p q d", d=DK),
                       b3(gate(i, 3 * p, 4, 6), DK), ALU.mult).then_inc(sem("y_cmp"), 1)
            dve.wait_ge(sem("y_cmp"), 8)
            units = [(i, g, b, hh) for i in range(NT) for g in range(NG) for b in range(2) for hh in range(4)]

            def side(w):
                pl = Place("oz1", 0)
                if w < 14:
                    split_lo(dve, pl, w + 4)
                f = w // 2
                if w % 2 == 0 and w:
                    dve.wait_ge(u_hi, UNITS["oz1"] + f)
                    tt(YALO[:, f - 1, :], OGATE[(f - 1) % 2][:], YAHI[:, f - 1, :].bitcast(F32), ALU.subtract)\
                        .then_inc(u_lo, 1)
                if w % 2:
                    dve.wait_ge(nonlin, GATES["oz1"] + f + 1)
                    o = OGATE[f % 2][:]
                    cnt.mark(tt(o, o, MHT[:, f, :], ALU.mult))
                    chained(tt(ZGATE[:], ZGATE[:], PS[:, pl.bank(w), :], ALU.mult))
                    dve.sem_inc(bank_free[pl.bank(w)], 1)
                    chained(tt(o, o, ZGATE[:], ALU.mult))
                    dve.sem_inc(product, 1)

            def add_branch(w):
                i, g, b, _ = units[4 * w]
                dve.wait_ge(sem("exp_done"), 4 * w + 4)
                chained(dve.reciprocal(col(AG, 4), col(SUM + 4 * (w % 2), 4)))
                chained(tt(col(AG + 4, 4), col(AG, 4), gate(i, 12 * g + 1 + b, 4, 3), ALU.mult))
                dve.wait_ge(sem("nsa_o"), 4 * w + 4)
                o = OTMP[:, 0:256].rearrange("p (h d) -> p h d", d=DK)
                chained(tt(o, PS[:, 7, 256 * (w % 2):256 * (w % 2) + 256].rearrange("p (h d) -> p h d", d=DK),
                           b3(col(AG + 4, 4), DK), ALU.mult))
                y = YTOK[:, i, 2 * g:2 * g + 2].rearrange("p q a d -> p (q a) d")
                tt(y, y, o, ALU.add).then_inc(sem("y_added"), 1)

            for u, (i, g, b, hh) in enumerate(units):
                n = (i + 1) * P
                if hh == 0:
                    side(u // 4)
                dve.wait_ge(sem("nsa_s"), u + 1)
                ps = PS[:, 4 + hh % 2, 0:n]
                if u >= 4:
                    dve.wait_ge(sem("exp_done"), u - 3)
                chained(dve.tensor_tensor_reduce(out=ps, in0=ps, in1=CST[:, K_CM + 512 - n:K_CM + 512], scale=DK ** -0.5,
                                                 scalar=-3.0e38, op0=ALU.add, op1=ALU.max, accum_out=col(MX + u % 4)))
                ts(col(MX + 4 + u % 4), col(MX + u % 4), -1.0, None, ALU.mult).then_inc(sem("max_ready"), 1)
                if u >= 6 and (u - 6) % 4 == 0:
                    add_branch((u - 6) // 4)
            for w in range((len(units) - 7) // 4 + 1, 16):
                add_branch(w)
            side(16)
            pl = Place("nz1", 0)
            for f in range(4):
                split_lo(dve, pl, f + AHEAD)
                pl.at_least(dve, nonlin, GATES["nz1"] + f + 1, 4)
                dve.wait_ge(sem("yt_ready"), f + 1)
                s = NZS[:, f % 2, :]
                chained(tt(s, s, PS[:, pl.bank(f), :], ALU.mult))
                tt(s, s, YT[:, f, :], ALU.mult).then_inc(product, 1)
                dve.sem_inc(bank_free[pl.bank(f)], 1)
                unit_lo(pl, "nz1", 4, f, YBLO[:, f, :], s, YBHI[:, f, :])

            def merge(name, gates, hi, lo):
                def body(pl):
                    for f in range(2):
                        for q in range(4):
                            split_lo(dve, pl, 4 * f + q + AHEAD)
                            if q >= 2:
                                tiles_ready(dve, pl, 4 * f + q)
                                g = gates[:, 2 * f + q - 2, :]
                                cnt.mark(tt(g, g, PS[:, pl.bank(4 * f + q), :], ALU.mult))
                        cnt.wait()
                        for q in (2, 3):
                            dve.sem_inc(bank_free[pl.bank(4 * f + q)], 1)
                        tt(gates[:, 2 * f, :], gates[:, 2 * f, :], gates[:, 2 * f + 1, :], ALU.add).then_inc(product, 1)
                        fk = ds(pl.i * 2 + f, 1)
                        unit_lo(pl, name, 2, f, lo[:, fk, :], gates[:, 2 * f:2 * f + 1, :], hi[:, fk, :])
                stage(name, 4, body)

            def residual(name, per_tile, gate_col, last=False):
                def body(pl):
                    for f in range(4):
                        for c in range(per_tile):
                            split_lo(dve, pl, per_tile * f + c + AHEAD)
                        tiles_ready(dve, pl, per_tile * f + per_tile - 1)
                        fk = ds(pl.i * 4 + f, 1)
                        ps = PS[:, pl.bank(f):pl.bank(f) + 1, :]
                        xt = XT[:, fk, :]
                        if gate_col is None:
                            ins = tt(xt, ps, xt, ALU.add)
                        else:
                            ins = stt(xt, ps, PAR[:, ds(pl.i * 4 + (gate_col + f), 1)], xt, ALU.mult, ALU.add)
                        cnt.mark(ins)
                        cnt.wait()
                        dve.sem_inc(x_ready, 1)
                        dve.sem_inc(bank_free[pl.bank(f)], 1)
                stage(name, 4, body)

            def ffn_in(name):
                def body(pl):
                    for f in range(2):
                        split_lo(dve, pl, 2 * f + AHEAD)
                        split_lo(dve, pl, 2 * f + 1 + AHEAD)
                        tiles_ready(dve, pl, 2 * f + 1)
                        pl.at_least(dve, bank_free[pl.bank(2 * f)], (pl.tile + 2 * f) // 4 + 1, pl.tb // 4)
                        cnt.mark(tt(FS[:, f, :], FS[:, f, :], PS[:, pl.bank(2 * f + 1), :], ALU.mult))
                        cnt.wait()
                        dve.sem_inc(product, 1)
                        dve.sem_inc(bank_free[pl.bank(2 * f + 1)], 1)
                        fk = ds(pl.i * 2 + f, 1)
                        unit_lo(pl, name, 2, f, HIDLO[:, fk, :], FS[:, f:f + 1, :], HIDHI[:, fk, :])
                stage(name, 2, body)

            def coef(sub):
                chained(stt(col(COEF, 8), col(MOD + 24 * sub + 8, 8), 1.0, col(G2 + 8 * sub, 8), ALU.add, ALU.mult))

            merge("merge1", GT, MGHI, MGLO)
            residual("out1", 1, None)

            for sub in (0, 2):
                chained(ts(col(MOD + 24 * sub + 16, 8), col(MOD + 24 * sub + 16, 8), 0.5, None, ALU.mult))
            coef(0)
            chained(tt(col(FCOEF, 8), col(COEF, 8), col(FNG, 8), ALU.mult))
            rms(1, FCOEF, idx=1, shift=MOD)
            dve.wait_ge(sem("normed"), 16)
            dve.wait_ge(sem("x_T"), KD + 1)
            for k in range(KD):
                stt(XT[:, k, :], XT[:, k, :], col(FNG + k), PS[:, 6, :], ALU.mult, ALU.mult).then_inc(x_ready, 1)
            ffn_in("ffn1_in")
            residual("ffn1_out", 3, MOD + 16)
            coef(1)
            rms(2, COEF, idx=2, shift=MOD + 24)
            conv_stage("conv2", 16)
            def side(n):
                if n < 20:
                    split_lo(dve, Place("v2", 0), n + AHEAD)
                if n == 0 or 8 < n <= 12:
                    return
                pl, k = side_place(n - 1)
                if n <= 8:
                    dve.wait_ge(sem("conv_base"), 32 + k + 1)
                    for j in range(1, 4):
                        o = QKV[:, 16 + k, j:T]
                        ins = stt(o, PS[:, pl.bank(k), 0:T - j], col(CW2 + 24 * (3 - j) + 16 + k), o, ALU.mult, ALU.add)
                        chained(ins)
                    dve.sem_inc(sem("conv_taps"), 1)
                else:
                    dve.wait_ge(nonlin, GATES["z2"] + k + 1)
                    chained(tt(waiting(4 + k), waiting(4 + k), by_chunk(PS[:, pl.bank(k), :]), ALU.mult))
                dve.sem_inc(bank_free[pl.bank(k)], 1)

            pl = Place("small2", 0)
            split_lo(dve, pl, AHEAD)
            side(0)

            e0, e1, e2 = (EROW[k][0:8, :] for k in range(3))
            l0, l1, l2 = (LPR[0:8, k, :] for k in range(3))
            dve.wait_ge(sem("softplus_parts"), 1)
            dve.wait_ge(sem("row_zero"), 5)
            chained(stt(SM[0:8, :], l2, 1.0, l0, ALU.is_equal, ALU.mult))
            chained(ts(l2, l2, -1.0, 2.0 ** -24, ALU.add, ALU.max))
            chained(dve.reciprocal(l2, l2))
            chained(tt(l2, l2, l0, ALU.mult))
            chained(tt(l1, l1, l2, ALU.mult))
            chained(tt(l1, l1, SM[0:8, :], ALU.add))
            chained(ts(e0, e0, 0.0, None, ALU.max))
            chained(tt(e0, e0, l1, ALU.add))
            chained(ts(e0, e0, PAR[0:8, ALOG:ALOG + 1], -1.0, ALU.mult, ALU.mult))
            chained(dve.tensor_tensor_scan(l0, e2, e0, 0.0, ALU.mult, ALU.add))
            cnt.mark(dve.tensor_copy(e0, l0))
            cnt.mark(dve.tensor_copy(SM[32:40, :], l0))
            g3 = l0.rearrange("p (c t) -> p c t", t=P)
            cnt.mark(tt(SM[64:72, :].rearrange("p (c t) -> p c t", t=P), g3[:, :, P - 1:P].to_broadcast([8, NT, P]), g3,
                        ALU.subtract))
            dve.wait_ge(sem("beta_rows"), 1)
            cnt.mark(dve.tensor_copy(SM[0:8, :], e1))
            cnt.wait()
            dve.sem_inc(sem("packed2"), 2)
            side(1)
            dve.wait_ge(sem("norm_root"), 1)
            dve.reciprocal(NRT[0:16, :], NRT[0:16, :]).then_inc(sem("lengths"), 1)
            side(2)
            for h in range(16):
                dve.wait_ge(sem("length_spread"), h + 1)
                tt(QKV[:, h, :], QKV[:, h, :], PS[:, 5 + h % 2, :], ALU.mult).then_inc(sem("qk_normed"), 1)
            dve.wait_ge(sem("delta_cols"), 1)

            def ps4(bk):
                return PS[:, bk, :].rearrange("p (h n) -> p h n", n=P)

            def ccol(base, c, a):
                return b3(PAR[:, base + 8 * c + 4 * a:base + 8 * c + 4 * a + 4], P)

            def o_scaled(c):
                dve.wait_ge(sem("o_rstd"), c + 1)
                tt(OO[:], OO[:], b3(col(RSO, 8), P), ALU.mult).then_inc(sem("o_normed"), 1)

            id4 = b3m(ID, 4)
            for c in range(NT):
                k2 = 2 * c
                for a in range(2):
                    h4 = slice(4 * a, 4 * a + 4)
                    dve.wait_ge(sem("end_decay"), k2 + a + 1)
                    if c and a == 0:
                        dve.wait_ge(sem("intra_sum"), 2 * c)
                    tt(DD[:, h4, :], ps4(4 + 2 * a), b3(SMT[:, c, 32 + 4 * a:36 + 4 * a], P), ALU.subtract)\
                        .then_inc(sem("decay_arg"), 1)
                    dve.wait_ge(sem("decay_arg"), k2 + a + 1)
                    tt(DD[:, h4, :], DD[:, h4, :], b3m(CST[:, K_CMT:K_CMT + P], 4), ALU.add)\
                        .then_inc(sem("decay_masked"), 1)
                if c:
                    o_scaled(c - 1)
                for a in range(2):
                    h4 = slice(4 * a, 4 * a + 4)
                    dve.wait_ge(sem("decay_exp"), k2 + a + 1)
                    dve.wait_ge(sem("kk_sum"), k2 + a + 1)
                    tt(MT[:, h4, :], ps4(5 + 2 * a), DD[:, h4, :], ALU.mult).then_inc(sem("kk_decayed"), 1)
                for a in range(2):
                    h4 = slice(4 * a, 4 * a + 4)
                    dve.wait_ge(sem("kk_decayed"), k2 + a + 1)
                    dve.wait_ge(sem("beta_bcast"), k2 + a + 1)
                    tt(MT[:, h4, :], ps4(4 + 2 * a), MT[:, h4, :], ALU.mult).then_inc(sem("delta_a"), 1)
                    dve.wait_ge(sem("qk_sum"), k2 + a + 1)
                    stt(QKM[:, h4, :], ps4(5 + 2 * a), float(128 ** -0.5), DD[:, h4, :], ALU.mult, ALU.mult)\
                        .then_inc(sem("qk_decayed"), 1)
                for a in range(2):
                    h4 = slice(4 * a, 4 * a + 4)
                    dve.wait_ge(sem("delta_a"), k2 + a + 1)
                    chained(tt(TT[:, h4, :], MT[:, h4, :], b3m(CST[:, K_LV:K_LV + P], 4), ALU.mult))
                    tt(TT[:, h4, :], id4, TT[:, h4, :], ALU.subtract).then_inc(sem("inv_T_ready"), 1)
                for lv in range(1, LEVELS):
                    if c == 0:
                        side(lv + 2)
                    elif lv <= 4 and c + lv > 2:
                        side(8 + 4 * (c - 1) + lv - 1)
                    elif c == 3 and lv == 5:
                        side(20)
                    for a in range(2):
                        h4 = slice(4 * a, 4 * a + 4)
                        dve.wait_ge(sem("inv_step"), (c * 6 + lv - 1) * 2 + a + 1)
                        dve.wait_ge(sem("inv_T_ready"), (c * LEVELS + lv - 1) * 2 + a + 1)
                        tt(TT[:, h4, :], TT[:, h4, :], ps4(5 + 2 * a), ALU.subtract).then_inc(sem("inv_T_ready"), 1)
                for a in range(2):
                    h4 = slice(4 * a, 4 * a + 4)
                    r = RV[:, h4, :]
                    dve.wait_ge(sem("v_tokens"), k2 + a + 1)
                    if c:
                        dve.wait_ge(sem("ks_sum"), k2 - 2 + a + 1)
                        chained(tt(DD[:, h4, :], ps4(5 + 2 * a), ccol(EG, c, a), ALU.mult))
                        chained(tt(r, r, DD[:, h4, :], ALU.subtract))
                    tt(r, r, b3(SMT[:, c, 4 * a:4 * a + 4], P), ALU.mult).then_inc(sem("rhs_ready"), 1)
                for a in range(2 if c < NT - 1 else 0):
                    h4 = slice(4 * a, 4 * a + 4)
                    dve.wait_ge(sem("k_T"), k2 + a + 1)
                    tt(KDT[:, h4, :], ps4(5 + 2 * a), ccol(EKD, c, a), ALU.mult).then_inc(sem("k_dec"), 1)
                for a in range(2):
                    h4 = slice(4 * a, 4 * a + 4)
                    o = OO[:, h4, :]
                    if c:
                        dve.wait_ge(sem("qs_sum"), k2 - 2 + a + 1)
                        tt(o, ps4(4 + 2 * a), ccol(QEG, c, a), ALU.mult).then_inc(sem("o_inter"), 1)
                        dve.wait_ge(sem("o_inter"), k2 - 2 + a + 1)
                    dve.wait_ge(sem("intra_sum"), k2 + a + 1)
                    if c:
                        chained(tt(o, ps4(5 + 2 * a), o, ALU.add))
                    else:
                        chained(dve.tensor_copy(o, ps4(5 + 2 * a)))
                for a in range(2 if c < NT - 1 else 0):
                    h4 = slice(4 * a, 4 * a + 4)
                    s = SS[:, h4, :]
                    dve.wait_ge(sem("state_sum"), k2 + a + 1)
                    if c:
                        chained(tt(s, s, b3(PAR[:, EGL + 4 * a:EGL + 4 * a + 4], P), ALU.mult))
                        tt(s, s, ps4(4 + 2 * a), ALU.add).then_inc(sem("state_new"), 1)
                    else:
                        dve.tensor_copy(s, ps4(4 + 2 * a)).then_inc(sem("state_new"), 1)
                chained(tt(XX[:], OO[:], OO[:], ALU.mult))
                chained(dve.tensor_reduce(col(RSO, 8), XX[:], AX, ALU.add))
                ts(col(RSO, 8), col(RSO, 8), 1.0 / P, EPS, ALU.mult, ALU.add).then_inc(sem("o_var"), 1)
            o_scaled(NT - 1)

            def z_product(f):
                tt(waiting(4 + f), waiting(4 + f), by_chunk(QKV[:, 16 + f, :]), ALU.mult).then_inc(product, 1)

            dve.wait_ge(sem("o_T_taken"), 8)
            z_product(0)
            for f in range(8):
                if f < 7:
                    z_product(f + 1)
                dve.wait_ge(u_hi, UNITS["z2"] + f + 1)
                tt(by_chunk(Y2LO[:, f, :]), waiting(4 + f), by_chunk(Y2HI[:, f, :].bitcast(F32)), ALU.subtract).then_inc(u_lo, 1)
            for g in range(4):
                dve.wait_ge(u_hi, UNITS["pool2"] + g + 1)
                stt(PLLO[:, g, :], PS[:, 4 + g, :], col(PSC + g), PLHI[:, g, :].bitcast(F32), ALU.mult, ALU.subtract)\
                    .then_inc(u_lo, 1)
                dve.sem_inc(product, 1)
            merge("merge2", GT2, M2HI, M2LO)
            residual("out2", 1, MOD + 24 + 16)
            coef(2)
            rms(3, COEF, idx=3, shift=MOD + 48)
            ffn_in("ffn2_in")
            for i in range(INFO["ffn2_out"]["iters"]):
                pl = Place("ffn2_out", 0)
                pl.chunk += pl.nb * i
                pl.tile += pl.tb * i
                pl.iters = 1
                for f in range(4):
                    for q in range(3):
                        split_lo(dve, pl, 3 * f + q + AHEAD)
                    tiles_ready(dve, pl, 3 * f + 2)
                    xt = XT[:, 4 * i + f, :]
                    chained(stt(xt, PS[:, pl.bank(f), :], col(MOD + 48 + 16 + 4 * i + f), xt, ALU.mult, ALU.add))
                    dve.sem_inc(x_ready, 1)
                    dve.sem_inc(bank_free[pl.bank(f)], 1)
            rms(4, FG2, dst=XT)


_INS = ["x", "positions", "norm_g", "w_in", "conv_q_w", "conv_q_b", "conv_k_w", "conv_k_b", "b_igate", "b_fgate",
        "mh_norm_g", "cmp_pos_k", "cmp_w1_k", "cmp_w2_k", "cmp_pos_v", "cmp_w1_v", "cmp_w2_v", "b_nsa_gate",
        "w_branch_a", "w_branch_b", "w_out", "final_norm_g", "c_2", "ada_w_2", "ada_b_2", "norm_g_2",
        "ffn1_w_in_2", "ffn1_w_out_2", "ffn2_w_in_2", "ffn2_w_out_2", "mix_w_in_2", "conv_w_2", "a_log_2",
        "dt_bias_2", "dn_norm_g_2", "pool_w_2", "pool_scale_2", "pool_proj_2", "dn_proj_2", "mix_w_out_2",
        "final_g_2"]


def kernel(**inputs):
    import concourse.bacc as bacc
    from concourse.bass_utils import run_bass_kernel_spmd

    nc = bacc.Bacc("TRN2", target_bir_lowering=False, num_devices=1)
    arrays = {"in_constants": constants()}
    arrays.update({f"in_{n}": np.ascontiguousarray(inputs[n]) for n in _INS})
    args = [nc.dram_tensor(n, a.shape, mybir.dt.from_np(a.dtype), kind="ExternalInput").ap()
            for n, a in arrays.items()]
    out = nc.dram_tensor("out", (1, T, D), F32, kind="ExternalOutput").ap()
    two_blocks(nc, *args, out)
    return run_bass_kernel_spmd(nc, [arrays], core_ids=[0]).results[0]["out"]
```
